# Optimizing a Trainium2 kernel written in Bass

```python
import math
import jax, jax.numpy as jnp
from jax import lax
import numpy as np

D_MODEL = 2048
BATCH = 1
SEQ = 256
DEPTH = 1

N_HEADS_TOTAL = 16
HEAD_DIM = D_MODEL // N_HEADS_TOTAL
SWA_HEADS = 6
SWA_KV_HEADS = 2
SWA_GROUP = SWA_HEADS // SWA_KV_HEADS
WINDOW = 128
MOBA_HEADS = 4
MOBA_BLOCK = 256
MOBA_TOPK = 3
MOBA_Q_CHUNK = 64
DIFF_HEADS = 6
DIFF_QK_DIM = HEAD_DIM // 2
DIFF_V_DIM = HEAD_DIM
DIFF_Q_BLOCK = 128
MIX_WIDTH = (SWA_HEADS + MOBA_HEADS) * HEAD_DIM + DIFF_HEADS * DIFF_V_DIM
IN_SPLITS = (SWA_HEADS * HEAD_DIM, SWA_KV_HEADS * HEAD_DIM, SWA_KV_HEADS * HEAD_DIM,
             MOBA_HEADS * HEAD_DIM, MOBA_HEADS * HEAD_DIM, MOBA_HEADS * HEAD_DIM,
             DIFF_HEADS * 2 * DIFF_QK_DIM, DIFF_HEADS * 2 * DIFF_QK_DIM, DIFF_HEADS * DIFF_V_DIM)
IN_WIDTH = sum(IN_SPLITS)
IN_OFFSETS = tuple(int(o) for o in np.cumsum(IN_SPLITS)[:-1])
REL_BUCKETS = 32
REL_EXACT = REL_BUCKETS // 2
REL_MAX_DIST = 128
N_GROUPS = 4
EXPERTS_PER_GROUP = 8
N_EXPERTS = N_GROUPS * EXPERTS_PER_GROUP
TOP_E = 2
D_EXPERT = 512
MOE_BLOCK = 256
PLE_DIM = 256
EPS = 1e-6
NEG = -1e30

kernel_name = 'hymba_style_hybrid_swa_moba_diff_hmoe'

def rms_norm(x, g):
    xf = x.astype(jnp.float32)
    y = xf * lax.rsqrt(jnp.mean(xf * xf, axis=-1, keepdims=True) + EPS)
    return (y * g.astype(jnp.float32)).astype(x.dtype)

def rel_bucket(dist):
    n = jnp.maximum(dist, 0)
    is_small = n < REL_EXACT
    nf = jnp.maximum(n, 1).astype(jnp.float32)
    large = REL_EXACT + (jnp.log(nf / REL_EXACT) / math.log(REL_MAX_DIST / REL_EXACT)
                         * (REL_BUCKETS - REL_EXACT)).astype(jnp.int32)
    large = jnp.minimum(large, REL_BUCKETS - 1)
    return jnp.where(is_small, n, large)

def swa_sink_attention(q, k, v, bias_tab, sinks):
    b, s = q.shape[:2]
    nw = s // WINDOW
    qb = q.reshape(b, nw, WINDOW, SWA_KV_HEADS, SWA_GROUP, HEAD_DIM)
    kb = k.reshape(b, nw, WINDOW, SWA_KV_HEADS, HEAD_DIM)
    vb = v.reshape(b, nw, WINDOW, SWA_KV_HEADS, HEAD_DIM)
    pad = jnp.zeros_like(kb[:, :1])
    kcat = jnp.concatenate([jnp.concatenate([pad, kb[:, :-1]], axis=1), kb], axis=2)
    vcat = jnp.concatenate([jnp.concatenate([pad, vb[:, :-1]], axis=1), vb], axis=2)
    logits = jnp.einsum('bnqkgd,bnpkd->bkgnqp', qb, kcat).astype(jnp.float32) * (HEAD_DIM ** -0.5)
    qi = jnp.arange(WINDOW)[:, None]
    pj = jnp.arange(2 * WINDOW)[None, :]
    dist = qi + WINDOW - pj
    bias = bias_tab[rel_bucket(dist)].astype(jnp.float32)
    bias = bias.reshape(WINDOW, 2 * WINDOW, SWA_KV_HEADS, SWA_GROUP).transpose(2, 3, 0, 1)[None, :, :, None]
    in_window = (dist >= 0) & (dist < WINDOW)
    key_exists = (jnp.arange(nw)[:, None, None] > 0) | (pj >= WINDOW)[None]
    mask = in_window[None] & key_exists
    logits = jnp.where(mask, logits + bias, NEG)
    sink = sinks.astype(jnp.float32).reshape(SWA_KV_HEADS, SWA_GROUP)[None, :, :, None, None, None]
    sink = jnp.broadcast_to(sink, logits.shape[:-1] + (1,))
    probs = jax.nn.softmax(jnp.concatenate([logits, sink], axis=-1), axis=-1)[..., :-1]
    out = jnp.einsum('bkgnqp,bnpkd->bnqkgd', probs.astype(v.dtype), vcat)
    return out.reshape(b, s, SWA_HEADS * HEAD_DIM)

def moba_attention(q, k, v, bias_tab):
    b, s = q.shape[:2]
    nb = -(-s // MOBA_BLOCK)
    s_pad = nb * MOBA_BLOCK
    padw = ((0, 0), (0, s_pad - s), (0, 0), (0, 0))
    kb = jnp.pad(k, padw).reshape(b, nb, MOBA_BLOCK, MOBA_HEADS, HEAD_DIM).transpose(0, 3, 1, 2, 4)
    vb = jnp.pad(v, padw).reshape(b, nb, MOBA_BLOCK, MOBA_HEADS, HEAD_DIM).transpose(0, 3, 1, 2, 4)
    kmean = jnp.mean(kb.astype(jnp.float32), axis=3)
    topk = min(MOBA_TOPK, nb)
    nc = s // MOBA_Q_CHUNK
    qc = q.reshape(b, nc, MOBA_Q_CHUNK, MOBA_HEADS, HEAD_DIM).transpose(1, 0, 2, 3, 4)
    bi = jnp.arange(b)[:, None, None, None]
    hi = jnp.arange(MOBA_HEADS)[None, None, :, None]
    offs = jnp.arange(MOBA_BLOCK)
    scale = HEAD_DIM ** -0.5

    def chunk(args):
        qblk, c = args
        qpos = c * MOBA_Q_CHUNK + jnp.arange(MOBA_Q_CHUNK)
        j = (c * MOBA_Q_CHUNK) // MOBA_BLOCK
        gate = jnp.einsum('bqhd,bhnd->bqhn', qblk.astype(jnp.float32), kmean)
        gate = jnp.where(jnp.arange(nb) < j, gate, -jnp.inf)
        _, idx = lax.top_k(gate, topk)
        valid = jnp.arange(topk) < j
        kg = kb[bi, hi, idx]
        vg = vb[bi, hi, idx]
        l_sel = jnp.einsum('bqhd,bqhtsd->bqhts', qblk, kg).astype(jnp.float32) * scale
        kpos_sel = idx[..., None] * MOBA_BLOCK + offs
        dist_sel = qpos[None, :, None, None, None] - kpos_sel
        bias_sel = bias_tab[rel_bucket(dist_sel), hi[..., None]].astype(jnp.float32)
        l_sel = jnp.where(valid[:, None], l_sel + bias_sel, NEG)
        kown = lax.dynamic_index_in_dim(kb, j, axis=2, keepdims=False)
        vown = lax.dynamic_index_in_dim(vb, j, axis=2, keepdims=False)
        l_own = jnp.einsum('bqhd,bhsd->bqhs', qblk, kown).astype(jnp.float32) * scale
        dist_own = qpos[:, None] - (j * MOBA_BLOCK + offs)[None, :]
        bias_own = bias_tab[rel_bucket(dist_own)].astype(jnp.float32).transpose(0, 2, 1)[None]
        l_own = jnp.where((dist_own >= 0)[None, :, None, :], l_own + bias_own, NEG)
        logits = jnp.concatenate([l_sel.reshape(b, MOBA_Q_CHUNK, MOBA_HEADS, topk * MOBA_BLOCK), l_own], axis=-1)
        probs = jax.nn.softmax(logits, axis=-1).astype(v.dtype)
        p_sel = probs[..., :topk * MOBA_BLOCK].reshape(b, MOBA_Q_CHUNK, MOBA_HEADS, topk, MOBA_BLOCK)
        p_own = probs[..., topk * MOBA_BLOCK:]
        return (jnp.einsum('bqhts,bqhtsd->bqhd', p_sel, vg)
                + jnp.einsum('bqhs,bhsd->bqhd', p_own, vown))

    out = lax.map(chunk, (qc, jnp.arange(nc)))
    return out.transpose(1, 0, 2, 3, 4).reshape(b, s, MOBA_HEADS * HEAD_DIM)

def diff_attention(q, k, v, bias_tab, lam, sub_g, lambda_init):
    b, s = q.shape[:2]
    nq = s // DIFF_Q_BLOCK
    qblocks = q.reshape(b, nq, DIFF_Q_BLOCK, DIFF_HEADS, 2, DIFF_QK_DIM).transpose(1, 0, 2, 3, 4, 5)
    kpos = jnp.arange(s)
    scale = DIFF_QK_DIM ** -0.5

    def block(args):
        qblk, c = args
        qpos = c * DIFF_Q_BLOCK + jnp.arange(DIFF_Q_BLOCK)
        logits = jnp.einsum('bqhcd,bkhcd->bhcqk', qblk, k).astype(jnp.float32) * scale
        dist = qpos[:, None] - kpos[None, :]
        bias = bias_tab[rel_bucket(dist)].astype(jnp.float32).transpose(2, 0, 1)[None, :, None]
        logits = jnp.where(dist >= 0, logits + bias, NEG)
        probs = jax.nn.softmax(logits, axis=-1)
        attn = probs[:, :, 0] - lam * probs[:, :, 1]
        return jnp.einsum('bhqk,bkhe->bqhe', attn.astype(v.dtype), v)

    out = lax.map(block, (qblocks, jnp.arange(nq)))
    out = out.transpose(1, 0, 2, 3, 4).reshape(b, s, DIFF_HEADS, DIFF_V_DIM)
    out = rms_norm(out, sub_g) * (1.0 - lambda_init)
    return out.reshape(b, s, DIFF_HEADS * DIFF_V_DIM)

def hier_moe(v, w_group, w_expert, w1, w3, w2):
    b, s, d = v.shape
    t = b * s
    xf = v.reshape(t, d)
    g_prob = jax.nn.softmax((xf @ w_group).astype(jnp.float32), axis=-1)
    grp = jnp.argmax(g_prob, axis=-1)
    g_w = jnp.take_along_axis(g_prob, grp[:, None], axis=1)
    e_logits = (xf @ w_expert).astype(jnp.float32).reshape(t, N_GROUPS, EXPERTS_PER_GROUP)
    e_in = jnp.take_along_axis(e_logits, grp[:, None, None], axis=1)[:, 0]
    top_l, top_i = lax.top_k(e_in, TOP_E)
    gate = g_w * jax.nn.softmax(top_l, axis=-1)
    n_assign = t * TOP_E
    eid = (grp[:, None] * EXPERTS_PER_GROUP + top_i).reshape(n_assign)
    tok = jnp.arange(n_assign) // TOP_E
    wts = gate.reshape(n_assign)
    order = jnp.argsort(eid)
    se = eid[order]
    counts = jnp.bincount(eid, length=N_EXPERTS)
    starts = jnp.cumsum(counts) - counts
    pcounts = ((counts + MOE_BLOCK - 1) // MOE_BLOCK) * MOE_BLOCK
    pends = jnp.cumsum(pcounts)
    pstarts = pends - pcounts
    dest = pstarts[se] + (jnp.arange(n_assign) - starts[se])
    p_rows = n_assign + N_EXPERTS * MOE_BLOCK
    buf_tok = jnp.zeros((p_rows,), jnp.int32).at[dest].set(tok[order].astype(jnp.int32))
    buf_w = jnp.zeros((p_rows,), jnp.float32).at[dest].set(wts[order])
    nblk = p_rows // MOE_BLOCK
    blk_e = jnp.minimum(jnp.searchsorted(pends, jnp.arange(nblk) * MOE_BLOCK, side='right'), N_EXPERTS - 1)

    def expert_block(args):
        toks, e = args
        xb = xf[toks]
        hdn = jax.nn.silu(xb @ w1[e]) * (xb @ w3[e])
        return hdn @ w2[e]

    yb = lax.map(expert_block, (buf_tok.reshape(nblk, MOE_BLOCK), blk_e))
    y = jax.ops.segment_sum(yb.reshape(p_rows, d) * buf_w[:, None].astype(yb.dtype), buf_tok, num_segments=t)
    return y.reshape(b, s, d)

def setup_inputs(seed: int = 0) -> dict:
    key = jax.random.key(seed)
    ks = jax.random.split(key, 24)

    def nrm(k, shape, scale):
        return jax.random.normal(k, shape, jnp.float32) * scale

    return {
        'x': nrm(ks[0], (BATCH, SEQ, D_MODEL), 1.0),
        'p': nrm(ks[1], (DEPTH, BATCH, SEQ, PLE_DIM), 1.0),
        'rel_bias': nrm(ks[2], (REL_BUCKETS, N_HEADS_TOTAL), 0.5),
        'g_final': 1.0 + nrm(ks[3], (D_MODEL,), 0.05),
        'g_mix': 1.0 + nrm(ks[4], (DEPTH, D_MODEL), 0.05),
        'w_in': nrm(ks[5], (DEPTH, D_MODEL, IN_WIDTH), D_MODEL ** -0.5),
        'swa_sinks': nrm(ks[6], (DEPTH, SWA_HEADS), 0.5),
        'lam_q1': nrm(ks[7], (DEPTH, DIFF_QK_DIM), 0.1),
        'lam_k1': nrm(ks[8], (DEPTH, DIFF_QK_DIM), 0.1),
        'lam_q2': nrm(ks[9], (DEPTH, DIFF_QK_DIM), 0.1),
        'lam_k2': nrm(ks[10], (DEPTH, DIFF_QK_DIM), 0.1),
        'diff_subln': 1.0 + nrm(ks[11], (DEPTH, DIFF_V_DIM), 0.05),
        'w_out': nrm(ks[12], (DEPTH, MIX_WIDTH, D_MODEL), MIX_WIDTH ** -0.5),
        'g_ffn': 1.0 + nrm(ks[13], (DEPTH, D_MODEL), 0.05),
        'w_group': nrm(ks[14], (DEPTH, D_MODEL, N_GROUPS), D_MODEL ** -0.5),
        'w_expert': nrm(ks[15], (DEPTH, D_MODEL, N_EXPERTS), D_MODEL ** -0.5),
        'w1': nrm(ks[16], (DEPTH, N_EXPERTS, D_MODEL, D_EXPERT), D_MODEL ** -0.5),
        'w3': nrm(ks[17], (DEPTH, N_EXPERTS, D_MODEL, D_EXPERT), D_MODEL ** -0.5),
        'w2': nrm(ks[18], (DEPTH, N_EXPERTS, D_EXPERT, D_MODEL), D_EXPERT ** -0.5),
        'g_ple': 1.0 + nrm(ks[19], (DEPTH, D_MODEL), 0.05),
        'w_ple_gate': nrm(ks[20], (DEPTH, D_MODEL, D_MODEL), D_MODEL ** -0.5),
        'w_ple_proj': nrm(ks[21], (DEPTH, PLE_DIM, D_MODEL), PLE_DIM ** -0.5),
    }

def reference(x, p, rel_bias, g_final, g_mix, w_in, swa_sinks, lam_q1, lam_k1, lam_q2, lam_k2,
              diff_subln, w_out, g_ffn, w_group, w_expert, w1, w3, w2, g_ple, w_ple_gate, w_ple_proj):
    b, s, _ = x.shape
    bias_a = rel_bias[:, :SWA_HEADS]
    bias_b = rel_bias[:, SWA_HEADS:SWA_HEADS + MOBA_HEADS]
    bias_c = rel_bias[:, SWA_HEADS + MOBA_HEADS:]
    h = x
    for i in range(DEPTH):
        u = rms_norm(h, g_mix[i])
        proj = u @ w_in[i]
        qa, ka, va, qb, kb, vb, qc, kc, vc = jnp.split(proj, IN_OFFSETS, axis=-1)
        ya = swa_sink_attention(qa.reshape(b, s, SWA_HEADS, HEAD_DIM),
                                ka.reshape(b, s, SWA_KV_HEADS, HEAD_DIM),
                                va.reshape(b, s, SWA_KV_HEADS, HEAD_DIM), bias_a, swa_sinks[i])
        yb = moba_attention(qb.reshape(b, s, MOBA_HEADS, HEAD_DIM),
                            kb.reshape(b, s, MOBA_HEADS, HEAD_DIM),
                            vb.reshape(b, s, MOBA_HEADS, HEAD_DIM), bias_b)
        lambda_init = 0.8 - 0.6 * math.exp(-0.3 * i)
        lam = (jnp.exp(jnp.sum(lam_q1[i].astype(jnp.float32) * lam_k1[i].astype(jnp.float32)))
               - jnp.exp(jnp.sum(lam_q2[i].astype(jnp.float32) * lam_k2[i].astype(jnp.float32)))
               + lambda_init)
        yc = diff_attention(qc.reshape(b, s, DIFF_HEADS, 2, DIFF_QK_DIM),
                            kc.reshape(b, s, DIFF_HEADS, 2, DIFF_QK_DIM),
                            vc.reshape(b, s, DIFF_HEADS, DIFF_V_DIM), bias_c, lam, diff_subln[i], lambda_init)
        h = h + jnp.concatenate([ya, yb, yc], axis=-1) @ w_out[i]
        h = h + hier_moe(rms_norm(h, g_ffn[i]), w_group[i], w_expert[i], w1[i], w3[i], w2[i])
        h = h + jax.nn.sigmoid(rms_norm(h, g_ple[i]) @ w_ple_gate[i]) * (p[i] @ w_ple_proj[i])
    return rms_norm(h, g_final)


_drawn_inputs = setup_inputs


def setup_inputs(seed=0):
    import zlib

    import numpy as np

    out = dict(_drawn_inputs(seed))
    spreads = {}
    factors = {'swa_sinks': 8.0, 'lam_q2': 4.545, 'lam_k2': 8.0, 'g_ple': 7.002}
    for name, (base, spread) in spreads.items():
        noise = np.random.default_rng([zlib.crc32(name.encode()), seed]).standard_normal(out[name].shape)
        drawn = base * np.exp(spread * noise) if base else spread * noise
        out[name] = __import__('jax').numpy.asarray(drawn.astype(out[name].dtype))
    for name, factor in factors.items():
        out[name] = (out[name] * factor).astype(out[name].dtype)
    return out
```

```python
import math
from contextlib import ExitStack

import numpy as np
import concourse.bass as bass
from concourse import mybir

F32 = mybir.dt.float32
I32 = mybir.dt.int32
ALU = mybir.AluOpType
ACT = mybir.ActivationFunctionType
AX = mybir.AxisListType

P = 128
D = 2048
S = 256
TT = S // P
KT = D // P
HD = 128
SWA_HEADS, SWA_KV, MOBA_HEADS, DIFF_HEADS = 6, 2, 4, 6
HEADS = SWA_HEADS + MOBA_HEADS + DIFF_HEADS
WINDOW = 128
BUCKETS, EXACT, MAX_DIST = 32, 16, 128
GROUPS, PER_GROUP = 4, 8
EXPERTS = GROUPS * PER_GROUP
DE = 512
JT = DE // P
PLE = 256
EPS = 1e-6
NEG = -1e30
LAMBDA_INIT = 0.8 - 0.6 * math.exp(-0.3 * 0)

SLOT = 2048
RING = 16
SLOTS = 32
QUAD = P // SLOTS
BLOCKS = EXPERTS // QUAD
MAX_ROUNDS = S // SLOTS
REL = 3 * P

C_ID, C_FLIP, C_BEFORE, C_ONES, C_SLOT = (i * P for i in range(5))
C_IG = 5 * P
C_IE = C_IG + TT * GROUPS
C_TH = C_IE + TT * EXPERTS
C_POW = C_TH + MAX_ROUNDS
C_END = C_POW + 4


def constants():
    c = np.zeros((P, C_END), np.float32)
    i = np.arange(P)
    c[i, C_ID + i] = 1.0
    c[i, C_FLIP + P - 1 - i] = 1.0
    c[:, C_BEFORE:C_BEFORE + P] = i[:, None] < i[None, :]
    c[:, C_ONES:C_ONES + P] = 1.0
    c[:, C_SLOT:C_SLOT + P] = i[None, :] % SLOTS
    c[:, C_IG:C_IE] = np.arange(TT * GROUPS) % GROUPS
    c[:, C_IE:C_TH] = np.arange(TT * EXPERTS) % EXPERTS
    c[:, C_TH:C_POW] = np.arange(MAX_ROUNDS) * SLOTS
    c[:, C_POW:C_END] = -0.5
    return c


def bucket_choice():
    dist = 2 * P - 1 - np.arange(REL)
    n = np.maximum(dist, 0)
    nf = np.maximum(n, 1).astype(np.float32)
    large = EXACT + (np.log(nf / np.float32(EXACT)) / np.float32(math.log(MAX_DIST / EXACT))
                     * (BUCKETS - EXACT)).astype(np.int32)
    bucket = np.where(n < EXACT, n, np.minimum(large, BUCKETS - 1))
    c = np.zeros((BUCKETS + 1, 2, REL), np.float32)
    for swa in range(2):
        seen = (dist >= 0) & ((dist < WINDOW) | (swa == 0))
        c[np.where(seen, bucket, BUCKETS), swa, np.arange(REL)] = 1.0
    return c.reshape(BUCKETS + 1, 2 * REL)


def head_plan():
    kv_cols = SWA_HEADS * HD
    moba = kv_cols + 2 * SWA_KV * HD
    diff = moba + 3 * MOBA_HEADS * HD
    steps = []
    for h in range(SWA_HEADS):
        g = h // (SWA_HEADS // SWA_KV)
        blocks = [("q", h * HD)]
        if h % (SWA_HEADS // SWA_KV) == 0:
            blocks += [("k", kv_cols + g * HD), ("v", kv_cols + (SWA_KV + g) * HD)]
        steps.append(("swa", g, blocks))
    for kind, base, n in (("moba", moba, MOBA_HEADS), ("diff", diff, DIFF_HEADS)):
        for h in range(n):
            blocks = [(b, base + (i * n + h) * HD) for i, b in enumerate("qkv")]
            steps.append((kind, steps[-1][1] + 1, blocks))
    return steps


STEPS = head_plan()
BLOCK_OF = {}
PROJ = []
for _h, (_kind, _kv, _blocks) in enumerate(STEPS):
    for _b, _col in _blocks:
        BLOCK_OF[_h, _b] = len(PROJ)
        PROJ.append((_b, _col, _h % 2 if _b == "q" else _kv % 2))

N_OUT = D // 256
FILLS_PROJ = len(PROJ)
FILLS_HEAD = FILLS_PROJ + 2 * N_OUT
FILLS_X = 12
FILLS_IT = QUAD * FILLS_X
assert FILLS_IT % RING == 0 and FILLS_HEAD % 2 == 0
TAIL_PROJ = FILLS_HEAD
TAIL_GATE = TAIL_PROJ + PLE // P

NORM_FILLS = KT // 2
D_NORM_A = 0
D_PROJ = D_NORM_A + NORM_FILLS
D_OUT = D_PROJ + FILLS_PROJ
D_NORM_B = D_OUT + N_OUT
D_NORM_C = D_NORM_B + NORM_FILLS
D_PLE = D_NORM_C + NORM_FILLS
D_GATE = D_PLE + N_OUT


def layer(nc, A, out):
    with ExitStack() as ctx:
        def sb(name, shape, dt=F32):
            return ctx.enter_context(nc.sbuf_tensor(name, shape, dt))

        def sem(name):
            return ctx.enter_context(nc.semaphore(name))

        bank = [ctx.enter_context(nc.psum_tensor(f"bank{i}", [P, 512], F32)) for i in range(8)]
        bias_rows = nc.dram_tensor("bias_rows", [HEADS, REL], F32, kind="Internal").ap()

        ring = sb("ring", [P, RING * SLOT])
        actT = sb("actT", [P, KT, S])
        h = sb("h", [P, TT, D])
        xn = sb("xn", [P, TT, KT, P])
        cst = sb("cst", [P, C_END])
        g_mixT, g_ffnT, g_pleT = (sb(f"gT{i}", [P, KT]) for i in range(3))
        router = sb("router", [P, KT, GROUPS + EXPERTS])
        slot_of = sb("slot_of", [P, TT, EXPERTS])
        gate_of = sb("gate_of", [P, TT, EXPERTS])
        rounds_i = sb("rounds_i", [P, 1], I32)
        sumsq = sb("sumsq", [P, 4, TT])
        rstd = sb("rstd", [P, 4, TT])
        lam = sb("lam", [P, 4, HD // 2])
        small = sb("small", [P, 64])
        sinks = sb("sinks", [P, SWA_HEADS])
        nsinks = sb("nsinks", [P, SWA_HEADS])
        subg = sb("subg", [P, 1])
        work = sb("work", [P, 5376])

        ident = cst[:, C_ID:C_ID + P]
        flip = cst[:, C_FLIP:C_FLIP + P]
        before = cst[:, C_BEFORE:C_BEFORE + P]
        ones = cst[:, C_ONES:C_ONES + P]

        def slots(fill, n=1):
            s0 = fill % RING
            return ring[:, s0 * SLOT:(s0 + n) * SLOT]

        bias_raw = work[:, 0:512].rearrange("p (b k) -> p b k", b=2)
        bias_T = work[:, 512:768]
        qkv = {b: work[:, 768 + 512 * i:1280 + 512 * i].rearrange("p (b t) -> p b t", b=2)
               for i, b in enumerate("qkv")}
        probs = work[:, 2304:3072].rearrange("p (m k) -> p m k", m=2)
        probsT = work[:, 3072:3456]
        head_out = work[:, 3456:3712].rearrange("p (t d) -> p t d", t=TT)
        choice = work[0:BUCKETS + 1, 3712:3712 + 2 * REL]
        rows_sb = work[:, 4480:4480 + 2 * REL]
        table = work[0:BUCKETS + 1, 5248:5248 + HEADS]
        junk64 = work[:, 5264:5328]
        yT = xn[:, :, :, :].rearrange("p a k q -> p (a k q)").rearrange("p (h t) -> p h t", t=S)
        nmax = small[:, 0:4]
        sums = small[:, 4:8]
        esink = small[:, 8:10]
        den = small[:, 10:14]
        rden = small[:, 14:18]
        osq = small[:, 18:20]
        orstd = small[:, 20:22]
        lamdot = small[:, 22:24]
        lamexp = small[:, 24:26]
        neglam = small[:, 26:27]
        wg_raw = work[:, 0:KT * GROUPS]
        we_raw = work[:, 64:64 + KT * EXPERTS]
        rt = work[:, 1024:1024 + 16 * 64].rearrange("p (n t e) -> p n t e", n=16, t=TT)
        gl = rt[:, 0, :, 0:GROUPS]
        el, cand, one1, one2, masked = (rt[:, i, :, :] for i in (1, 2, 3, 4, 5))
        gcand = rt[:, 6, :, 0:GROUPS]
        gone = rt[:, 6, :, 8:8 + GROUPS]
        gexp = rt[:, 6, :, 16:16 + GROUPS]
        gmax = rt[:, 7, :, 0:1]
        gmin = rt[:, 7, :, 1:2]
        gsum = rt[:, 7, :, 2:3]
        m1 = rt[:, 7, :, 3:4]
        m2 = rt[:, 7, :, 4:5]
        cmin = rt[:, 7, :, 5:6]
        ed = rt[:, 7, :, 6:7]
        den2 = rt[:, 7, :, 7:8]
        w_a = rt[:, 7, :, 8:9]
        w_b = rt[:, 7, :, 9:10]
        gw = rt[:, 7, :, 10:11]
        iota_g = cst[:, C_IG:C_IE].rearrange("p (t g) -> p t g", t=TT)
        iota_e = cst[:, C_IE:C_TH].rearrange("p (t g) -> p t g", t=TT)
        o4 = work[:, 0:2048]
        sel = work[:, 2048:2304].rearrange("p (t c) -> p t c", t=TT)
        selg = work[:, 2304:2560].rearrange("p (t c) -> p t c", t=TT)
        selgT = work[:, 2560:2816]
        esig, sig1, sig, hmul, hid, hidT = (work[:, 2816 + P * i:2944 + P * i] for i in range(6))
        tokT = actT[:, :, 0:P]
        g_fin = work[:, 0:2048]
        p_tok = work[:, 2048:2560].rearrange("p (t c) -> p t c", t=TT)
        pT = work[:, 2560:3072].rearrange("p (k t) -> p k t", k=TT)
        zexp = work[:, 3072:4096].rearrange("p (b t c) -> p b t c", b=2, t=TT)
        zsig = work[:, 4096:5120].rearrange("p (b t c) -> p b t c", b=2, t=TT)
        flat_xn = xn[:, :, :, :].rearrange("p a k q -> p a (k q)")
        ple = flat_xn

        x_loaded = [sem(f"x_loaded{i}") for i in range(TT)]
        small_loaded = sem("small_loaded")
        SMALL_LOADS = 11
        router_loaded = sem("router_loaded")
        slot_loaded = [sem(f"slot_loaded{i}") for i in range(RING)]
        ring_used = sem("ring_used")
        table_masked = sem("table_masked")
        table_loaded = sem("table_loaded")
        rows_filled = sem("rows_filled")
        rows_copied = sem("rows_copied")
        rows_stored = sem("rows_stored")
        bias_loaded = [sem(f"bias_loaded{i}") for i in range(2)]
        bias_flipped = sem("bias_flipped")
        bias_ready = sem("bias_ready")
        squares_done = sem("squares_done")
        mean_done = sem("mean_done")
        rstd_done = sem("rstd_done")
        xn_ready = sem("xn_ready")
        dense_ready = [sem(f"dense_ready{i}") for i in range(2)]
        dense_taken = [sem(f"dense_taken{i}") for i in range(2)]
        lam_dots = sem("lam_dots")
        lam_exps = sem("lam_exps")
        logits_ready = sem("logits_ready")
        nmax_ready = sem("nmax_ready")
        exp_ready = sem("exp_ready")
        probs_ready = sem("probs_ready")
        probsT_filled = sem("probsT_filled")
        probsT_ready = sem("probsT_ready")
        pv_ready = sem("pv_ready")
        osq_ready = sem("osq_ready")
        omean_ready = sem("omean_ready")
        orstd_ready = sem("orstd_ready")
        head_out_ready = sem("head_out_ready")
        outT_ready = sem("outT_ready")
        y_ready = sem("y_ready")
        h_ready = sem("h_ready")
        router_ready = sem("router_ready")
        rlogits_ready = sem("rlogits_ready")
        chosen = sem("chosen")
        small_exps = sem("small_exps")
        ranks_filled = sem("ranks_filled")
        rounds_known = sem("rounds_known")
        dve_step = sem("dve_step")
        dve_loop = sem("dve_loop")
        sel_ready = sem("sel_ready")
        gather_filled = sem("gather_filled")
        gather_taken = sem("gather_taken")
        selgT_filled = sem("selgT_filled")
        selgT_ready = sem("selgT_ready")
        esig_ready = sem("esig_ready")
        hid_ready = sem("hid_ready")
        hidT_filled = sem("hidT_filled")
        hidT_ready = sem("hidT_ready")
        o4_dve = sem("o4_dve")
        o4_act = sem("o4_act")
        scatter_filled = sem("scatter_filled")
        scatter_taken = sem("scatter_taken")
        loop_done = sem("loop_done")
        tail_loaded = sem("tail_loaded")
        pT_filled = sem("pT_filled")
        pT_ready = sem("pT_ready")
        zexp_ready = sem("zexp_ready")
        out_ready = sem("out_ready")
        out_stored = sem("out_stored")

        w_in = A["w_in"][0].rearrange("(p t) n -> p t n", t=KT)
        w_out = A["w_out"][0].rearrange("(h p) n -> p h n", p=P)
        w1, w3 = (A[n][0].rearrange("e (p t) f -> e p (t f)", t=KT) for n in ("w1", "w3"))
        w2 = A["w2"][0].rearrange("e (j p) n -> e j p n", p=P)
        w_gate = A["w_ple_gate"][0].rearrange("(p t) n -> p t n", t=KT)
        w_ple = A["w_ple_proj"][0].rearrange("(k p) n -> k p n", p=P)
        x_t = A["x"][0].rearrange("(t p) n -> t p n", p=P)
        out_t = out[0].rearrange("(t p) n -> t p n", p=P)

        def slot_value(fill):
            return 16 * (fill // RING + 1)

        block = ctx.enter_context(nc.Block())

        @block.sync
        def _(sp):
            for t in range(TT):
                sp.dma_start(h[:, t, :], x_t[t]).then_inc(x_loaded[t], 16)

            def wait_slot(fill, turns=0):
                before_, experts = fill - RING, fill - RING - FILLS_HEAD
                if before_ < 0:
                    return
                if not isinstance(turns, int) or turns or experts >= 0:
                    sp.wait_ge(ring_used, turns + (RING + experts + 1))
                    return
                f = D_PROJ + before_ if before_ < FILLS_PROJ else D_OUT + (before_ - FILLS_PROJ) // 2
                sp.wait_ge(dense_ready[f % 2], f // 2 + 1)

            def fill_proj(n):
                wait_slot(n)
                col = PROJ[n][1]
                sp.dma_start(slots(n).rearrange("p (t c) -> p t c", t=KT),
                             w_in[:, :, col:col + HD]).then_inc(slot_loaded[n % RING], 16)

            for n in range(3):
                fill_proj(n)
            loads = 0
            for dst, src in (
                (cst[:, :], A["cst"]), (choice, A["choice"]),
                (g_mixT[:, :], A["g_mix"][0].rearrange("(p t) -> p t", t=KT)),
                (g_ffnT[:, :], A["g_ffn"][0].rearrange("(p t) -> p t", t=KT)),
                (g_pleT[:, :], A["g_ple"][0].rearrange("(p t) -> p t", t=KT)),
                (sinks[:, :], A["swa_sinks"].partition_broadcast(P)),
                (subg[:, :], A["diff_subln"][0].rearrange("(p a) -> p a", a=1)),
                (lam[:, 0, :], A["lam_q1"].partition_broadcast(P)),
                (lam[:, 1, :], A["lam_k1"].partition_broadcast(P)),
                (lam[:, 2, :], A["lam_q2"].partition_broadcast(P)),
                (lam[:, 3, :], A["lam_k2"].partition_broadcast(P)),
            ):
                sp.dma_start(dst, src).then_inc(small_loaded, 16)
                loads += 1
            assert loads == SMALL_LOADS
            sp.wait_ge(table_masked, 1)
            sp.dma_start(table[0:BUCKETS, :], A["rel_bias"]).then_inc(table_loaded, 16)
            for n in range(3, RING):
                fill_proj(n)
            for n in range(RING, FILLS_PROJ):
                fill_proj(n)
            for c in range(N_OUT):
                for half in range(2):
                    n = FILLS_PROJ + 2 * c + half
                    wait_slot(n)
                    sp.dma_start(slots(n).rearrange("p (h c) -> p h c", h=HEADS // 2),
                                 w_out[:, half * 8:half * 8 + 8, c * 256:c * 256 + 256])\
                      .then_inc(slot_loaded[n % RING], 16)

            def fill_expert(e, x, turns):
                for k in range(FILLS_X):
                    n = FILLS_HEAD + x * FILLS_X + k
                    if k < 8:
                        src = (w1, w3)[k % 2][e + x][:, (k // 2) * SLOT:(k // 2 + 1) * SLOT]
                    else:
                        src = w2[e + x, k - 8]
                    wait_slot(n, turns)
                    sp.dma_start(slots(n), src).then_inc(slot_loaded[n % RING], 16)

            for x in range(QUAD):
                fill_expert(0, x, 0)
            with sp.Fori(1, BLOCKS) as b:
                for x in range(QUAD):
                    fill_expert(b * QUAD, x, b * FILLS_IT)
            sp.wait_ge(rounds_known, 1)
            rounds = sp.value_load(rounds_i[0:1, 0:1], min_val=1, max_val=MAX_ROUNDS)
            with sp.If(rounds > 1):
                with sp.Fori(BLOCKS, rounds * BLOCKS, BLOCKS) as r:
                    with sp.Fori(0, BLOCKS) as b:
                        for x in range(QUAD):
                            fill_expert(b * QUAD, x, (r + b) * FILLS_IT)
            turns = rounds * (BLOCKS * FILLS_IT)
            for k in range(PLE // P):
                n = TAIL_PROJ + k
                wait_slot(n, turns)
                sp.dma_start(slots(n), w_ple[k]).then_inc(slot_loaded[n % RING], 16)
            for c in range(N_OUT):
                for half in range(2):
                    n = TAIL_GATE + 2 * c + half
                    if n - RING >= TAIL_GATE - PLE // P and n - RING < TAIL_GATE:
                        sp.wait_ge(dense_ready[(D_GATE - 1) % 2], D_GATE // 2)
                    else:
                        wait_slot(n, turns)
                    sp.dma_start(slots(n).rearrange("p (t c) -> p t c", t=KT // 2),
                                 w_gate[:, half * 8:half * 8 + 8, c * 256:c * 256 + 256])\
                      .then_inc(slot_loaded[n % RING], 16)
            for t in range(TT):
                sp.wait_ge(out_ready, t + 1)
                sp.dma_start(out_t[t], flat_xn[:, t, :]).then_inc(out_stored, 16)
            sp.wait_ge(out_stored, 16 * TT)

        @block.gpsimd
        def _(pool):
            def norm_power(n):
                pool.wait_ge(squares_done, TT * (n + 1))
                nc.gpsimd.tensor_scalar(sumsq[:, n, :], sumsq[:, n, :], 1.0 / D, EPS,
                                        ALU.mult, ALU.add).then_inc(mean_done, 1)
                pool.wait_ge(mean_done, n + 1)
                nc.gpsimd.tensor_tensor(rstd[:, n, :], sumsq[:, n, :], cst[:, C_POW:C_POW + TT],
                                        ALU.pow).then_inc(rstd_done, 1)

            pool.wait_ge(small_loaded, 16 * SMALL_LOADS)
            norm_power(0)
            pool.wait_ge(rows_copied, 2)
            pool.dma_start(bias_rows[0:SWA_HEADS, :], rows_sb[0:SWA_HEADS, 0:REL]).then_inc(rows_stored, 16)
            pool.dma_start(bias_rows[SWA_HEADS:HEADS, :], rows_sb[0:HEADS - SWA_HEADS, REL:2 * REL])\
                .then_inc(rows_stored, 16)
            pool.wait_ge(rows_stored, 32)

            def load_bias(a):
                if a >= 2:
                    pool.wait_ge(bias_flipped, a - 1)
                src = bass.AP(tensor=bias_rows.tensor, offset=a * REL, ap=[[1, P], [1, 2 * P]])
                pool.dma_start(bias_raw[:, a % 2, :], src).then_inc(bias_loaded[a % 2], 16)

            load_bias(0)
            load_bias(1)
            n_diff = 0
            for a in range(HEADS):
                if STEPS[a][0] == "diff":
                    n_diff += 1
                    pool.wait_ge(osq_ready, n_diff)
                    nc.gpsimd.tensor_scalar(osq, osq, 1.0 / HD, EPS, ALU.mult, ALU.add).then_inc(omean_ready, 1)
                    pool.wait_ge(omean_ready, n_diff)
                    nc.gpsimd.tensor_tensor(orstd, osq, cst[:, C_POW:C_POW + TT], ALU.pow)\
                        .then_inc(orstd_ready, 1)
                if a + 2 < HEADS:
                    load_bias(a + 2)
            pool.wait_ge(y_ready, HEADS)
            pool.dma_start(wg_raw, A["w_group"][0].rearrange("(p t) g -> p (t g)", t=KT)).then_inc(router_loaded, 16)
            pool.dma_start(we_raw, A["w_expert"][0].rearrange("(p t) g -> p (t g)", t=KT)).then_inc(router_loaded, 16)
            pool.wait_ge(router_loaded, 32)
            nc.gpsimd.tensor_copy(router[:, :, 0:GROUPS], wg_raw.rearrange("p (t g) -> p t g", t=KT))
            nc.gpsimd.tensor_copy(router[:, :, GROUPS:], we_raw.rearrange("p (t g) -> p t g", t=KT))\
                .then_inc(router_ready, 1)
            norm_power(1)
            pool.wait_ge(loop_done, 1)
            pool.dma_start(g_fin, A["g_final"].partition_broadcast(P)).then_inc(tail_loaded, 16)
            pool.dma_start(p_tok, A["p"][0, 0].rearrange("(t p) c -> p t c", p=P)).then_inc(tail_loaded, 16)
            norm_power(2)
            norm_power(3)

        @block.scalar
        def _(act):
            def squares(n, junk):
                for t in range(TT):
                    if n == 0:
                        act.wait_ge(x_loaded[t], 16)
                    nc.scalar.activation(junk[:, t, :], h[:, t, :], ACT.Square,
                                         accum_out=sumsq[:, n, t:t + 1]).then_inc(squares_done, 1)

            squares(0, flat_xn)
            act.wait_ge(lam_dots, 1)
            nc.scalar.activation(lamexp, lamdot, ACT.Exp).then_inc(lam_exps, 1)

            def take_block(n):
                f = D_PROJ + n
                b, _, buf = PROJ[n]
                act.wait_ge(dense_ready[f % 2], f // 2 + 1)
                nc.scalar.copy(qkv[b][:, buf, :], bank[f % 2][:, 0:S]).then_inc(dense_taken[f % 2], 1)

            def take_bias(a):
                act.wait_ge(bias_flipped, a + 1)
                nc.scalar.copy(bias_T, bank[7][:, 0:2 * P]).then_inc(bias_ready, 1)

            def exps(a):
                act.wait_ge(nmax_ready, a + 1)
                kind = STEPS[a][0]
                for m in range(2 if kind == "diff" else 1):
                    for t, (k0, k1) in enumerate(((0, P), (P, 3 * P))):
                        c = 2 * m + t
                        last = nc.scalar.activation(probs[:, m, k0:k1], probs[:, m, k0:k1], ACT.Exp,
                                                    bias=nmax[:, c:c + 1], accum_out=sums[:, c:c + 1])
                if kind == "swa":
                    last = nc.scalar.activation(esink, nmax[:, 0:TT], ACT.Exp, bias=sinks[:, a:a + 1])
                last.then_inc(exp_ready, 1)

            def take_probsT(a):
                act.wait_ge(probsT_filled, a + 1)
                nc.scalar.copy(probsT, bank[4][:, 0:3 * P]).then_inc(probsT_ready, 1)

            for s in range(HEADS + 1):
                names = [b for b, _ in STEPS[s][2]] if s < HEADS else []
                if s >= 1:
                    take_bias(s - 1)
                if "q" in names:
                    take_block(BLOCK_OF[s, "q"])
                if s >= 1:
                    exps(s - 1)
                if "k" in names:
                    take_block(BLOCK_OF[s, "k"])
                if s >= 1:
                    take_probsT(s - 1)
                if "v" in names:
                    take_block(BLOCK_OF[s, "v"])

            for i in range(2):
                act.wait_ge(dense_taken[i], D_NORM_B // 2)
            squares(1, flat_xn)
            act.wait_ge(chosen, 2)
            nc.scalar.activation(gexp, gexp, ACT.Exp).then_inc(small_exps, 1)
            nc.scalar.activation(ed, ed, ACT.Exp).then_inc(small_exps, 1)

            act.wait_ge(rounds_known, 1)
            rounds = act.value_load(rounds_i[0:1, 0:1], min_val=1, max_val=MAX_ROUNDS)
            with act.Fori(0, rounds * BLOCKS) as it:
                for x in range(QUAD):
                    n = it * QUAD + (x + 1)
                    act.wait_ge(ring_used, it * FILLS_IT + (RING + x * FILLS_X + 8))
                    nc.scalar.activation(esig, bank[x % 2][:, 0:P], ACT.Exp, scale=-1.0).then_inc(esig_ready, 1)
                    act.wait_ge(hidT_filled, n)
                    nc.scalar.copy(hidT, bank[4][:, 0:P]).then_inc(hidT_ready, 1)
                    act.wait_ge(ring_used, it * FILLS_IT + (RING + (x + 1) * FILLS_X))
                    for q in (2, 3):
                        last = nc.scalar.copy(o4[SLOTS * x:SLOTS * (x + 1), q * 512:q * 512 + 512],
                                              bank[5 + x % 2][SLOTS * q:SLOTS * (q + 1), :])
                    last.then_inc(o4_act, 1)

            act.wait_ge(loop_done, 1)
            squares(2, flat_xn)
            for c in range(N_OUT):
                f = D_PLE + c
                act.wait_ge(dense_ready[f % 2], f // 2 + 1)
                nc.scalar.copy(ple[:, :, c * 256:c * 256 + 256],
                               bank[f % 2][:, :].rearrange("p (t c) -> p t c", t=TT))\
                    .then_inc(dense_taken[f % 2], 1)
            for c in range(N_OUT):
                f = D_GATE + c
                act.wait_ge(dense_ready[f % 2], f // 2 + 1)
                if c >= 2:
                    act.wait_ge(h_ready, c - 1)
                nc.scalar.activation(zexp[:, c % 2, :, :].rearrange("p t c -> p (t c)"), bank[f % 2][:, :],
                                     ACT.Exp, scale=-1.0).then_inc(dense_taken[f % 2], 1)
            act.wait_ge(h_ready, N_OUT)
            squares(3, actT[:, :, :].rearrange("p k t -> p (k t)").rearrange("p (a n) -> p a n", a=TT))

        @block.vector
        def _(dve):
            steps = [0]

            def link(ins):
                steps[0] += 1
                ins.then_inc(dve_step, 1)
                dve.wait_ge(dve_step, steps[0])

            nc.vector.memset(table, NEG).then_inc(table_masked, 1)

            def normalise(n):
                dve.wait_ge(rstd_done, n + 1)
                for t in range(TT):
                    nc.vector.tensor_scalar(xn[:, t, :, :], h[:, t, :].rearrange("p (q k) -> p k q", k=KT),
                                            rstd[:, n, t:t + 1], None, ALU.mult).then_inc(xn_ready, 1)

            def take_transposed(first, gT):
                for i in range(NORM_FILLS):
                    f = first + i
                    dve.wait_ge(dense_ready[f % 2], f // 2 + 1)
                    nc.vector.tensor_tensor(
                        actT[:, 2 * i:2 * i + 2, :], bank[f % 2][:, :].rearrange("p (k t) -> p k t", k=2),
                        gT[:, 2 * i:2 * i + 2].unsqueeze(2).broadcast_to([P, 2, S]),
                        ALU.mult).then_inc(dense_taken[f % 2], 1)

            dve.wait_ge(small_loaded, 16 * SMALL_LOADS)
            normalise(0)
            for i, n in enumerate((SWA_HEADS, HEADS - SWA_HEADS)):
                dve.wait_ge(rows_filled, i + 1)
                nc.vector.tensor_copy(rows_sb[0:n, i * REL:(i + 1) * REL], bank[6 + i][0:n, 0:REL])\
                    .then_inc(rows_copied, 1)
            take_transposed(D_NORM_A, g_mixT)
            for i in range(2):
                last = nc.vector.tensor_tensor_reduce(junk64, lam[:, 2 * i, :], lam[:, 2 * i + 1, :], 1.0, 0.0,
                                                      ALU.mult, ALU.add, lamdot[:, i:i + 1])
                if i == 0:
                    link(last)
            last.then_inc(lam_dots, 1)
            nc.vector.tensor_scalar(nsinks[:, :], sinks[:, :], -1.0, None, ALU.mult)
            dve.wait_ge(lam_exps, 1)
            link(nc.vector.tensor_tensor(neglam, lamexp[:, 1:2], lamexp[:, 0:1], ALU.subtract))
            link(nc.vector.tensor_scalar(neglam, neglam, -LAMBDA_INIT, None, ALU.add))

            def softmax_in(a):
                kind = STEPS[a][0]
                scale = (HD // 2 if kind == "diff" else HD) ** -0.5
                maps = 2 if kind == "diff" else 1
                dve.wait_ge(bias_ready, a + 1)
                dve.wait_ge(logits_ready, a + 1)
                for m in range(maps):
                    nc.vector.scalar_tensor_tensor(probs[:, m, 0:P], bank[2 + m][:, 0:P], scale,
                                                   bias_T[:, P:2 * P], ALU.mult, ALU.add)
                    last = nc.vector.scalar_tensor_tensor(probs[:, m, P:3 * P], bank[2 + m][:, P:3 * P], scale,
                                                          bias_T, ALU.mult, ALU.add)
                link(last)
                for m in range(maps):
                    nc.vector.tensor_reduce(nmax[:, 2 * m:2 * m + 1], probs[:, m, 0:P], AX.X, ALU.max, negate=True)
                    last = nc.vector.tensor_reduce(nmax[:, 2 * m + 1:2 * m + 2], probs[:, m, P:3 * P], AX.X,
                                                   ALU.max, negate=True)
                if kind == "swa":
                    link(last)
                    last = nc.vector.tensor_scalar(nmax[:, 0:TT], nmax[:, 0:TT], nsinks[:, a:a + 1], None, ALU.min)
                last.then_inc(nmax_ready, 1)

            def softmax_out(a):
                kind = STEPS[a][0]
                dve.wait_ge(exp_ready, a + 1)
                if kind == "swa":
                    link(nc.vector.tensor_tensor(den[:, 0:TT], sums[:, 0:TT], esink, ALU.add))
                    last = nc.vector.reciprocal(rden[:, 0:TT], den[:, 0:TT])
                elif kind == "moba":
                    last = nc.vector.reciprocal(rden[:, 0:TT], sums[:, 0:TT])
                else:
                    link(nc.vector.reciprocal(rden, sums))
                    link(nc.vector.tensor_scalar(rden[:, TT:2 * TT], rden[:, TT:2 * TT], neglam, None, ALU.mult))
                    for t, (k0, k1) in enumerate(((0, P), (P, 3 * P))):
                        last = nc.vector.tensor_scalar(probs[:, 0, k0:k1], probs[:, 0, k0:k1], rden[:, t:t + 1],
                                                       None, ALU.mult)
                    link(last)
                    for t, (k0, k1) in enumerate(((0, P), (P, 3 * P))):
                        last = nc.vector.scalar_tensor_tensor(
                            probs[:, 0, k0:k1], probs[:, 1, k0:k1], rden[:, TT + t:TT + t + 1],
                            probs[:, 0, k0:k1], ALU.mult, ALU.add)
                last.then_inc(probs_ready, 1)

            diffs = [0]

            def take_out(a):
                pv = bank[5][:, 0:S].rearrange("p (t d) -> p t d", t=TT)
                dve.wait_ge(pv_ready, a + 1)
                if a >= 1:
                    dve.wait_ge(outT_ready, a)
                if STEPS[a][0] == "diff":
                    diffs[0] += 1
                    link(nc.vector.tensor_copy(head_out, pv))
                    for t in range(TT):
                        last = nc.vector.tensor_tensor_reduce(probs[:, 1, t * P:t * P + P], head_out[:, t, :],
                                                              head_out[:, t, :], 1.0, 0.0, ALU.mult, ALU.add,
                                                              osq[:, t:t + 1])
                    last.then_inc(osq_ready, 1)
                    dve.wait_ge(orstd_ready, diffs[0])
                    for t in range(TT):
                        last = nc.vector.tensor_scalar(head_out[:, t, :], head_out[:, t, :], orstd[:, t:t + 1],
                                                       None, ALU.mult)
                else:
                    for t in range(TT):
                        last = nc.vector.tensor_scalar(head_out[:, t, :], pv[:, t, :], rden[:, t:t + 1],
                                                       None, ALU.mult)
                last.then_inc(head_out_ready, 1)

            def take_outT(a):
                dve.wait_ge(outT_ready, a + 1)
                if STEPS[a][0] == "diff":
                    last = nc.vector.tensor_scalar(yT[:, a, :], bank[6][:, 0:S], subg[:, 0:1],
                                                   1.0 - LAMBDA_INIT, ALU.mult, ALU.mult)
                else:
                    last = nc.vector.tensor_copy(yT[:, a, :], bank[6][:, 0:S])
                last.then_inc(y_ready, 1)

            for s in range(1, HEADS + 2):
                if s >= 2:
                    take_outT(s - 2)
                if s <= HEADS:
                    softmax_in(s - 1)
                    softmax_out(s - 1)
                    take_out(s - 1)

            for c in range(N_OUT):
                f = D_OUT + c
                dve.wait_ge(dense_ready[f % 2], f // 2 + 1)
                hc = h[:, :, c * 256:c * 256 + 256]
                ins = nc.vector.tensor_tensor(hc, bank[f % 2][:, :].rearrange("p (t c) -> p t c", t=TT), hc, ALU.add)
                ins.then_inc(dense_taken[f % 2], 1)

            normalise(1)
            take_transposed(D_NORM_B, g_ffnT)

            V = nc.vector

            def over(ap, n):
                return ap.broadcast_to([P, TT, n])

            def first_max(onehot, values, top, scratch, low, iota, n):
                link(V.tensor_reduce(top, values, AX.X, ALU.max))
                link(V.tensor_tensor(onehot, values, over(top, n), ALU.is_ge))
                link(V.scalar_tensor_tensor(scratch, onehot, -64.0, iota, ALU.mult, ALU.add))
                link(V.tensor_reduce(low, scratch, AX.X, ALU.min))
                link(V.tensor_tensor(onehot, scratch, over(low, n), ALU.is_equal))

            dve.wait_ge(rlogits_ready, 1)
            rl = bank[2][:, 0:TT * (GROUPS + EXPERTS)].rearrange("p (t e) -> p t e", t=TT)
            V.tensor_copy(gl, rl[:, :, 0:GROUPS])
            link(V.tensor_copy(el, rl[:, :, GROUPS:]))
            first_max(gone, gl, gmax, gcand, gmin, iota_g, GROUPS)
            V.tensor_tensor(gexp, gl, over(gmax, GROUPS), ALU.subtract).then_inc(chosen, 1)
            link(V.tensor_scalar(gcand, gone, 1.0, -NEG, ALU.subtract, ALU.mult))
            for t in range(TT):
                last = V.tensor_tensor(
                    masked[:, t, :].rearrange("p (g e) -> p g e", g=GROUPS),
                    el[:, t, :].rearrange("p (g e) -> p g e", g=GROUPS),
                    gcand[:, t, :].unsqueeze(2).broadcast_to([P, GROUPS, PER_GROUP]), ALU.add)
            link(last)
            first_max(one1, masked, m1, cand, cmin, iota_e, EXPERTS)
            link(V.scalar_tensor_tensor(masked, one1, 3 * NEG, masked, ALU.mult, ALU.add))
            first_max(one2, masked, m2, cand, cmin, iota_e, EXPERTS)
            V.tensor_tensor(ed, m2, m1, ALU.subtract).then_inc(chosen, 1)
            V.tensor_tensor(cand, one1, one2, ALU.add).then_inc(chosen, 1)
            dve.wait_ge(small_exps, 2)
            link(V.tensor_reduce(gsum, gexp, AX.X, ALU.add))
            link(V.reciprocal(gw, gsum))
            link(V.tensor_scalar(den2, ed, 1.0, None, ALU.add))
            link(V.reciprocal(w_a, den2))
            link(V.tensor_tensor(w_a, w_a, gw, ALU.mult))
            link(V.tensor_tensor(w_b, w_a, ed, ALU.mult))
            V.tensor_tensor(one1, one1, over(w_a, EXPERTS), ALU.mult)
            link(V.tensor_tensor(one2, one2, over(w_b, EXPERTS), ALU.mult))
            link(V.tensor_tensor(gate_of[:, :, :], one1, one2, ALU.add))
            dve.wait_ge(ranks_filled, 1)
            rank = bank[3][:, 0:TT * EXPERTS].rearrange("p (t e) -> p t e", t=TT)
            total = bank[3][:, TT * EXPERTS:(TT + 1) * EXPERTS]
            link(V.scalar_tensor_tensor(slot_of[:, :, :], rank, 1.0, cand, ALU.add, ALU.mult))
            link(V.tensor_scalar(slot_of[:, :, :], slot_of[:, :, :], -1.0, None, ALU.add))
            fullest = rt[:, 8, 0, 0:1]
            over_th = rt[:, 8, 1, 0:MAX_ROUNDS]
            nround = rt[:, 8, 0, 1:2]
            link(V.tensor_reduce(fullest, total, AX.X, ALU.max))
            link(V.tensor_tensor(over_th, fullest.broadcast_to([P, MAX_ROUNDS]), cst[:, C_TH:C_POW], ALU.is_gt))
            link(V.tensor_reduce(nround, over_th, AX.X, ALU.add))
            V.tensor_copy(rounds_i[:, :], nround).then_inc(rounds_known, 1)

            dve.wait_ge(rounds_known, 1)
            rounds = dve.value_load(rounds_i[0:1, 0:1], min_val=1, max_val=MAX_ROUNDS)
            LINKS = 1 + 3 * QUAD
            with dve.Fori(0, rounds * BLOCKS, BLOCKS) as r:
                with dve.Fori(0, BLOCKS) as b:
                    it = r + b
                    done = [0]

                    def link_in(ins):
                        done[0] += 1
                        ins.then_inc(dve_loop, 1)
                        dve.wait_ge(dve_loop, it * LINKS + done[0])

                    cols = bass.ds(b * QUAD, QUAD)
                    slot_no = cst[:, C_SLOT:C_SLOT + P].rearrange("p (e s) -> p e s", e=QUAD)
                    for t in range(TT):
                        last = nc.vector.tensor_tensor(
                            sel[:, t, :].rearrange("p (e s) -> p e s", e=QUAD),
                            slot_of[:, t, cols].unsqueeze(2).broadcast_to([P, QUAD, SLOTS]), slot_no, ALU.is_equal)
                    link_in(last)
                    for t in range(TT):
                        last = nc.vector.tensor_tensor(
                            selg[:, t, :].rearrange("p (e s) -> p e s", e=QUAD),
                            sel[:, t, :].rearrange("p (e s) -> p e s", e=QUAD),
                            gate_of[:, t, cols].unsqueeze(2).broadcast_to([P, QUAD, SLOTS]), ALU.mult)
                    last.then_inc(sel_ready, 1)
                    nc.vector.tensor_scalar(slot_of[:, :, cols], slot_of[:, :, cols], -float(SLOTS), None, ALU.add)
                    for i in range(4):
                        dve.wait_ge(gather_filled, it * 4 + (i + 1))
                        nc.vector.tensor_tensor(
                            tokT[:, 4 * i:4 * i + 4, :], bank[2 + i % 2][:, :].rearrange("p (k c) -> p k c", k=4),
                            g_ffnT[:, 4 * i:4 * i + 4].unsqueeze(2).broadcast_to([P, 4, P]),
                            ALU.mult).then_inc(gather_taken, 1)
                    dve.wait_ge(selgT_filled, it + 1)
                    nc.vector.tensor_copy(selgT, bank[4][:, 0:S]).then_inc(selgT_ready, 1)
                    for x in range(QUAD):
                        n = it * QUAD + (x + 1)
                        dve.wait_ge(esig_ready, n)
                        link_in(nc.vector.tensor_scalar(sig1, esig, 1.0, None, ALU.add))
                        link_in(nc.vector.reciprocal(sig, sig1))
                        link_in(nc.vector.tensor_tensor(hmul, bank[x % 2][:, 0:P], sig, ALU.mult))
                        nc.vector.tensor_tensor(hid, bank[x % 2][:, P:2 * P], hmul, ALU.mult).then_inc(hid_ready, 1)
                        dve.wait_ge(ring_used, it * FILLS_IT + (RING + (x + 1) * FILLS_X))
                        for q in (0, 1):
                            last = nc.vector.tensor_copy(o4[SLOTS * x:SLOTS * (x + 1), q * 512:q * 512 + 512],
                                                         bank[5 + x % 2][SLOTS * q:SLOTS * (q + 1), :])
                        last.then_inc(o4_dve, 1)
                    for i in range(2 * TT * 2):
                        t, q = i // 4, i % 4
                        dve.wait_ge(scatter_filled, it * 8 + (i + 1))
                        hc = h[:, t, q * 512:q * 512 + 512]
                        nc.vector.tensor_tensor(hc, bank[2 + i % 2][:, :], hc, ALU.add).then_inc(scatter_taken, 1)
            nc.vector.memset(small[:, 60:61], 0.0).then_inc(loop_done, 1)

            normalise(2)
            dve.wait_ge(pT_filled, 1)
            nc.vector.tensor_copy(pT, bank[4][:, :].rearrange("p (k t) -> p k t", k=2)).then_inc(pT_ready, 1)
            take_transposed(D_NORM_C, g_pleT)
            for c in range(N_OUT):
                f = D_GATE + c
                z, sg = zexp[:, c % 2, :, :], zsig[:, c % 2, :, :]
                dve.wait_ge(dense_taken[f % 2], f // 2 + 1)
                link(nc.vector.tensor_scalar(z, z, 1.0, None, ALU.add))
                link(nc.vector.reciprocal(sg, z))
                link(nc.vector.tensor_tensor(sg, sg, ple[:, :, c * 256:c * 256 + 256], ALU.mult))
                hc = h[:, :, c * 256:c * 256 + 256]
                nc.vector.tensor_tensor(hc, sg, hc, ALU.add).then_inc(h_ready, 1)
            dve.wait_ge(rstd_done, 4)
            dve.wait_ge(tail_loaded, 32)
            for t in range(TT):
                nc.vector.scalar_tensor_tensor(flat_xn[:, t, :], h[:, t, :], rstd[:, 3, t:t + 1], g_fin,
                                               ALU.mult, ALU.mult).then_inc(out_ready, 1)

        @block.tensor
        def _(pe):
            mm = nc.tensor.matmul

            pe.wait_ge(small_loaded, 16 * SMALL_LOADS)
            pe.wait_ge(table_loaded, 16)
            mm(bank[6][0:SWA_HEADS, 0:REL], table[:, 0:SWA_HEADS], choice[:, REL:2 * REL],
               start=True, stop=True).then_inc(rows_filled, 1)
            mm(bank[7][0:HEADS - SWA_HEADS, 0:REL], table[:, SWA_HEADS:HEADS], choice[:, 0:REL],
               start=True, stop=True).then_inc(rows_filled, 1)

            def bank_free(f):
                if f >= 2:
                    pe.wait_ge(dense_taken[f % 2], f // 2)

            def transpose_act(first, n):
                pe.wait_ge(xn_ready, TT * (n + 1))
                for i in range(NORM_FILLS):
                    f = first + i
                    bank_free(f)
                    for k in range(2):
                        for t in range(TT):
                            last = nc.tensor.transpose(bank[f % 2][:, (2 * k + t) * P:(2 * k + t + 1) * P],
                                                       xn[:, t, 2 * i + k, :], ident)
                    last.then_inc(dense_ready[f % 2], 1)

            def act_ready(first):
                for b in range(2):
                    pe.wait_ge(dense_taken[b], (first + NORM_FILLS) // 2)

            def slot_here(fill, turns=0):
                pe.wait_ge(slot_loaded[fill % RING], turns + slot_value(fill))

            transpose_act(D_NORM_A, 0)
            act_ready(D_NORM_A)

            def project(n):
                f = D_PROJ + n
                w = slots(n).rearrange("p (k c) -> p k c", k=KT)
                bank_free(f)
                slot_here(n)
                if PROJ[n][0] == "v":
                    for t in range(TT):
                        for k in range(KT):
                            last = mm(bank[f % 2][:, t * P:(t + 1) * P], actT[:, k, t * P:(t + 1) * P], w[:, k, :],
                                      start=k == 0, stop=k == KT - 1)
                else:
                    for k in range(KT):
                        last = mm(bank[f % 2][:, 0:S], w[:, k, :], actT[:, k, :], start=k == 0, stop=k == KT - 1)
                last.then_inc(dense_ready[f % 2], 1)

            def flip_bias(a):
                pe.wait_ge(bias_loaded[a % 2], 16 * (a // 2 + 1))
                mm(bank[7][:, 0:2 * P], flip, bias_raw[:, a % 2, :], start=True, stop=True).then_inc(bias_flipped, 1)

            def logits(a):
                kind, kv, _ = STEPS[a]
                need = max(n for (hh, b), n in BLOCK_OF.items() if hh <= a and b in "qk")
                for b in range(2):
                    fs = [f for f in range(D_PROJ, D_PROJ + need + 1) if f % 2 == b]
                    pe.wait_ge(dense_taken[b], fs[-1] // 2 + 1)
                q, k = qkv["q"][:, a % 2, :], qkv["k"][:, kv % 2, :]
                width = HD // 2 if kind == "diff" else HD
                for m in range(HD // width):
                    r0, r1 = m * width, (m + 1) * width
                    mm(bank[2 + m][:, 0:P], q[r0:r1, 0:P], k[r0:r1, 0:P], start=True, stop=True)
                    last = mm(bank[2 + m][:, P:3 * P], q[r0:r1, P:2 * P], k[r0:r1, :], start=True, stop=True)
                last.then_inc(logits_ready, 1)

            def transpose_probs(a):
                pe.wait_ge(probs_ready, a + 1)
                for i in range(3):
                    last = nc.tensor.transpose(bank[4][:, i * P:(i + 1) * P], probs[:, 0, i * P:(i + 1) * P], ident)
                last.then_inc(probsT_filled, 1)

            def times_v(a):
                kv = STEPS[a][1]
                v = qkv["v"][:, kv % 2, :]
                pe.wait_ge(probsT_ready, a + 1)
                mm(bank[5][:, 0:P], probsT[:, 0:P], v[:, 0:P], start=True, stop=True)
                mm(bank[5][:, P:2 * P], probsT[:, P:2 * P], v[:, 0:P], start=True, stop=False)
                mm(bank[5][:, P:2 * P], probsT[:, 2 * P:3 * P], v[:, P:2 * P], start=False, stop=True)\
                    .then_inc(pv_ready, 1)

            def transpose_out(a):
                pe.wait_ge(head_out_ready, a + 1)
                for t in range(TT):
                    last = nc.tensor.transpose(bank[6][:, t * P:(t + 1) * P], head_out[:, t, :], ident)
                last.then_inc(outT_ready, 1)

            for s in range(HEADS + 2):
                names = [b for b, _ in STEPS[s][2]] if s < HEADS else []
                live = 1 <= s <= HEADS
                if live:
                    flip_bias(s - 1)
                if "q" in names:
                    project(BLOCK_OF[s, "q"])
                if s >= 2:
                    transpose_out(s - 2)
                if live:
                    logits(s - 1)
                if "k" in names:
                    project(BLOCK_OF[s, "k"])
                if live:
                    transpose_probs(s - 1)
                if "v" in names:
                    project(BLOCK_OF[s, "v"])
                if live:
                    times_v(s - 1)

            pe.wait_ge(y_ready, HEADS)

            def dense_chunk(f, fill, act_tiles, turns=0):
                w = slots(fill, 2).rearrange("p (k c) -> p k c", k=KT)
                bank_free(f)
                slot_here(fill, turns)
                slot_here(fill + 1, turns)
                for t in range(TT):
                    for k in range(KT):
                        last = mm(bank[f % 2][:, t * 256:(t + 1) * 256], act_tiles[:, k, t * P:(t + 1) * P],
                                  w[:, k, :], start=k == 0, stop=k == KT - 1)
                last.then_inc(dense_ready[f % 2], 1)

            for c in range(N_OUT):
                dense_chunk(D_OUT + c, FILLS_PROJ + 2 * c, yT)

            transpose_act(D_NORM_B, 1)
            act_ready(D_NORM_B)
            pe.wait_ge(router_ready, 1)
            n_r = GROUPS + EXPERTS
            for t in range(TT):
                for k in range(KT):
                    last = mm(bank[2][:, t * n_r:(t + 1) * n_r], actT[:, k, t * P:(t + 1) * P], router[:, k, :],
                              start=k == 0, stop=k == KT - 1)
            last.then_inc(rlogits_ready, 1)
            pe.wait_ge(chosen, 3)
            picked = rt[:, 2, :, :]
            rank = bank[3]
            mm(rank[:, 0:EXPERTS], before, picked[:, 0, :], start=True, stop=True).then_inc(ring_used, RING)
            mm(rank[:, EXPERTS:2 * EXPERTS], ones, picked[:, 0, :], start=True, stop=False)
            mm(rank[:, EXPERTS:2 * EXPERTS], before, picked[:, 1, :], start=False, stop=True)
            mm(rank[:, 2 * EXPERTS:3 * EXPERTS], ones, picked[:, 0, :], start=True, stop=False)
            mm(rank[:, 2 * EXPERTS:3 * EXPERTS], ones, picked[:, 1, :], start=False, stop=True)\
                .then_inc(ranks_filled, 1)

            pe.wait_ge(rounds_known, 1)
            rounds = pe.value_load(rounds_i[0:1, 0:1], min_val=1, max_val=MAX_ROUNDS)
            with pe.Fori(0, rounds * BLOCKS) as it:
                pe.wait_ge(sel_ready, it + 1)
                for i in range(4):
                    if i >= 2:
                        pe.wait_ge(gather_taken, it * 4 + (i - 1))
                    for k in range(4):
                        for t in range(TT):
                            last = mm(bank[2 + i % 2][:, k * P:(k + 1) * P], xn[:, t, 4 * i + k, :], sel[:, t, :],
                                      start=t == 0, stop=t == TT - 1)
                    last.then_inc(gather_filled, 1)
                for t in range(TT):
                    last = nc.tensor.transpose(bank[4][:, t * P:(t + 1) * P], selg[:, t, :], ident)
                last.then_inc(selgT_filled, 1)
                pe.wait_ge(selgT_ready, it + 1)
                pe.wait_ge(gather_taken, it * 4 + 4)
                turns = it * FILLS_IT
                for x in range(QUAD):
                    n = it * QUAD + (x + 1)
                    for quarter in range(4):
                        fill = FILLS_HEAD + x * FILLS_X + 2 * quarter
                        slot_here(fill, turns)
                        slot_here(fill + 1, turns)
                        w = slots(fill, 2).rearrange("p (m k f) -> p k m f", m=2, k=4)
                        for k in range(4):
                            for j in range(QUAD):
                                last = mm(bank[x % 2][SLOTS * j:SLOTS * (j + 1), 0:2 * P]
                                          .rearrange("p (m f) -> p m f", m=2),
                                          tokT[:, 4 * quarter + k, SLOTS * x:SLOTS * (x + 1)],
                                          w[:, k, :, j * P:(j + 1) * P],
                                          start=quarter == 0 and k == 0, stop=quarter == 3 and k == 3)
                        last.then_inc(ring_used, 2)
                    pe.wait_ge(hid_ready, n)
                    nc.tensor.transpose(bank[4][:, 0:P], hid, ident).then_inc(hidT_filled, 1)
                    pe.wait_ge(hidT_ready, n)
                    for j in range(JT):
                        fill = FILLS_HEAD + x * FILLS_X + 8 + j
                        slot_here(fill, turns)
                        w = slots(fill)
                        for q in range(QUAD):
                            last = mm(bank[5 + x % 2][SLOTS * q:SLOTS * (q + 1), :], hidT[:, SLOTS * j:SLOTS * (j + 1)],
                                      w[:, q * 512:(q + 1) * 512], start=j == 0, stop=j == JT - 1)
                        last.then_inc(ring_used, 1)
                pe.wait_ge(o4_dve, it * QUAD + QUAD)
                pe.wait_ge(o4_act, it * QUAD + QUAD)
                for i in range(8):
                    t, q = i // 4, i % 4
                    if i >= 2:
                        pe.wait_ge(scatter_taken, it * 8 + (i - 1))
                    mm(bank[2 + i % 2][:, :], selgT[:, t * P:(t + 1) * P], o4[:, q * 512:(q + 1) * 512],
                       start=True, stop=True).then_inc(scatter_filled, 1)

            turns = rounds * (BLOCKS * FILLS_IT)
            pe.wait_ge(tail_loaded, 32)
            for k in range(2):
                for t in range(TT):
                    last = nc.tensor.transpose(bank[4][:, (2 * k + t) * P:(2 * k + t + 1) * P],
                                               p_tok[:, t, k * P:(k + 1) * P], ident)
            last.then_inc(pT_filled, 1)
            transpose_act(D_NORM_C, 2)
            pe.wait_ge(pT_ready, 1)
            for k in range(2):
                slot_here(TAIL_PROJ + k, turns)
            act_ready(D_NORM_C)
            for c in range(N_OUT):
                f = D_PLE + c
                bank_free(f)
                for t in range(TT):
                    for k in range(2):
                        last = mm(bank[f % 2][:, t * 256:(t + 1) * 256], pT[:, k, t * P:(t + 1) * P],
                                  slots(TAIL_PROJ + k)[:, c * 256:(c + 1) * 256], start=k == 0, stop=k == 1)
                last.then_inc(dense_ready[f % 2], 1)
            for c in range(N_OUT):
                dense_chunk(D_GATE + c, TAIL_GATE + 2 * c, actT, turns)


_INPUTS = ["x", "p", "rel_bias", "g_final", "g_mix", "w_in", "swa_sinks", "lam_q1", "lam_k1", "lam_q2", "lam_k2",
           "diff_subln", "w_out", "g_ffn", "w_group", "w_expert", "w1", "w3", "w2", "g_ple", "w_ple_gate",
           "w_ple_proj"]


def kernel(**inputs):
    import concourse.bacc as bacc
    from concourse.bass_utils import run_bass_kernel_spmd

    nc = bacc.Bacc("TRN2", target_bir_lowering=False, num_devices=1)
    arrays = {f"in_{n}": np.ascontiguousarray(inputs[n]) for n in _INPUTS}
    arrays["in_cst"] = constants()
    arrays["in_choice"] = bucket_choice()
    A = {n[3:]: nc.dram_tensor(n, a.shape, mybir.dt.from_np(a.dtype), kind="ExternalInput").ap()
         for n, a in arrays.items()}
    out = nc.dram_tensor("out_h", (1, S, D), F32, kind="ExternalOutput").ap()
    layer(nc, A, out)
    r = run_bass_kernel_spmd(nc, [arrays], core_ids=[0])
    return r.results[0]["out_h"]
```

```python
import math
from contextlib import ExitStack

import numpy as np
import concourse.bass as bass
from concourse import mybir

F32 = mybir.dt.float32
F32R = mybir.dt.float32r
I32 = mybir.dt.int32
ALU = mybir.AluOpType
ACT = mybir.ActivationFunctionType
AX = mybir.AxisListType

P = 128
D = 2048
S = 256
TT = S // P
KT = D // P
HD = 128
SWA_HEADS, SWA_KV, MOBA_HEADS, DIFF_HEADS = 6, 2, 4, 6
HEADS = SWA_HEADS + MOBA_HEADS + DIFF_HEADS
WINDOW = 128
BUCKETS, EXACT, MAX_DIST = 32, 16, 128
GROUPS, PER_GROUP = 4, 8
EXPERTS = GROUPS * PER_GROUP
DE = 512
JT = DE // P
PLE = 256
EPS = 1e-6
NEG = -1e30
LAMBDA_INIT = 0.8 - 0.6 * math.exp(-0.3 * 0)

SLOT = 2048
RING = 16
HEAD_RING = 8
SLOTS = 32
QUAD = P // SLOTS
BLOCKS = EXPERTS // QUAD
MAX_ROUNDS = S // SLOTS
REL = 3 * P

C_ID, C_FLIP, C_BEFORE, C_ONES, C_SLOT = (i * P for i in range(5))
C_IG = 5 * P
C_IE = C_IG + TT * GROUPS
C_TH = C_IE + TT * EXPERTS
C_POW = C_TH + MAX_ROUNDS
C_END = C_POW + 4


def constants():
    c = np.zeros((P, C_END), np.float32)
    i = np.arange(P)
    c[i, C_ID + i] = 1.0
    c[i, C_FLIP + P - 1 - i] = 1.0
    c[:, C_BEFORE:C_BEFORE + P] = i[:, None] < i[None, :]
    c[:, C_ONES:C_ONES + P] = 1.0
    c[:, C_SLOT:C_SLOT + P] = i[None, :] % SLOTS
    c[:, C_IG:C_IE] = np.arange(TT * GROUPS) % GROUPS
    c[:, C_IE:C_TH] = np.arange(TT * EXPERTS) % EXPERTS
    c[:, C_TH:C_POW] = np.arange(MAX_ROUNDS) * SLOTS
    c[:, C_POW:C_END] = -0.5
    return c


def bucket_choice():
    dist = 2 * P - 1 - np.arange(REL)
    n = np.maximum(dist, 0)
    nf = np.maximum(n, 1).astype(np.float32)
    large = EXACT + (np.log(nf / np.float32(EXACT)) / np.float32(math.log(MAX_DIST / EXACT))
                     * (BUCKETS - EXACT)).astype(np.int32)
    bucket = np.where(n < EXACT, n, np.minimum(large, BUCKETS - 1))
    c = np.zeros((BUCKETS + 1, 2, REL), np.float32)
    for swa in range(2):
        seen = (dist >= 0) & ((dist < WINDOW) | (swa == 0))
        c[np.where(seen, bucket, BUCKETS), swa, np.arange(REL)] = 1.0
    return c.reshape(BUCKETS + 1, 2 * REL)


ORDER = [0, 10, 1, 11, 2, 12, 3, 13, 4, 14, 5, 15, 6, 7, 8, 9]
assert sorted(ORDER) == list(range(HEADS))


def head_plan():
    kv_cols = SWA_HEADS * HD
    moba = kv_cols + 2 * SWA_KV * HD
    diff = moba + 3 * MOBA_HEADS * HD
    plan, own = [], 0
    for a in ORDER:
        if a < SWA_HEADS:
            g = a // (SWA_HEADS // SWA_KV)
            blocks = [("q", a * HD)]
            if a % (SWA_HEADS // SWA_KV) == 0:
                blocks += [("k", kv_cols + g * HD), ("v", kv_cols + (SWA_KV + g) * HD)]
            plan.append(("swa", 2, blocks))
            continue
        kind, base, n, h = (("moba", moba, MOBA_HEADS, a - SWA_HEADS) if a < SWA_HEADS + MOBA_HEADS else
                            ("diff", diff, DIFF_HEADS, a - SWA_HEADS - MOBA_HEADS))
        plan.append((kind, own % 2, [(b, base + (i * n + h) * HD) for i, b in enumerate("qkv")]))
        own += 1
    return plan


STEPS = head_plan()
PROJ = []
NEED_K = []
START = []
for _i, (_kind, _kv, _blocks) in enumerate(STEPS):
    for _b, _col in _blocks:
        PROJ.append((_b, _col, _i % 2 if _b == "q" else _kv))
    NEED_K.append(len(PROJ) - (_blocks[-1][0] == "v"))
    START.append(len(PROJ) if _i == 0 else max(START[-1] + 2, len(PROJ)))
OUT_AT = [n + 3 for n in START[:-1]] + [START[-1] + 2]
V_BLOCKS = [n for n, _block in enumerate(PROJ) if _block[0] == "v"]

N_PROJ = len(PROJ)
N_OUT = D // 256
HALVES = [(0, 0), (1, 0), (0, 1), (1, 1)] + [(c, half) for c in range(2, N_OUT) for half in range(2)]
N_HEAD = N_PROJ + len(HALVES)
HEAD_TURNS = N_HEAD // HEAD_RING
HI_RING = 4
FILLS_X = 12
FILLS_IT = QUAD * FILLS_X
assert N_HEAD % HEAD_RING == 0 and FILLS_IT % RING == 0 and START[-1] == N_PROJ
HALF_READY = [max(ORDER.index(a) for a in range(8 * half, 8 * half + 8)) + 1 for half in range(2)]

D_PROJ = 0
D_OUT = D_PROJ + N_PROJ
D_PLE = D_OUT + N_OUT
D_GATE = D_PLE + N_OUT
D_END = D_GATE + N_OUT
NORM_FILLS = KT // 2


def layer(nc, A, out):
    with ExitStack() as ctx:
        def sem(name):
            return ctx.enter_context(nc.semaphore(name))

        bank = [ctx.enter_context(nc.psum_tensor(f"bank{i}", [P, 512], F32)) for i in range(8)]
        bias_rows = nc.dram_tensor("bias_rows", [HEADS, REL], F32, kind="Internal").ap()

        KB = 1024
        base = (nc.sbuf_base + 31) // 32 * 32
        RING_AT = base
        U_AT = RING_AT + HEAD_RING * SLOT * 4
        Y_AT = U_AT + 32 * KB
        W_AT = Y_AT + 32 * KB
        H_AT = W_AT + 32 * KB
        at = [H_AT + 16 * KB]

        def place(name, shape, offset, dt=F32):
            return nc.alloc_sbuf_tensor_at(name, shape, dt, offset=offset)

        def sb(name, shape, dt=F32):
            o = at[0]
            at[0] += (int(np.prod(shape[1:])) * 4 + 31) // 32 * 32
            return place(name, shape, o, dt)

        ring_a = place("ring_a", [P, HEAD_RING * SLOT], RING_AT)
        uhi = place("uhi", [P, KT, S], U_AT, F32R)
        ulo = place("ulo", [P, KT, S], U_AT + 16 * KB, F32R)
        hp = place("hp", [P, TT, KT, P], U_AT)
        ring_u = place("ring_u", [P, 2 * SLOT], U_AT + 16 * KB)
        out_sb = place("out_sb", [P, TT, D], U_AT)
        yhi = place("yhi", [P, HEADS, S], Y_AT, F32R)
        ylo = place("ylo", [P, HEADS, S], Y_AT + 16 * KB, F32R)
        ring_y = place("ring_y", [P, 4 * SLOT], Y_AT)
        ring_w = place("ring_w", [P, 2 * SLOT], W_AT)
        tokT = place("tokT", [P, KT, P], W_AT + 16 * KB)
        hT = place("hT", [P, 4, 2, S], W_AT + 16 * KB)
        ple0 = place("ple0", [P, D], W_AT + 24 * KB)
        gate_junk = place("gate_junk", [P, TT, D], W_AT)
        gate_sig = place("gate_sig", [P, 2, TT, 256], W_AT)
        whi = [[place(f"whi{p}{i}", [P, SLOT], o + 8 * KB * i, F32R) for i in range(HI_RING)]
               for p, o in enumerate((W_AT, Y_AT))]
        wlo = [place(f"wlo{i}", [P, SLOT], RING_AT + 8 * KB * i, F32R) for i in range(HEAD_RING)]
        h = place("h", [P, TT, D], H_AT)

        cst = sb("cst", [P, C_END])
        g_mixT, g_ffnT, g_pleT = (sb(f"gT{i}", [P, KT]) for i in range(3))
        router = sb("router", [P, KT, GROUPS + EXPERTS])
        slot_of = sb("slot_of", [P, TT, EXPERTS])
        gate_of = sb("gate_of", [P, TT, EXPERTS])
        rounds_i = sb("rounds_i", [P, 1], I32)
        sq = sb("sq", [P, 4, TT, N_OUT])
        sumsq = sb("sumsq", [P, 4, TT])
        rstd = sb("rstd", [P, 4, TT])
        lam = sb("lam", [P, 4, HD // 2])
        small = sb("small", [P, 64])
        sinks = sb("sinks", [P, SWA_HEADS])
        nsinks = sb("nsinks", [P, SWA_HEADS])
        subg = sb("subg", [P, 2])
        work = sb("work", [P, 5632])
        assert at[0] <= nc.sbuf_usable_end, at[0]

        ident = cst[:, C_ID:C_ID + P]
        flip = cst[:, C_FLIP:C_FLIP + P]
        before = cst[:, C_BEFORE:C_BEFORE + P]
        ones = cst[:, C_ONES:C_ONES + P]

        def slots(pos, n=1):
            pos %= RING
            for tile, first, count in ((ring_a, 0, 8), (ring_u, 8, 2), (ring_y, 10, 4), (ring_w, 14, 2)):
                if first <= pos and pos + n <= first + count:
                    return tile[:, (pos - first) * SLOT:(pos - first + n) * SLOT]
            raise ValueError(pos)

        bias_raw = work[:, 0:512].rearrange("p (b k) -> p b k", b=2)
        bias_T = work[:, 512:768]
        qkv = {b: [work[:, 768 + 512 * i:1024 + 512 * i], work[:, 1024 + 512 * i:1280 + 512 * i]]
               for i, b in enumerate("qkv")}
        v_raw = work[:, 3712:3968]
        qkv["k"].append(work[:, 3968:4224])
        qkv["v"].append(work[:, 4224:4480])
        probs = work[:, 2304:3072].rearrange("p (m k) -> p m k", m=2)
        probsT = work[:, 3072:3456]
        head_out = work[:, 3456:3712].rearrange("p (t d) -> p t d", t=TT)
        choice = work[0:BUCKETS + 1, 3712:3712 + 2 * REL]
        rows_sb = work[:, 4480:4480 + 2 * REL]
        table = work[0:BUCKETS + 1, 5248:5248 + HEADS]
        diag = work[:, 5312:5312 + 2 * P].rearrange("p (t c) -> p t c", t=TT)
        wg_raw = work[:, 4480:4480 + KT * GROUPS]
        we_raw = work[:, 4544:4544 + KT * EXPERTS]
        nmax = small[:, 0:4]
        sums = small[:, 4:8]
        esink = small[:, 8:10]
        den = small[:, 10:14]
        rden = small[:, 14:18]
        osq = small[:, 18:20]
        orstd = small[:, 20:22]
        lamdot = small[:, 22:24]
        lamexp = small[:, 24:26]
        neglam = small[:, 26:27]
        rlT = work[0:GROUPS + EXPERTS, 0:S]
        rt = work[:, 1024:1024 + 16 * 64].rearrange("p (n t e) -> p n t e", n=16, t=TT)
        pT = work[:, 256:768].rearrange("p (k t) -> p k t", k=TT)
        p_tok = work[:, 2560:3072].rearrange("p (t c) -> p t c", t=TT)
        gl = rt[:, 0, :, 0:GROUPS]
        el, cand, one1, one2, masked = (rt[:, i, :, :] for i in (1, 2, 3, 4, 5))
        gcand = rt[:, 6, :, 0:GROUPS]
        gone = rt[:, 6, :, 8:8 + GROUPS]
        gexp = rt[:, 6, :, 16:16 + GROUPS]
        gmax = rt[:, 7, :, 0:1]
        gmin = rt[:, 7, :, 1:2]
        gsum = rt[:, 7, :, 2:3]
        m1 = rt[:, 7, :, 3:4]
        m2 = rt[:, 7, :, 4:5]
        cmin = rt[:, 7, :, 5:6]
        ed = rt[:, 7, :, 6:7]
        den2 = rt[:, 7, :, 7:8]
        w_a = rt[:, 7, :, 8:9]
        w_b = rt[:, 7, :, 9:10]
        gw = rt[:, 7, :, 10:11]
        iota_g = cst[:, C_IG:C_IE].rearrange("p (t g) -> p t g", t=TT)
        iota_e = cst[:, C_IE:C_TH].rearrange("p (t g) -> p t g", t=TT)
        o4 = work[:, 0:2048]
        sel = work[:, 2048:2304].rearrange("p (t c) -> p t c", t=TT)
        selg = work[:, 2304:2560].rearrange("p (t c) -> p t c", t=TT)
        selgT = work[:, 2560:2816]
        esig, sig1, sig, hmul, hid, hidT = (work[:, 2816 + P * i:2944 + P * i] for i in range(6))
        ple = [ple0[:, :], work[:, 3584:5632]]
        g_fin = work[:, 0:2048]

        x_loaded = [sem(f"x_loaded{i}") for i in range(TT)]
        cst_loaded = sem("cst_loaded")
        table_masked = sem("table_masked")
        table_loaded = sem("table_loaded")
        small_loaded = sem("small_loaded")
        SMALL_LOADS = 8
        router_loaded = sem("router_loaded")
        slot_loaded = [sem(f"slot_loaded{i}") for i in range(RING)]
        ring_used = sem("ring_used")
        whi_ready = sem("whi_ready")
        wlo_ready = sem("wlo_ready")
        half_used = sem("half_used")
        g_mix_loaded = sem("g_mix_loaded")
        norm_ready = sem("norm_ready")
        norm_taken = [sem(f"norm_taken{i}") for i in range(2)]
        v_filled = sem("v_filled")
        v_ready = sem("v_ready")
        scaled = sem("scaled")
        rows_filled = sem("rows_filled")
        rows_copied = sem("rows_copied")
        rows_stored = sem("rows_stored")
        bias_loaded = [sem(f"bias_loaded{i}") for i in range(2)]
        bias_flipped = sem("bias_flipped")
        bias_ready = sem("bias_ready")
        chunk_squares = [sem(f"chunk_squares{i}") for i in range(4)]
        sumsq_ready = [sem(f"sumsq_ready{i}") for i in range(4)]
        mean_done = sem("mean_done")
        rstd_done = sem("rstd_done")
        diag_ready = sem("diag_ready")
        uhi_ready = sem("uhi_ready")
        dense_ready = [sem(f"dense_ready{i}") for i in range(2)]
        dense_taken = [sem(f"dense_taken{i}") for i in range(2)]
        lam_dots = sem("lam_dots")
        lam_exps = sem("lam_exps")
        logits_ready = sem("logits_ready")
        nmax_ready = sem("nmax_ready")
        exp_ready = sem("exp_ready")
        probs_ready = sem("probs_ready")
        probsT_filled = sem("probsT_filled")
        probsT_ready = sem("probsT_ready")
        pv_ready = sem("pv_ready")
        osq_ready = sem("osq_ready")
        omean_ready = sem("omean_ready")
        orstd_ready = sem("orstd_ready")
        head_out_ready = sem("head_out_ready")
        outT_ready = sem("outT_ready")
        yhi_ready = sem("yhi_ready")
        y_ready = sem("y_ready")
        hp_ready = sem("hp_ready")
        h_ready = sem("h_ready")
        router_ready = sem("router_ready")
        rlogits_filled = sem("rlogits_filled")
        rlogits_copied = sem("rlogits_copied")
        rlogits_ready = sem("rlogits_ready")
        chosen = sem("chosen")
        small_exps = sem("small_exps")
        hT_used = sem("hT_used")
        ranks_filled = sem("ranks_filled")
        rounds_known = sem("rounds_known")
        p_loaded = sem("p_loaded")
        ple_loaded = sem("ple_loaded")
        pT_filled = sem("pT_filled")
        pT_ready = sem("pT_ready")
        dve_step = sem("dve_step")
        dve_loop = sem("dve_loop")
        sel_ready = sem("sel_ready")
        gather_filled = sem("gather_filled")
        gather_taken = sem("gather_taken")
        selgT_filled = sem("selgT_filled")
        selgT_ready = sem("selgT_ready")
        esig_ready = sem("esig_ready")
        hid_ready = sem("hid_ready")
        hidT_filled = sem("hidT_filled")
        hidT_ready = sem("hidT_ready")
        o4_dve = sem("o4_dve")
        o4_act = sem("o4_act")
        scatter_filled = sem("scatter_filled")
        scatter_taken = sem("scatter_taken")
        loop_done = sem("loop_done")
        gain_loaded = sem("gain_loaded")
        out_ready = [sem(f"out_ready{t}") for t in range(TT)]
        out_stored = sem("out_stored")

        w_in = A["w_in"][0].rearrange("(t p) n -> p t n", p=P)
        w_out = A["w_out"][0].rearrange("(h p) n -> p h n", p=P)
        w1, w3 = (A[n][0].rearrange("e (p t) f -> e p (t f)", t=KT) for n in ("w1", "w3"))
        w2 = A["w2"][0].rearrange("e (j p) n -> e j p n", p=P)
        w_gate = A["w_ple_gate"][0].rearrange("(t p) n -> p t n", p=P)
        w_ple = A["w_ple_proj"][0].rearrange("(k p) n -> p k n", p=P)
        x_t = A["x"][0].rearrange("(t p) n -> t p n", p=P)
        out_t = out[0].rearrange("(t p) n -> t p n", p=P)

        def filled(eng, f):
            eng.wait_ge(dense_ready[f % 2], f // 2 + 1)

        def taken(eng, f):
            eng.wait_ge(dense_taken[f % 2], f // 2 + 1)

        def used(eng, n):
            if n < N_PROJ:
                filled(eng, D_PROJ + n)
                return
            tail = n >= N_HEAD
            c, half = HALVES[n - (N_HEAD if tail else N_PROJ)]
            if half == 0:
                eng.wait_ge(half_used, c + 1 + (N_OUT if tail else 0))
            else:
                filled(eng, (D_GATE if tail else D_OUT) + c)

        def dense_loaded(eng, n, turns):
            turn = n // HEAD_RING + 1
            eng.wait_ge(slot_loaded[n % HEAD_RING], 16 * turn if turns is None else turns + 16 * turn)

        def hi_of(n):
            return whi[n >= N_HEAD][n % HI_RING]

        def norm_bank(g):
            return bank[(2 if g < NORM_FILLS else 4) + g % 4]

        def norm_read(eng, g):
            eng.wait_ge(norm_taken[g % 2], g // 2 + 1)

        block = ctx.enter_context(nc.Block())

        @block.sync
        def _(sp):
            def fill_proj(n):
                if n >= HEAD_RING:
                    used(sp, n - HEAD_RING)
                col = PROJ[n][1]
                sp.dma_start(slots(n % HEAD_RING).rearrange("p (t c) -> p t c", t=KT),
                             w_in[:, :, col:col + HD]).then_inc(slot_loaded[n % HEAD_RING], 16)

            def fill_half(n, w, c, half):
                sp.dma_start(slots(n % HEAD_RING).rearrange("p (k c) -> p k c", k=KT // 2),
                             w[:, half * 8:half * 8 + 8, c * 256:c * 256 + 256])\
                  .then_inc(slot_loaded[n % HEAD_RING], 16)

            sp.dma_start(h[:, 0, :], x_t[0]).then_inc(x_loaded[0], 16)
            sp.dma_start(cst[:, :], A["cst"]).then_inc(cst_loaded, 16)
            sp.dma_start(choice, A["choice"]).then_inc(table_loaded, 16)
            sp.wait_ge(table_masked, 1)
            sp.dma_start(table[0:BUCKETS, :], A["rel_bias"]).then_inc(table_loaded, 16)
            sp.dma_start(h[:, 1, :], x_t[1]).then_inc(x_loaded[1], 16)
            sp.dma_start(g_mixT[:, :], A["g_mix"]).then_inc(g_mix_loaded, 16)
            for n in range(2):
                fill_proj(n)
            loads = 0
            for dst, src in (
                (g_ffnT[:, :], A["g_ffn"][0].rearrange("(p t) -> p t", t=KT)),
                (sinks[:, :], A["swa_sinks"].partition_broadcast(P)),
                (subg[:, 1:2], A["diff_subln"][0].rearrange("(p a) -> p a", a=1)),
                (lam[:, 0, :], A["lam_q1"].partition_broadcast(P)),
                (lam[:, 1, :], A["lam_k1"].partition_broadcast(P)),
                (lam[:, 2, :], A["lam_q2"].partition_broadcast(P)),
                (lam[:, 3, :], A["lam_k2"].partition_broadcast(P)),
                (g_pleT[:, :], A["g_ple"]),
            ):
                sp.dma_start(dst, src).then_inc(small_loaded, 16)
                loads += 1
            assert loads == SMALL_LOADS
            sp.wait_ge(rows_copied, 2)
            sp.dma_start(bias_rows[0:SWA_HEADS, :], rows_sb[0:SWA_HEADS, 0:REL]).then_inc(rows_stored, 16)
            sp.dma_start(bias_rows[SWA_HEADS:HEADS, :], rows_sb[0:HEADS - SWA_HEADS, REL:2 * REL])\
                .then_inc(rows_stored, 16)
            for n in range(2, N_PROJ):
                fill_proj(n)
            for i, (c, half) in enumerate(HALVES):
                used(sp, N_PROJ + i - HEAD_RING)
                fill_half(N_PROJ + i, w_out, c, half)

            def fill_expert(e, x, turns=None):
                for k in range(x * FILLS_X, (x + 1) * FILLS_X):
                    part = k % FILLS_X
                    if part < 8:
                        src = (w1, w3)[part % 2][e + x][:, (part // 2) * SLOT:(part // 2 + 1) * SLOT]
                    else:
                        src = w2[e + x, part - 8]
                    if turns is not None:
                        sp.wait_ge(ring_used, turns + (k + 1))
                    elif k >= RING:
                        sp.wait_ge(ring_used, k + 1)
                    elif k < 8:
                        used(sp, N_HEAD - HEAD_RING + k)
                    elif k == 8:
                        filled(sp, D_OUT - 1)
                    elif k == 10:
                        used(sp, N_HEAD - 1)
                        sp.dma_start(ring_w[:, :].rearrange("p (k n) -> p k n", k=2), w_ple)\
                            .then_inc(ple_loaded, 16)
                    elif k == 14:
                        filled(sp, D_GATE - 1)
                    sp.dma_start(slots(k), src).then_inc(slot_loaded[k % RING], 16)

            for x in range(QUAD):
                fill_expert(0, x)
            with sp.Fori(1, BLOCKS) as b:
                for x in range(QUAD):
                    fill_expert(b * QUAD, x, b * FILLS_IT)
            sp.wait_ge(rounds_known, 1)
            rounds = sp.value_load(rounds_i[0:1, 0:1], min_val=1, max_val=MAX_ROUNDS)
            with sp.If(rounds > 1):
                with sp.Fori(BLOCKS, rounds * BLOCKS, BLOCKS) as r:
                    with sp.Fori(0, BLOCKS) as b:
                        for x in range(QUAD):
                            fill_expert(b * QUAD, x, (r + b) * FILLS_IT)
            for j, (c, half) in enumerate(HALVES):
                if j < HEAD_RING:
                    sp.wait_ge(ring_used, rounds * (BLOCKS * FILLS_IT) + (j + 1))
                else:
                    used(sp, N_HEAD + j - HEAD_RING)
                fill_half(N_HEAD + j, w_gate, c, half)
            for i in range(2 * TT):
                t, c0 = i % TT, i // TT * (D // 2)
                sp.wait_ge(out_ready[t], i // TT + 1)
                sp.dma_start(out_t[t][:, c0:c0 + D // 2], h[:, t, c0:c0 + D // 2]).then_inc(out_stored, 16)
            sp.wait_ge(out_stored, 16 * 2 * TT)

        @block.gpsimd
        def _(pool):
            def norm_power(n):
                nc.gpsimd.tensor_scalar(sumsq[:, n, :], sumsq[:, n, :], 1.0 / D, EPS,
                                        ALU.mult, ALU.add).then_inc(mean_done, 1)
                pool.wait_ge(mean_done, n + 1)
                nc.gpsimd.tensor_tensor(rstd[:, n, :], sumsq[:, n, :], cst[:, C_POW:C_POW + TT],
                                        ALU.pow).then_inc(rstd_done, 1)

            pool.wait_ge(cst_loaded, 16)
            pool.wait_ge(chunk_squares[0], TT)
            norm_power(0)
            pool.wait_ge(rows_stored, 32)

            def load_bias(a):
                if a >= 2:
                    pool.wait_ge(bias_flipped, a - 1)
                src = bass.AP(tensor=bias_rows.tensor, offset=ORDER[a] * REL, ap=[[1, P], [1, 2 * P]])
                pool.dma_start(bias_raw[:, a % 2, :], src).then_inc(bias_loaded[a % 2], 16)

            load_bias(0)
            load_bias(1)
            pool.dma_start(wg_raw, A["w_group"][0].rearrange("(p t) g -> p (t g)", t=KT)).then_inc(router_loaded, 16)
            pool.dma_start(we_raw, A["w_expert"][0].rearrange("(p t) g -> p (t g)", t=KT)).then_inc(router_loaded, 16)
            pool.wait_ge(router_loaded, 32)
            nc.gpsimd.tensor_copy(router[:, :, 0:GROUPS], wg_raw.rearrange("p (t g) -> p t g", t=KT))
            nc.gpsimd.tensor_copy(router[:, :, GROUPS:], we_raw.rearrange("p (t g) -> p t g", t=KT))\
                .then_inc(router_ready, 1)
            n_diff = 0
            for a in range(HEADS):
                if a + 2 < HEADS:
                    load_bias(a + 2)
                if STEPS[a][0] == "diff":
                    n_diff += 1
                    pool.wait_ge(osq_ready, n_diff)
                    nc.gpsimd.tensor_scalar(osq, osq, 1.0 / HD, EPS, ALU.mult, ALU.add).then_inc(omean_ready, 1)
                    pool.wait_ge(omean_ready, n_diff)
                    nc.gpsimd.tensor_tensor(orstd, osq, cst[:, C_POW:C_POW + TT], ALU.pow)\
                        .then_inc(orstd_ready, 1)
            pool.wait_ge(y_ready, HEADS)
            pool.dma_start(p_tok, A["p"][0, 0].rearrange("(t p) c -> p t c", p=P)).then_inc(p_loaded, 16)
            pool.wait_ge(sumsq_ready[1], 1)
            norm_power(1)
            pool.wait_ge(loop_done, 1)
            pool.dma_start(g_fin, A["g_final"].partition_broadcast(P)).then_inc(gain_loaded, 16)
            pool.wait_ge(chunk_squares[2], TT)
            norm_power(2)
            pool.wait_ge(sumsq_ready[3], 1)
            norm_power(3)

        @block.scalar
        def _(act):
            def squares(n, junk):
                for t in range(TT):
                    if n == 0:
                        act.wait_ge(x_loaded[t], 16)
                    nc.scalar.activation(junk[:, t, :], h[:, t, :], ACT.Square,
                                         accum_out=sumsq[:, n, t:t + 1]).then_inc(chunk_squares[n], 1)

            def squares_of(n, c, junk):
                if c > 0:
                    act.wait_ge(chunk_squares[n], TT * c)
                for t in range(TT):
                    nc.scalar.activation(junk[:, t, :], h[:, t, c * 256:c * 256 + 256], ACT.Square,
                                         accum_out=sq[:, n, t, c:c + 1]).then_inc(chunk_squares[n], 1)

            def split_hi(n, turns=None):
                dense_loaded(act, n, turns)
                if n >= HI_RING and not N_HEAD <= n < N_HEAD + HI_RING:
                    used(act, n - HI_RING)
                nc.scalar.copy(hi_of(n)[:, :], slots(n % HEAD_RING)).then_inc(whi_ready, 1)

            def take_hi(norm, gT, fills=range(NORM_FILLS)):
                for i in fills:
                    g = norm * NORM_FILLS + i
                    act.wait_ge(norm_ready, g + 1)
                    for k in range(2):
                        last = nc.scalar.activation(uhi[:, 2 * i + k, :], norm_bank(g)[:, k * S:(k + 1) * S],
                                                    ACT.Copy, scale=gT[:, 2 * i + k:2 * i + k + 1])
                    last.then_inc(uhi_ready, 1)

            squares(0, out_sb)
            act.wait_ge(g_mix_loaded, 16)
            split_hi(0)
            take_hi(0, g_mixT)
            split_hi(1)
            split_hi(2)
            act.wait_ge(small_loaded, 16 * SMALL_LOADS)
            act.wait_ge(lam_dots, 1)
            nc.scalar.activation(lamexp, lamdot, ACT.Exp).then_inc(lam_exps, 1)

            def take_block(n):
                f = D_PROJ + n
                b, _, buf = PROJ[n]
                filled(act, f)
                nc.scalar.copy(v_raw if b == "v" else qkv[b][buf], bank[f % 2][:, 0:S])\
                    .then_inc(dense_taken[f % 2], 1)

            def take_v(i):
                act.wait_ge(v_filled, i + 1)
                nc.scalar.copy(qkv["v"][PROJ[V_BLOCKS[i]][2]], bank[7][:, S:2 * S]).then_inc(v_ready, 1)

            def take_bias(a):
                act.wait_ge(bias_flipped, a + 1)
                nc.scalar.copy(bias_T, bank[7][:, 0:2 * P]).then_inc(bias_ready, 1)

            def exps(a):
                act.wait_ge(nmax_ready, a + 1)
                kind = STEPS[a][0]
                for m in range(2 if kind == "diff" else 1):
                    for t, (k0, k1) in enumerate(((0, P), (P, 3 * P))):
                        c = 2 * m + t
                        last = nc.scalar.activation(probs[:, m, k0:k1], probs[:, m, k0:k1], ACT.Exp,
                                                    bias=nmax[:, c:c + 1], accum_out=sums[:, c:c + 1])
                if kind == "swa":
                    last = nc.scalar.activation(esink, nmax[:, 0:TT], ACT.Exp, bias=sinks[:, ORDER[a]:ORDER[a] + 1])
                last.then_inc(exp_ready, 1)

            def take_probsT(a):
                act.wait_ge(probsT_filled, a + 1)
                nc.scalar.copy(probsT, bank[4][:, 0:3 * P]).then_inc(probsT_ready, 1)

            def take_yhi(a):
                act.wait_ge(outT_ready, a + 1)
                g = int(STEPS[a][0] == "diff")
                nc.scalar.activation(yhi[:, ORDER[a], :], bank[6][:, 0:S], ACT.Copy, scale=subg[:, g:g + 1])\
                    .then_inc(yhi_ready, 1)

            for j in range(N_HEAD + 1):
                if 0 < j <= N_PROJ:
                    take_block(j - 1)
                if j - 2 in V_BLOCKS:
                    take_v(V_BLOCKS.index(j - 2))
                for a in range(HEADS):
                    if START[a] + 1 == j:
                        take_probsT(a)
                    if OUT_AT[a] == j:
                        take_yhi(a)
                    if START[a] - 1 == j:
                        take_bias(a)
                if j + 3 < N_HEAD:
                    split_hi(j + 3)
                for a in range(HEADS):
                    if START[a] == j:
                        exps(a)
                if j > N_PROJ and HALVES[j - 1 - N_PROJ][1] == 1:
                    c = HALVES[j - 1 - N_PROJ][0]
                    taken(act, D_OUT + c)
                    squares_of(1, c, work[:, 256:768].rearrange("p (t c) -> p t c", t=TT))

            def take_hT(i):
                g = NORM_FILLS + i
                act.wait_ge(norm_ready, g + 1)
                if i >= 4:
                    act.wait_ge(hT_used, i - 3)
                for k in range(2):
                    last = nc.scalar.activation(hT[:, i % 4, k, :], norm_bank(g)[:, k * S:(k + 1) * S],
                                                ACT.Copy, scale=g_ffnT[:, 2 * i + k:2 * i + k + 1])
                last.then_inc(norm_taken[1], 1)

            for i in range(1, NORM_FILLS, 2):
                take_hT(i)
            def take_ple(c):
                f = D_PLE + c
                filled(act, f)
                for t in range(TT):
                    last = nc.scalar.copy(ple[t][:, c * 256:c * 256 + 256], bank[f % 2][:, t * 256:(t + 1) * 256])
                last.then_inc(dense_taken[f % 2], 1)

            for c in range(N_OUT):
                if c == 1:
                    act.wait_ge(chosen, 1)
                    nc.scalar.activation(gexp, gexp, ACT.Exp).then_inc(small_exps, 1)
                if c == 3:
                    act.wait_ge(chosen, 2)
                    nc.scalar.activation(ed, ed, ACT.Exp).then_inc(small_exps, 1)
                take_ple(c)

            act.wait_ge(rounds_known, 1)
            rounds = act.value_load(rounds_i[0:1, 0:1], min_val=1, max_val=MAX_ROUNDS)
            with act.Fori(0, rounds * BLOCKS) as it:
                for x in range(QUAD):
                    n = it * QUAD + (x + 1)
                    act.wait_ge(ring_used, it * FILLS_IT + (RING + x * FILLS_X + 8))
                    nc.scalar.activation(esig, bank[x % 2][:, 0:P], ACT.Exp, scale=-1.0).then_inc(esig_ready, 1)
                    act.wait_ge(hidT_filled, n)
                    nc.scalar.copy(hidT, bank[4][:, 0:P]).then_inc(hidT_ready, 1)
                    act.wait_ge(ring_used, it * FILLS_IT + (RING + (x + 1) * FILLS_X))
                    for q in (2, 3):
                        last = nc.scalar.copy(o4[SLOTS * x:SLOTS * (x + 1), q * 512:q * 512 + 512],
                                              bank[5 + x % 2][SLOTS * q:SLOTS * (q + 1), :])
                    last.then_inc(o4_act, 1)

            turns = rounds * (BLOCKS * FILLS_IT)
            for n in range(N_HEAD, N_HEAD + HI_RING):
                split_hi(n, turns)
            act.wait_ge(loop_done, 1)
            take_hi(2, g_pleT)
            squares(2, gate_junk)
            act.wait_ge(rstd_done, 3)
            for j, (c, half) in enumerate(HALVES):
                if j + HI_RING < len(HALVES):
                    split_hi(N_HEAD + j + HI_RING, turns)
                if half == 0:
                    continue
                f = D_GATE + c
                filled(act, f)
                if c >= 2:
                    act.wait_ge(h_ready, c - 1)
                for t in range(TT):
                    last = nc.scalar.activation(gate_sig[:, c % 2, t, :], bank[f % 2][:, t * 256:(t + 1) * 256],
                                                ACT.Sigmoid, scale=rstd[:, 2, t:t + 1])
                last.then_inc(dense_taken[f % 2], 1)
                act.wait_ge(h_ready, c + 1)
                squares_of(3, c, tokT[:, 0:4, :].rearrange("p (t a) c -> p t (a c)", t=TT))
            act.wait_ge(rstd_done, 4)
            act.wait_ge(scaled, N_OUT)
            for c0 in (0, D // 2):
                nc.scalar.activation(h[:, 1, c0:c0 + D // 2], h[:, 1, c0:c0 + D // 2], ACT.Copy,
                                     scale=rstd[:, 3, 1:2]).then_inc(out_ready[1], 1)

        @block.vector
        def _(dve):
            V = nc.vector
            steps = [0]

            def link(ins):
                steps[0] += 1
                ins.then_inc(dve_step, 1)
                dve.wait_ge(dve_step, steps[0])

            V.memset(table, NEG).then_inc(table_masked, 1)
            V.memset(subg[:, 0:1], 1.0)

            def split_lo(n):
                dve.wait_ge(whi_ready, n + 1)
                V.tensor_tensor(wlo[n % HEAD_RING][:, :], slots(n % HEAD_RING), hi_of(n)[:, :].bitcast(F32),
                                ALU.subtract).then_inc(wlo_ready, 1)

            def take_lo(norm, gT, fills):
                for i in fills:
                    g = norm * NORM_FILLS + i
                    dve.wait_ge(uhi_ready, (norm > 0) * NORM_FILLS + i + 1)
                    for k in range(2):
                        kt = 2 * i + k
                        last = V.scalar_tensor_tensor(ulo[:, kt, :], norm_bank(g)[:, k * S:(k + 1) * S],
                                                      gT[:, kt:kt + 1], uhi[:, kt, :].bitcast(F32),
                                                      ALU.mult, ALU.subtract)
                    last.then_inc(norm_taken[g % 2], 1)

            for i, n in enumerate((SWA_HEADS, HEADS - SWA_HEADS)):
                dve.wait_ge(rows_filled, i + 1)
                V.tensor_copy(rows_sb[0:n, i * REL:(i + 1) * REL], bank[6 + i][0:n, 0:REL])\
                    .then_inc(rows_copied, 1)
            dve.wait_ge(rstd_done, 1)
            for t in range(TT):
                V.tensor_scalar(diag[:, t, :], ident, rstd[:, 0, t:t + 1], None, ALU.mult).then_inc(diag_ready, 1)
            split_lo(0)
            take_lo(0, g_mixT, range(NORM_FILLS))
            split_lo(1)
            dve.wait_ge(small_loaded, 16 * SMALL_LOADS)
            for i in range(2):
                last = V.tensor_tensor_reduce(lam[:, 2 * i, :], lam[:, 2 * i, :], lam[:, 2 * i + 1, :], 1.0, 0.0,
                                              ALU.mult, ALU.add, lamdot[:, i:i + 1])
                if i == 0:
                    link(last)
            last.then_inc(lam_dots, 1)
            V.tensor_scalar(nsinks[:, :], sinks[:, :], -1.0, None, ALU.mult)
            link(V.tensor_scalar(subg[:, 1:2], subg[:, 1:2], 1.0 - LAMBDA_INIT, None, ALU.mult))
            dve.wait_ge(lam_exps, 1)
            link(V.tensor_tensor(neglam, lamexp[:, 1:2], lamexp[:, 0:1], ALU.subtract))
            link(V.tensor_scalar(neglam, neglam, -LAMBDA_INIT, None, ALU.add))

            def softmax_in(a):
                kind = STEPS[a][0]
                scale = (HD // 2 if kind == "diff" else HD) ** -0.5
                maps = 2 if kind == "diff" else 1
                dve.wait_ge(bias_ready, a + 1)
                dve.wait_ge(logits_ready, a + 1)
                for m in range(maps):
                    nc.vector.scalar_tensor_tensor(probs[:, m, 0:P], bank[2 + m][:, 0:P], scale,
                                                   bias_T[:, P:2 * P], ALU.mult, ALU.add)
                    last = nc.vector.scalar_tensor_tensor(probs[:, m, P:3 * P], bank[2 + m][:, P:3 * P], scale,
                                                          bias_T, ALU.mult, ALU.add)
                link(last)
                for m in range(maps):
                    nc.vector.tensor_reduce(nmax[:, 2 * m:2 * m + 1], probs[:, m, 0:P], AX.X, ALU.max, negate=True)
                    last = nc.vector.tensor_reduce(nmax[:, 2 * m + 1:2 * m + 2], probs[:, m, P:3 * P], AX.X,
                                                   ALU.max, negate=True)
                if kind == "swa":
                    link(last)
                    last = nc.vector.tensor_scalar(nmax[:, 0:TT], nmax[:, 0:TT], nsinks[:, ORDER[a]:ORDER[a] + 1], None, ALU.min)
                last.then_inc(nmax_ready, 1)

            def softmax_out(a):
                kind = STEPS[a][0]
                dve.wait_ge(exp_ready, a + 1)
                if kind == "swa":
                    link(nc.vector.tensor_tensor(den[:, 0:TT], sums[:, 0:TT], esink, ALU.add))
                    last = nc.vector.reciprocal(rden[:, 0:TT], den[:, 0:TT])
                elif kind == "moba":
                    last = nc.vector.reciprocal(rden[:, 0:TT], sums[:, 0:TT])
                else:
                    link(nc.vector.reciprocal(rden, sums))
                    link(nc.vector.tensor_scalar(rden[:, TT:2 * TT], rden[:, TT:2 * TT], neglam, None, ALU.mult))
                    for t, (k0, k1) in enumerate(((0, P), (P, 3 * P))):
                        last = nc.vector.tensor_scalar(probs[:, 0, k0:k1], probs[:, 0, k0:k1], rden[:, t:t + 1],
                                                       None, ALU.mult)
                    link(last)
                    for t, (k0, k1) in enumerate(((0, P), (P, 3 * P))):
                        last = nc.vector.scalar_tensor_tensor(
                            probs[:, 0, k0:k1], probs[:, 1, k0:k1], rden[:, TT + t:TT + t + 1],
                            probs[:, 0, k0:k1], ALU.mult, ALU.add)
                last.then_inc(probs_ready, 1)

            diffs = [0]

            def take_out(a):
                pv = bank[5][:, 0:S].rearrange("p (t d) -> p t d", t=TT)
                dve.wait_ge(pv_ready, a + 1)
                if a >= 1:
                    dve.wait_ge(outT_ready, a)
                if STEPS[a][0] == "diff":
                    diffs[0] += 1
                    link(nc.vector.tensor_copy(head_out, pv))
                    for t in range(TT):
                        last = nc.vector.tensor_tensor_reduce(probs[:, 1, t * P:t * P + P], head_out[:, t, :],
                                                              head_out[:, t, :], 1.0, 0.0, ALU.mult, ALU.add,
                                                              osq[:, t:t + 1])
                    last.then_inc(osq_ready, 1)
                    dve.wait_ge(orstd_ready, diffs[0])
                    for t in range(TT):
                        last = nc.vector.tensor_scalar(head_out[:, t, :], head_out[:, t, :], orstd[:, t:t + 1],
                                                       None, ALU.mult)
                else:
                    for t in range(TT):
                        last = nc.vector.tensor_scalar(head_out[:, t, :], pv[:, t, :], rden[:, t:t + 1],
                                                       None, ALU.mult)
                last.then_inc(head_out_ready, 1)

            def take_ylo(a):
                g = int(STEPS[a][0] == "diff")
                dve.wait_ge(yhi_ready, a + 1)
                V.scalar_tensor_tensor(ylo[:, ORDER[a], :], bank[6][:, 0:S], subg[:, g:g + 1],
                                       yhi[:, ORDER[a], :].bitcast(F32), ALU.mult, ALU.subtract).then_inc(y_ready, 1)

            def add_chunk(c):
                f = D_OUT + c
                filled(dve, f)
                hc = h[:, :, c * 256:c * 256 + 256]
                V.tensor_tensor(hc, bank[f % 2][:, :].rearrange("p (t c) -> p t c", t=TT), hc, ALU.add)\
                    .then_inc(dense_taken[f % 2], 1)
                taken(dve, f)
                for t in range(TT):
                    last = V.tensor_copy(hp[:, t, :, 16 * c:16 * c + 16],
                                         h[:, t, c * 256:c * 256 + 256].rearrange("p (q k) -> p k q", k=KT))
                last.then_inc(hp_ready, 1)

            for j in range(N_HEAD + 1):
                for a in range(HEADS):
                    if START[a] + 2 == j:
                        take_out(a)
                for a in range(HEADS):
                    if START[a] == j:
                        softmax_in(a)
                    if OUT_AT[a] == j:
                        take_ylo(a)
                if j > N_PROJ and HALVES[j - 1 - N_PROJ][1] == 1:
                    add_chunk(HALVES[j - 1 - N_PROJ][0])
                if j + 2 < N_HEAD:
                    split_lo(j + 2)
                for a in range(HEADS):
                    if START[a] == j:
                        softmax_out(a)

            def take_hT(i):
                g = NORM_FILLS + i
                dve.wait_ge(norm_ready, g + 1)
                if i >= 4:
                    dve.wait_ge(hT_used, i - 3)
                V.tensor_tensor(hT[:, i % 4, :, :], norm_bank(g)[:, :].rearrange("p (k t) -> p k t", k=2),
                                g_ffnT[:, 2 * i:2 * i + 2].unsqueeze(2).broadcast_to([P, 2, S]),
                                ALU.mult).then_inc(norm_taken[0], 1)

            take_hT(0)
            take_hT(2)
            dve.wait_ge(chunk_squares[1], TT * N_OUT)
            V.tensor_reduce(sumsq[:, 1, :], sq[:, 1, :, :], AX.X, ALU.add).then_inc(sumsq_ready[1], 1)
            take_hT(4)
            take_hT(6)


            def over(ap, n):
                return ap.broadcast_to([P, TT, n])

            def first_max(onehot, values, top, scratch, low, iota, n):
                link(V.tensor_reduce(top, values, AX.X, ALU.max))
                link(V.tensor_tensor(onehot, values, over(top, n), ALU.is_ge))
                link(V.scalar_tensor_tensor(scratch, onehot, -64.0, iota, ALU.mult, ALU.add))
                link(V.tensor_reduce(low, scratch, AX.X, ALU.min))
                link(V.tensor_tensor(onehot, scratch, over(low, n), ALU.is_equal))

            dve.wait_ge(hT_used, NORM_FILLS)
            V.tensor_copy(rlT, bank[2][0:GROUPS + EXPERTS, 0:S]).then_inc(rlogits_copied, 1)
            dve.wait_ge(pT_filled, 1)
            V.tensor_copy(pT, bank[4][:, :].rearrange("p (k t) -> p k t", k=2)).then_inc(pT_ready, 1)
            dve.wait_ge(rlogits_ready, 1)
            dve.wait_ge(rstd_done, 2)
            rl = bank[3][:, 0:TT * (GROUPS + EXPERTS)].rearrange("p (t e) -> p t e", t=TT)
            for t in range(TT):
                V.tensor_scalar(gl[:, t, :], rl[:, t, 0:GROUPS], rstd[:, 1, t:t + 1], None, ALU.mult)
                last = V.tensor_scalar(el[:, t, :], rl[:, t, GROUPS:], rstd[:, 1, t:t + 1], None, ALU.mult)
            link(last)
            first_max(gone, gl, gmax, gcand, gmin, iota_g, GROUPS)
            V.tensor_tensor(gexp, gl, over(gmax, GROUPS), ALU.subtract).then_inc(chosen, 1)
            link(V.tensor_scalar(gcand, gone, 1.0, -NEG, ALU.subtract, ALU.mult))
            for t in range(TT):
                last = V.tensor_tensor(
                    masked[:, t, :].rearrange("p (g e) -> p g e", g=GROUPS),
                    el[:, t, :].rearrange("p (g e) -> p g e", g=GROUPS),
                    gcand[:, t, :].unsqueeze(2).broadcast_to([P, GROUPS, PER_GROUP]), ALU.add)
            link(last)
            first_max(one1, masked, m1, cand, cmin, iota_e, EXPERTS)
            link(V.scalar_tensor_tensor(masked, one1, 3 * NEG, masked, ALU.mult, ALU.add))
            first_max(one2, masked, m2, cand, cmin, iota_e, EXPERTS)
            V.tensor_tensor(ed, m2, m1, ALU.subtract).then_inc(chosen, 1)
            V.tensor_tensor(cand, one1, one2, ALU.add).then_inc(chosen, 1)
            dve.wait_ge(small_exps, 2)
            link(V.tensor_reduce(gsum, gexp, AX.X, ALU.add))
            link(V.reciprocal(gw, gsum))
            link(V.tensor_scalar(den2, ed, 1.0, None, ALU.add))
            link(V.reciprocal(w_a, den2))
            link(V.tensor_tensor(w_a, w_a, gw, ALU.mult))
            link(V.tensor_tensor(w_b, w_a, ed, ALU.mult))
            V.tensor_tensor(one1, one1, over(w_a, EXPERTS), ALU.mult)
            link(V.tensor_tensor(one2, one2, over(w_b, EXPERTS), ALU.mult))
            link(V.tensor_tensor(gate_of[:, :, :], one1, one2, ALU.add))
            dve.wait_ge(ranks_filled, 1)
            rank = bank[3][:, 0:TT * EXPERTS].rearrange("p (t e) -> p t e", t=TT)
            total = bank[3][:, TT * EXPERTS:(TT + 1) * EXPERTS]
            link(V.scalar_tensor_tensor(slot_of[:, :, :], rank, 1.0, cand, ALU.add, ALU.mult))
            link(V.tensor_scalar(slot_of[:, :, :], slot_of[:, :, :], -1.0, None, ALU.add))
            fullest = rt[:, 8, 0, 0:1]
            over_th = rt[:, 8, 1, 0:MAX_ROUNDS]
            nround = rt[:, 8, 0, 1:2]
            link(V.tensor_reduce(fullest, total, AX.X, ALU.max))
            link(V.tensor_tensor(over_th, fullest.broadcast_to([P, MAX_ROUNDS]), cst[:, C_TH:C_POW], ALU.is_gt))
            link(V.tensor_reduce(nround, over_th, AX.X, ALU.add))
            V.tensor_copy(rounds_i[:, :], nround).then_inc(rounds_known, 1)
            dve.wait_ge(rounds_known, 1)
            rounds = dve.value_load(rounds_i[0:1, 0:1], min_val=1, max_val=MAX_ROUNDS)
            LINKS = 1 + 3 * QUAD
            with dve.Fori(0, rounds * BLOCKS, BLOCKS) as r:
                with dve.Fori(0, BLOCKS) as b:
                    it = r + b
                    done = [0]

                    def link_in(ins):
                        done[0] += 1
                        ins.then_inc(dve_loop, 1)
                        dve.wait_ge(dve_loop, it * LINKS + done[0])

                    cols = bass.ds(b * QUAD, QUAD)
                    slot_no = cst[:, C_SLOT:C_SLOT + P].rearrange("p (e s) -> p e s", e=QUAD)
                    for t in range(TT):
                        last = nc.vector.tensor_tensor(
                            sel[:, t, :].rearrange("p (e s) -> p e s", e=QUAD),
                            slot_of[:, t, cols].unsqueeze(2).broadcast_to([P, QUAD, SLOTS]), slot_no, ALU.is_equal)
                    link_in(last)
                    for t in range(TT):
                        last = nc.vector.tensor_tensor(
                            selg[:, t, :].rearrange("p (e s) -> p e s", e=QUAD),
                            sel[:, t, :].rearrange("p (e s) -> p e s", e=QUAD),
                            gate_of[:, t, cols].unsqueeze(2).broadcast_to([P, QUAD, SLOTS]), ALU.mult)
                    for t in range(TT):
                        last = nc.vector.tensor_scalar(sel[:, t, :], sel[:, t, :], rstd[:, 1, t:t + 1], None, ALU.mult)
                    last.then_inc(sel_ready, 1)
                    nc.vector.tensor_scalar(slot_of[:, :, cols], slot_of[:, :, cols], -float(SLOTS), None, ALU.add)
                    for i in range(4):
                        dve.wait_ge(gather_filled, it * 4 + (i + 1))
                        nc.vector.tensor_tensor(
                            tokT[:, 4 * i:4 * i + 4, :], bank[2 + i % 2][:, :].rearrange("p (k c) -> p k c", k=4),
                            g_ffnT[:, 4 * i:4 * i + 4].unsqueeze(2).broadcast_to([P, 4, P]),
                            ALU.mult).then_inc(gather_taken, 1)
                    dve.wait_ge(selgT_filled, it + 1)
                    nc.vector.tensor_copy(selgT, bank[4][:, 0:S]).then_inc(selgT_ready, 1)
                    for x in range(QUAD):
                        n = it * QUAD + (x + 1)
                        dve.wait_ge(esig_ready, n)
                        link_in(nc.vector.tensor_scalar(sig1, esig, 1.0, None, ALU.add))
                        link_in(nc.vector.reciprocal(sig, sig1))
                        link_in(nc.vector.tensor_tensor(hmul, bank[x % 2][:, 0:P], sig, ALU.mult))
                        nc.vector.tensor_tensor(hid, bank[x % 2][:, P:2 * P], hmul, ALU.mult).then_inc(hid_ready, 1)
                        dve.wait_ge(ring_used, it * FILLS_IT + (RING + (x + 1) * FILLS_X))
                        for q in (0, 1):
                            last = nc.vector.tensor_copy(o4[SLOTS * x:SLOTS * (x + 1), q * 512:q * 512 + 512],
                                                         bank[5 + x % 2][SLOTS * q:SLOTS * (q + 1), :])
                        last.then_inc(o4_dve, 1)
                    for i in range(2 * TT * 2):
                        q, t = i // TT, i % TT
                        dve.wait_ge(scatter_filled, it * 8 + (i + 1))
                        hc = h[:, t, q * 512:q * 512 + 512]
                        nc.vector.tensor_tensor(hc, bank[2 + i % 2][:, :], hc, ALU.add).then_inc(scatter_taken, 1)
            V.memset(small[:, 60:61], 0.0).then_inc(loop_done, 1)

            split_lo(N_HEAD)
            take_lo(2, g_pleT, range(NORM_FILLS // 2))
            split_lo(N_HEAD + 1)
            take_lo(2, g_pleT, range(NORM_FILLS // 2, NORM_FILLS))
            split_lo(N_HEAD + 2)

            def scale_chunk(c):
                if c == 0:
                    dve.wait_ge(gain_loaded, 16)
                dve.wait_ge(chunk_squares[3], TT * (c + 1))
                for t in range(TT):
                    hc = h[:, t, c * 256:c * 256 + 256]
                    last = V.tensor_tensor(hc, hc, g_fin[:, c * 256:c * 256 + 256], ALU.mult)
                last.then_inc(scaled, 1)

            for j, (c, half) in enumerate(HALVES):
                if j + 3 < len(HALVES):
                    split_lo(N_HEAD + j + 3)
                if half == 0:
                    continue
                f = D_GATE + c
                sg = gate_sig[:, c % 2, :, :]
                taken(dve, f)
                for t in range(TT):
                    last = V.tensor_tensor(sg[:, t, :], sg[:, t, :], ple[t][:, c * 256:c * 256 + 256], ALU.mult)
                link(last)
                hc = h[:, :, c * 256:c * 256 + 256]
                V.tensor_tensor(hc, sg, hc, ALU.add).then_inc(h_ready, 1)
                if c >= 1:
                    scale_chunk(c - 1)
            dve.wait_ge(chunk_squares[3], TT * N_OUT)
            V.tensor_reduce(sumsq[:, 3, :], sq[:, 3, :, :], AX.X, ALU.add).then_inc(sumsq_ready[3], 1)
            scale_chunk(N_OUT - 1)
            dve.wait_ge(rstd_done, 4)
            dve.wait_ge(scaled, N_OUT)
            for c0 in (0, D // 2):
                V.tensor_scalar(h[:, 0, c0:c0 + D // 2], h[:, 0, c0:c0 + D // 2], rstd[:, 3, 0:1], None,
                                ALU.mult).then_inc(out_ready[0], 1)

        @block.tensor
        def _(pe):
            mm = nc.tensor.matmul

            pe.wait_ge(table_loaded, 32)
            mm(bank[6][0:SWA_HEADS, 0:REL], table[:, 0:SWA_HEADS], choice[:, REL:2 * REL],
               start=True, stop=True).then_inc(rows_filled, 1)
            mm(bank[7][0:HEADS - SWA_HEADS, 0:REL], table[:, SWA_HEADS:HEADS], choice[:, 0:REL],
               start=True, stop=True).then_inc(rows_filled, 1)

            def bank_free(f):
                if f >= 2:
                    taken(pe, f - 2)

            def norm_free(norm, i):
                if i >= 4:
                    norm_read(pe, norm * NORM_FILLS + i - 4)

            pe.wait_ge(diag_ready, TT)
            for i in range(NORM_FILLS):
                norm_free(0, i)
                for k in range(2):
                    for t in range(TT):
                        c0 = (2 * i + k) * P
                        last = mm(norm_bank(i)[:, (2 * k + t) * P:(2 * k + t + 1) * P], h[:, t, c0:c0 + P],
                                  diag[:, t, :], start=True, stop=True)
                last.then_inc(norm_ready, 1)
            for b in range(2):
                norm_read(pe, NORM_FILLS - 1 - b)

            def project(n):
                f = D_PROJ + n
                hi, lo = (w[:, :].rearrange("p (k c) -> p k c", k=KT) for w in (hi_of(n), wlo[n % HEAD_RING]))
                bank_free(f)
                pe.wait_ge(wlo_ready, n + 1)
                o = bank[f % 2][:, 0:S]
                for k in range(KT):
                    mm(o, hi[:, k, :], uhi[:, k, :], start=k == 0, stop=False)
                    mm(o, hi[:, k, :], ulo[:, k, :], start=False, stop=False)
                    last = mm(o, lo[:, k, :], uhi[:, k, :], start=False, stop=k == KT - 1)
                last.then_inc(dense_ready[f % 2], 1)

            flips, turned = [0], [0]

            def bank7_read():
                if flips[0]:
                    pe.wait_ge(bias_ready, flips[0])
                if turned[0]:
                    pe.wait_ge(v_ready, turned[0])

            def flip_bias(a):
                bank7_read()
                flips[0] += 1
                pe.wait_ge(bias_loaded[a % 2], 16 * (a // 2 + 1))
                mm(bank[7][:, 0:2 * P], flip, bias_raw[:, a % 2, :], start=True, stop=True).then_inc(bias_flipped, 1)

            def transpose_v(n):
                bank7_read()
                turned[0] += 1
                taken(pe, D_PROJ + n)
                for t in range(TT):
                    last = nc.tensor.transpose(bank[7][:, S + t * P:S + (t + 1) * P],
                                               v_raw[:, t * P:(t + 1) * P], ident)
                last.then_inc(v_filled, 1)

            def logits(a):
                kind, kv, _ = STEPS[a]
                for b in range(2):
                    taken(pe, D_PROJ + NEED_K[a] - 1 - b)
                q, k = qkv["q"][a % 2], qkv["k"][kv]
                width = HD // 2 if kind == "diff" else HD
                for m in range(HD // width):
                    r0, r1 = m * width, (m + 1) * width
                    mm(bank[2 + m][:, 0:P], q[r0:r1, 0:P], k[r0:r1, 0:P], start=True, stop=True)
                    last = mm(bank[2 + m][:, P:3 * P], q[r0:r1, P:2 * P], k[r0:r1, :], start=True, stop=True)
                last.then_inc(logits_ready, 1)

            def transpose_probs(a):
                pe.wait_ge(probs_ready, a + 1)
                for i in range(3):
                    last = nc.tensor.transpose(bank[4][:, i * P:(i + 1) * P], probs[:, 0, i * P:(i + 1) * P], ident)
                last.then_inc(probsT_filled, 1)

            def times_v(a):
                kv = STEPS[a][1]
                v = qkv["v"][kv]
                pe.wait_ge(v_ready, sum(n < START[a] for n in V_BLOCKS))
                pe.wait_ge(probsT_ready, a + 1)
                mm(bank[5][:, 0:P], probsT[:, 0:P], v[:, 0:P], start=True, stop=True)
                mm(bank[5][:, P:2 * P], probsT[:, P:2 * P], v[:, 0:P], start=True, stop=False)
                mm(bank[5][:, P:2 * P], probsT[:, 2 * P:3 * P], v[:, P:2 * P], start=False, stop=True)\
                    .then_inc(pv_ready, 1)

            def transpose_out(a):
                pe.wait_ge(head_out_ready, a + 1)
                if a >= 1:
                    pe.wait_ge(y_ready, a)
                for t in range(TT):
                    last = nc.tensor.transpose(bank[6][:, t * P:(t + 1) * P], head_out[:, t, :], ident)
                last.then_inc(outT_ready, 1)

            def half_chunk(n, j, first_fill, xhi, xlo):
                c, half = HALVES[j]
                f = first_fill + c
                hi, lo = (w[:, :].rearrange("p (k c) -> p k c", k=KT // 2) for w in (hi_of(n), wlo[n % HEAD_RING]))
                if half == 0:
                    bank_free(f)
                pe.wait_ge(wlo_ready, n + 1)
                for t in range(TT):
                    o, ts = bank[f % 2][:, t * 256:(t + 1) * 256], slice(t * P, (t + 1) * P)
                    for k in range(KT // 2):
                        kk, first, end = half * 8 + k, half == t == k == 0, half == 1 and k == KT // 2 - 1
                        mm(o, xhi[:, kk, ts], hi[:, k, :], start=first, stop=False, skip_group_check=True)
                        mm(o, xhi[:, kk, ts], lo[:, k, :], start=False, stop=False, skip_group_check=True)
                        last = mm(o, xlo[:, kk, ts], hi[:, k, :], start=False, stop=end, skip_group_check=True)
                last.then_inc((half_used, dense_ready[f % 2])[half], 1)

            for j in range(N_HEAD + 1):
                for a in range(HEADS):
                    if START[a] + 2 == j:
                        times_v(a)
                for a in range(HEADS):
                    if START[a] == j:
                        logits(a)
                if j - 2 in V_BLOCKS:
                    transpose_v(j - 2)
                for a in range(HEADS):
                    if START[a] + 1 == j:
                        transpose_probs(a)
                    if OUT_AT[a] == j:
                        transpose_out(a)
                    if START[a] - 1 == j:
                        flip_bias(a)
                if j < N_PROJ:
                    project(j)
                elif j < N_HEAD:
                    if j - N_PROJ in (0, 2):
                        pe.wait_ge(y_ready, HALF_READY[j - N_PROJ == 2])
                    half_chunk(j, j - N_PROJ, D_OUT, yhi, ylo)

            pe.wait_ge(hp_ready, N_OUT)
            pe.wait_ge(router_ready, 1)

            def transpose_h(i):
                norm_free(1, i)
                for k in range(2):
                    for t in range(TT):
                        last = nc.tensor.transpose(norm_bank(NORM_FILLS + i)[:, (2 * k + t) * P:(2 * k + t + 1) * P],
                                                   hp[:, t, 2 * i + k, :], ident)
                last.then_inc(norm_ready, 1)

            n_r = GROUPS + EXPERTS

            def route(i):
                norm_read(pe, NORM_FILLS + i)
                for k in range(2):
                    last = mm(bank[2][0:n_r, 0:S], router[:, 2 * i + k, :], hT[:, i % 4, k, :],
                              start=i == k == 0, stop=i == NORM_FILLS - 1 and k == 1)
                last.then_inc(hT_used, 1)

            for i in range(NORM_FILLS):
                transpose_h(i)
                if i >= 1:
                    route(i - 1)
            route(NORM_FILLS - 1)
            pe.wait_ge(p_loaded, 16)
            for k in range(2):
                for t in range(TT):
                    last = nc.tensor.transpose(bank[4][:, (2 * k + t) * P:(2 * k + t + 1) * P],
                                               p_tok[:, t, k * P:(k + 1) * P], ident)
            last.then_inc(pT_filled, 1)
            pe.wait_ge(rlogits_copied, 1)
            for t in range(TT):
                last = nc.tensor.transpose(bank[3][:, t * n_r:(t + 1) * n_r], rlT[:, t * P:(t + 1) * P],
                                           ident[0:n_r, 0:n_r])
            last.then_inc(rlogits_ready, 1)

            pe.wait_ge(pT_ready, 1)
            pe.wait_ge(ple_loaded, 16)

            def ple_chunk(c):
                f = D_PLE + c
                bank_free(f)
                w = ring_w[:, :].rearrange("p (k n) -> p k n", k=2)
                for t in range(TT):
                    for k in range(2):
                        last = mm(bank[f % 2][:, t * 256:(t + 1) * 256], pT[:, k, t * P:(t + 1) * P],
                                  w[:, k, c * 256:(c + 1) * 256], start=k == 0, stop=k == 1)
                last.then_inc(dense_ready[f % 2], 1)

            for c in range(4):
                ple_chunk(c)
            pe.wait_ge(chosen, 3)
            picked = rt[:, 2, :, :]
            rank = bank[3]
            mm(rank[:, 0:EXPERTS], before, picked[:, 0, :], start=True, stop=True).then_inc(ring_used, RING)
            mm(rank[:, EXPERTS:2 * EXPERTS], ones, picked[:, 0, :], start=True, stop=False)
            mm(rank[:, EXPERTS:2 * EXPERTS], before, picked[:, 1, :], start=False, stop=True)
            mm(rank[:, 2 * EXPERTS:3 * EXPERTS], ones, picked[:, 0, :], start=True, stop=False)
            mm(rank[:, 2 * EXPERTS:3 * EXPERTS], ones, picked[:, 1, :], start=False, stop=True)\
                .then_inc(ranks_filled, 1)
            for c in range(4, N_OUT):
                ple_chunk(c)

            def slot_here(fill, turns):
                pos = fill % RING
                landed = 16 * (fill // RING + 1) + (16 * HEAD_TURNS if pos < HEAD_RING else 0)
                pe.wait_ge(slot_loaded[pos], turns + landed)

            for b in range(2):
                taken(pe, D_GATE - 1 - b)
            pe.wait_ge(rounds_known, 1)
            rounds = pe.value_load(rounds_i[0:1, 0:1], min_val=1, max_val=MAX_ROUNDS)
            with pe.Fori(0, rounds * BLOCKS) as it:
                pe.wait_ge(sel_ready, it + 1)
                for i in range(4):
                    if i >= 2:
                        pe.wait_ge(gather_taken, it * 4 + (i - 1))
                    for k in range(4):
                        for t in range(TT):
                            last = mm(bank[2 + i % 2][:, k * P:(k + 1) * P], hp[:, t, 4 * i + k, :], sel[:, t, :],
                                      start=t == 0, stop=t == TT - 1)
                    last.then_inc(gather_filled, 1)
                for t in range(TT):
                    last = nc.tensor.transpose(bank[4][:, t * P:(t + 1) * P], selg[:, t, :], ident)
                last.then_inc(selgT_filled, 1)
                pe.wait_ge(selgT_ready, it + 1)
                pe.wait_ge(gather_taken, it * 4 + 4)
                turns = it * FILLS_IT
                for x in range(QUAD):
                    n = it * QUAD + (x + 1)
                    for quarter in range(4):
                        fill = x * FILLS_X + 2 * quarter
                        slot_here(fill, turns)
                        slot_here(fill + 1, turns)
                        w = slots(fill, 2).rearrange("p (m k f) -> p k m f", m=2, k=4)
                        for k in range(4):
                            for j in range(QUAD):
                                last = mm(bank[x % 2][SLOTS * j:SLOTS * (j + 1), 0:2 * P]
                                          .rearrange("p (m f) -> p m f", m=2),
                                          tokT[:, 4 * quarter + k, SLOTS * x:SLOTS * (x + 1)],
                                          w[:, k, :, j * P:(j + 1) * P],
                                          start=quarter == 0 and k == 0, stop=quarter == 3 and k == 3)
                        last.then_inc(ring_used, 2)
                    pe.wait_ge(hid_ready, n)
                    nc.tensor.transpose(bank[4][:, 0:P], hid, ident).then_inc(hidT_filled, 1)
                    pe.wait_ge(hidT_ready, n)
                    for j in range(JT):
                        fill = x * FILLS_X + 8 + j
                        slot_here(fill, turns)
                        w = slots(fill)
                        for q in range(QUAD):
                            last = mm(bank[5 + x % 2][SLOTS * q:SLOTS * (q + 1), :], hidT[:, SLOTS * j:SLOTS * (j + 1)],
                                      w[:, q * 512:(q + 1) * 512], start=j == 0, stop=j == JT - 1)
                        last.then_inc(ring_used, 1)
                pe.wait_ge(o4_dve, it * QUAD + QUAD)
                pe.wait_ge(o4_act, it * QUAD + QUAD)
                for i in range(8):
                    q, t = i // TT, i % TT
                    if i >= 2:
                        pe.wait_ge(scatter_taken, it * 8 + (i - 1))
                    mm(bank[2 + i % 2][:, :], selgT[:, t * P:(t + 1) * P], o4[:, q * 512:(q + 1) * 512],
                       start=True, stop=True).then_inc(scatter_filled, 1)
            pe.wait_ge(loop_done, 1)
            for i in range(NORM_FILLS):
                norm_free(2, i)
                g = 2 * NORM_FILLS + i
                for k in range(2):
                    for t in range(TT):
                        c0 = (2 * i + k) * P
                        last = nc.tensor.transpose(norm_bank(g)[:, (2 * k + t) * P:(2 * k + t + 1) * P],
                                                   h[:, t, c0:c0 + P], ident)
                last.then_inc(norm_ready, 1)
            for j, (c, half) in enumerate(HALVES):
                for b in range(2):
                    norm_read(pe, 2 * NORM_FILLS + (half + 1) * NORM_FILLS // 2 - 1 - b)
                half_chunk(N_HEAD + j, j, D_GATE, uhi, ulo)


_INPUTS = ["x", "p", "rel_bias", "g_final", "g_mix", "w_in", "swa_sinks", "lam_q1", "lam_k1", "lam_q2", "lam_k2",
           "diff_subln", "w_out", "g_ffn", "w_group", "w_expert", "w1", "w3", "w2", "g_ple", "w_ple_gate",
           "w_ple_proj"]


def kernel(**inputs):
    import concourse.bacc as bacc
    from concourse.bass_utils import run_bass_kernel_spmd

    nc = bacc.Bacc("TRN2", target_bir_lowering=False, num_devices=1)
    arrays = {f"in_{n}": np.ascontiguousarray(inputs[n]) for n in _INPUTS}
    for g in ("in_g_mix", "in_g_ple"):
        arrays[g] = np.ascontiguousarray(arrays[g].reshape(KT, P).T)
    arrays["in_cst"] = constants()
    arrays["in_choice"] = bucket_choice()
    A = {n[3:]: nc.dram_tensor(n, a.shape, mybir.dt.from_np(a.dtype), kind="ExternalInput").ap()
         for n, a in arrays.items()}
    out = nc.dram_tensor("out_h", (1, S, D), F32, kind="ExternalOutput").ap()
    layer(nc, A, out)
    r = run_bass_kernel_spmd(nc, [arrays], core_ids=[0])
    return r.results[0]["out_h"]
```

```python
import math
from contextlib import ExitStack

import numpy as np
import concourse.bass as bass
from concourse import mybir

F32 = mybir.dt.float32
F32R = mybir.dt.float32r
I32 = mybir.dt.int32
ALU = mybir.AluOpType
ACT = mybir.ActivationFunctionType
AX = mybir.AxisListType

P = 128
D = 2048
S = 256
TT = S // P
KT = D // P
HD = 128
SWA_HEADS, SWA_KV, MOBA_HEADS, DIFF_HEADS = 6, 2, 4, 6
HEADS = SWA_HEADS + MOBA_HEADS + DIFF_HEADS
WINDOW = 128
BUCKETS, EXACT, MAX_DIST = 32, 16, 128
GROUPS, PER_GROUP = 4, 8
EXPERTS = GROUPS * PER_GROUP
DE = 512
JT = DE // P
PLE = 256
EPS = 1e-6
NEG = -1e30
LAMBDA_INIT = 0.8 - 0.6 * math.exp(-0.3 * 0)

SLOT = 2048
RING = 16
HEAD_RING = 8
SLOTS = 32
QUAD = P // SLOTS
BLOCKS = EXPERTS // QUAD
MAX_ROUNDS = S // SLOTS
REL = 3 * P

C_ID, C_BEFORE, C_ONES, C_SLOT = (i * P for i in range(4))
C_IG = 4 * P
C_IE = C_IG + TT * GROUPS
C_TH = C_IE + TT * EXPERTS
C_POW = C_TH + MAX_ROUNDS
C_END = C_POW + 4


def constants():
    c = np.zeros((P, C_END), np.float32)
    i = np.arange(P)
    c[i, C_ID + i] = 1.0
    c[:, C_BEFORE:C_BEFORE + P] = i[:, None] < i[None, :]
    c[:, C_ONES:C_ONES + P] = 1.0
    c[:, C_SLOT:C_SLOT + P] = i[None, :] % SLOTS
    c[:, C_IG:C_IE] = np.arange(TT * GROUPS) % GROUPS
    c[:, C_IE:C_TH] = np.arange(TT * EXPERTS) % EXPERTS
    c[:, C_TH:C_POW] = np.arange(MAX_ROUNDS) * SLOTS
    c[:, C_POW:C_END] = -0.5
    return c


def bucket_choice():
    dist = 2 * P - 1 - np.arange(REL)
    n = np.maximum(dist, 0)
    nf = np.maximum(n, 1).astype(np.float32)
    large = EXACT + (np.log(nf / np.float32(EXACT)) / np.float32(math.log(MAX_DIST / EXACT))
                     * (BUCKETS - EXACT)).astype(np.int32)
    bucket = np.where(n < EXACT, n, np.minimum(large, BUCKETS - 1))
    c = np.zeros((BUCKETS + 1, 2, REL), np.float32)
    for swa in range(2):
        seen = (dist >= 0) & ((dist < WINDOW) | (swa == 0))
        c[np.where(seen, bucket, BUCKETS), swa, np.arange(REL)] = 1.0
    return c.reshape(BUCKETS + 1, 2 * REL)


ORDER = [0, 10, 1, 11, 2, 12, 3, 13, 4, 14, 5, 15, 6, 7, 8, 9]
assert sorted(ORDER) == list(range(HEADS))


def head_plan():
    kv_cols = SWA_HEADS * HD
    moba = kv_cols + 2 * SWA_KV * HD
    diff = moba + 3 * MOBA_HEADS * HD
    plan, own = [], 0
    for a in ORDER:
        if a < SWA_HEADS:
            g = a // (SWA_HEADS // SWA_KV)
            blocks = [("q", a * HD)]
            if a % (SWA_HEADS // SWA_KV) == 0:
                blocks += [("k", kv_cols + g * HD), ("v", kv_cols + (SWA_KV + g) * HD)]
            plan.append(("swa", 2, blocks))
            continue
        kind, base, n, h = (("moba", moba, MOBA_HEADS, a - SWA_HEADS) if a < SWA_HEADS + MOBA_HEADS else
                            ("diff", diff, DIFF_HEADS, a - SWA_HEADS - MOBA_HEADS))
        plan.append((kind, own % 2, [(b, base + (i * n + h) * HD) for i, b in enumerate("qkv")]))
        own += 1
    return plan


STEPS = head_plan()
PROJ = []
NEED_K = []
START = []
for _i, (_kind, _kv, _blocks) in enumerate(STEPS):
    for _b, _col in _blocks:
        PROJ.append((_b, _col, _i % 2 if _b == "q" else _kv))
    NEED_K.append(len(PROJ) - (_blocks[-1][0] == "v"))
    START.append(len(PROJ) if _i == 0 else max(START[-1] + 2, len(PROJ)))
OUT_AT = [n + 3 for n in START[:-1]] + [START[-1] + 2]
NMAX = [sum(1 + (step[0] == "diff") for step in STEPS[:a]) for a in range(HEADS)]
V_BLOCKS = [n for n, _block in enumerate(PROJ) if _block[0] == "v"]

N_PROJ = len(PROJ)
N_OUT = D // 256
HALVES = [(0, 0), (1, 0), (0, 1), (1, 1)] + [(c, half) for c in range(2, N_OUT) for half in range(2)]
N_HEAD = N_PROJ + len(HALVES)
HEAD_TURNS = N_HEAD // HEAD_RING
OUT_PIECES = 4
HI_RING = 4
FILLS_X = 12
FILLS_IT = QUAD * FILLS_X
assert N_HEAD % HEAD_RING == 0 and FILLS_IT % RING == 0 and START[-1] == N_PROJ
P_AT = N_PROJ + 8
HALF_READY = max(ORDER.index(a) for a in range(HEADS // 2)) + 1
assert ORDER[-1] >= HEADS // 2 and HALVES[2] == (0, 1)

D_PROJ = 0
D_OUT = D_PROJ + N_PROJ
D_PLE = D_OUT + N_OUT
D_GATE = D_PLE + N_OUT
NORM_FILLS = KT // 2


def layer(nc, A, out):
    with ExitStack() as ctx:
        def sem(name):
            return ctx.enter_context(nc.semaphore(name))

        bank = [ctx.enter_context(nc.psum_tensor(f"bank{i}", [P, 512], F32)) for i in range(8)]
        bias_rows = nc.dram_tensor("bias_rows", [HEADS, P, REL], F32, kind="Internal").ap()

        KB = 1024
        base = (nc.sbuf_base + 31) // 32 * 32
        RING_AT = base
        U_AT = RING_AT + HEAD_RING * SLOT * 4
        Y_AT = U_AT + 32 * KB
        W_AT = Y_AT + 32 * KB
        H_AT = W_AT + 32 * KB
        at = [H_AT + 16 * KB]

        def place(name, shape, offset, dt=F32):
            return nc.alloc_sbuf_tensor_at(name, shape, dt, offset=offset)

        def sb(name, shape, dt=F32):
            o = at[0]
            at[0] += (int(np.prod(shape[1:])) * 4 + 31) // 32 * 32
            return place(name, shape, o, dt)

        ring_a = place("ring_a", [P, HEAD_RING * SLOT], RING_AT)
        uhi = place("uhi", [P, KT, S], U_AT, F32R)
        ulo = place("ulo", [P, KT, S], U_AT + 16 * KB, F32R)
        hp = place("hp", [P, TT, KT, P], U_AT)
        ring_u = place("ring_u", [P, 2 * SLOT], U_AT + 16 * KB)
        x_junk = place("x_junk", [P, TT, D], U_AT)
        ple_weights = ring_u[:, :].rearrange("p (g k n) -> p g k n", g=2, k=2)
        yhi = place("yhi", [P, HEADS, S], Y_AT, F32R)
        ylo = place("ylo", [P, HEADS, S], Y_AT + 16 * KB, F32R)
        ring_y = place("ring_y", [P, 4 * SLOT], Y_AT)
        ring_w = place("ring_w", [P, 2 * SLOT], W_AT)
        tokT = place("tokT", [P, KT, P], W_AT + 16 * KB)
        hT = place("hT", [P, 4, 2, S], W_AT + 16 * KB)
        ple0 = place("ple0", [P, D], W_AT + 24 * KB)
        gate_junk = place("gate_junk", [P, TT, D], W_AT)
        gate_sig = place("gate_sig", [P, 2, TT, 256], W_AT)
        whi = [[place(f"whi{p}{i}", [P, SLOT], o + 8 * KB * i, F32R) for i in range(HI_RING)]
               for p, o in enumerate((W_AT, Y_AT))]
        wlo = [place(f"wlo{i}", [P, SLOT], RING_AT + 8 * KB * i, F32R) for i in range(HEAD_RING)]
        h = place("h", [P, TT, D], H_AT)

        cst = sb("cst", [P, C_END])
        g_mixT, g_ffnT, g_pleT = (sb(f"gT{i}", [P, KT]) for i in range(3))
        router = sb("router", [P, KT, GROUPS + EXPERTS])
        slot_of = sb("slot_of", [P, TT, EXPERTS])
        gate_of = sb("gate_of", [P, TT, EXPERTS])
        rounds_i = sb("rounds_i", [P, 1], I32)
        sq = sb("sq", [P, 4, TT, N_OUT])
        sumsq = sb("sumsq", [P, 4, TT])
        rstd = sb("rstd", [P, 4, TT])
        lam = sb("lam", [P, 4, HD // 2])
        small = sb("small", [P, 64])
        sinks = sb("sinks", [P, SWA_HEADS])
        nsinks = sb("nsinks", [P, SWA_HEADS])
        subg = sb("subg", [P, 2])
        work = sb("work", [P, 5632])
        assert at[0] <= nc.sbuf_usable_end, at[0]

        ident = cst[:, C_ID:C_ID + P]
        before = cst[:, C_BEFORE:C_BEFORE + P]
        ones = cst[:, C_ONES:C_ONES + P]

        def slots(pos, n=1):
            pos %= RING
            for tile, first, count in ((ring_a, 0, 8), (ring_u, 8, 2), (ring_y, 10, 4), (ring_w, 14, 2)):
                if first <= pos and pos + n <= first + count:
                    return tile[:, (pos - first) * SLOT:(pos - first + n) * SLOT]
            raise ValueError(pos)

        bias = work[:, 0:512].rearrange("p (b k) -> p b k", b=2)
        qkv = {b: [work[:, 768 + 512 * i:1024 + 512 * i], work[:, 1024 + 512 * i:1280 + 512 * i]]
               for i, b in enumerate("qkv")}
        v_raw = work[:, 3712:3968]
        qkv["k"].append(work[:, 3968:4224])
        qkv["v"].append(work[:, 4224:4480])
        probs = work[:, 2304:3072].rearrange("p (m k) -> p m k", m=2)
        probsT = work[:, 3072:3456]
        head_out = work[:, 3456:3712].rearrange("p (t d) -> p t d", t=TT)
        choice = work[0:BUCKETS + 1, 3712:3712 + 2 * REL]
        rows_sb = work[:, 4480:4480 + 2 * REL]
        table = work[0:BUCKETS + 1, 5248:5248 + HEADS]
        diag = work[:, 5312:5312 + 2 * P].rearrange("p (t c) -> p t c", t=TT)
        junk = work[:, 5056:5312]
        wg_raw = work[:, 4480:4480 + KT * GROUPS]
        we_raw = work[:, 4544:4544 + KT * EXPERTS]
        nmax = small[:, 0:4]
        sums = small[:, 4:8]
        esink = small[:, 8:10]
        den = small[:, 10:14]
        rden = small[:, 14:18]
        osq = small[:, 18:20]
        orstd = small[:, 20:22]
        lamdot = small[:, 22:24]
        lamexp = small[:, 24:26]
        neglam = small[:, 26:27]
        rlT = work[0:GROUPS + EXPERTS, 0:S]
        rt = work[:, 1024:1024 + 16 * 64].rearrange("p (n t e) -> p n t e", n=16, t=TT)
        pT = work[:, 3072:3584].rearrange("p (k t) -> p k t", k=TT)
        p_tok = work[:, 2560:3072].rearrange("p (t c) -> p t c", t=TT)
        gl = rt[:, 0, :, 0:GROUPS]
        el, cand, one1, one2, masked = (rt[:, i, :, :] for i in (1, 2, 3, 4, 5))
        gcand = rt[:, 6, :, 0:GROUPS]
        gone = rt[:, 6, :, 8:8 + GROUPS]
        gexp = rt[:, 6, :, 16:16 + GROUPS]
        gmax = rt[:, 7, :, 0:1]
        gmin = rt[:, 7, :, 1:2]
        gsum = rt[:, 7, :, 2:3]
        m1 = rt[:, 7, :, 3:4]
        m2 = rt[:, 7, :, 4:5]
        cmin = rt[:, 7, :, 5:6]
        ed = rt[:, 7, :, 6:7]
        den2 = rt[:, 7, :, 7:8]
        w_a = rt[:, 7, :, 8:9]
        w_b = rt[:, 7, :, 9:10]
        gw = rt[:, 7, :, 10:11]
        iota_g = cst[:, C_IG:C_IE].rearrange("p (t g) -> p t g", t=TT)
        iota_e = cst[:, C_IE:C_TH].rearrange("p (t g) -> p t g", t=TT)
        o4 = work[:, 0:2048]
        sel = work[:, 2048:2304].rearrange("p (t c) -> p t c", t=TT)
        selg = work[:, 2304:2560].rearrange("p (t c) -> p t c", t=TT)
        selgT = work[:, 2560:2816]
        esig, sig1, sig, hmul, hid, hidT = (work[:, 2816 + P * i:2944 + P * i] for i in range(6))
        ple = [ple0[:, :], work[:, 3584:5632]]
        g_fin = work[:, 0:2048]

        x_loaded = [sem(f"x_loaded{i}") for i in range(TT)]
        cst_loaded = sem("cst_loaded")
        table_masked = sem("table_masked")
        table_loaded = sem("table_loaded")
        small_loaded = sem("small_loaded")
        SMALL_LOADS = 8
        router_loaded = sem("router_loaded")
        slot_loaded = [sem(f"slot_loaded{i}") for i in range(RING)]
        ring_used = sem("ring_used")
        whi_ready = sem("whi_ready")
        wlo_ready = sem("wlo_ready")
        half_used = sem("half_used")
        g_mix_loaded = sem("g_mix_loaded")
        norm_ready = sem("norm_ready")
        norm_taken = [sem(f"norm_taken{i}") for i in range(2)]
        v_filled = sem("v_filled")
        v_ready = sem("v_ready")
        scaled = sem("scaled")
        rows_filled = sem("rows_filled")
        rows_copied = sem("rows_copied")
        rows_stored = [sem(f"rows_stored{i}") for i in range(2)]
        bias_loaded = [sem(f"bias_loaded{i}") for i in range(2)]
        chunk_squares = [sem(f"chunk_squares{i}") for i in range(4)]
        sumsq_ready = [sem(f"sumsq_ready{i}") for i in range(4)]
        mean_done = sem("mean_done")
        rstd_done = sem("rstd_done")
        diag_ready = sem("diag_ready")
        uhi_ready = sem("uhi_ready")
        dense_ready = [sem(f"dense_ready{i}") for i in range(2)]
        dense_taken = [sem(f"dense_taken{i}") for i in range(2)]
        lam_dots = sem("lam_dots")
        lam_exps = sem("lam_exps")
        logits_ready = sem("logits_ready")
        nmax_ready = sem("nmax_ready")
        exp_ready = sem("exp_ready")
        probs_ready = sem("probs_ready")
        probsT_filled = sem("probsT_filled")
        probsT_ready = sem("probsT_ready")
        pv_ready = sem("pv_ready")
        osq_ready = sem("osq_ready")
        omean_ready = sem("omean_ready")
        orstd_ready = sem("orstd_ready")
        head_out_ready = sem("head_out_ready")
        outT_ready = sem("outT_ready")
        yhi_ready = sem("yhi_ready")
        y_ready = sem("y_ready")
        hp_ready = sem("hp_ready")
        h_ready = sem("h_ready")
        router_ready = sem("router_ready")
        rlogits_copied = sem("rlogits_copied")
        rlogits_ready = sem("rlogits_ready")
        chosen = sem("chosen")
        small_exps = sem("small_exps")
        hT_used = sem("hT_used")
        ranks_filled = sem("ranks_filled")
        rounds_known = sem("rounds_known")
        p_loaded = sem("p_loaded")
        ple_loaded = sem("ple_loaded")
        pT_filled = sem("pT_filled")
        pT_ready = sem("pT_ready")
        dve_step = sem("dve_step")
        dve_loop = sem("dve_loop")
        sel_ready = sem("sel_ready")
        gather_filled = sem("gather_filled")
        gather_taken = sem("gather_taken")
        selgT_filled = sem("selgT_filled")
        selgT_ready = sem("selgT_ready")
        esig_ready = sem("esig_ready")
        hid_ready = sem("hid_ready")
        hidT_filled = sem("hidT_filled")
        hidT_ready = sem("hidT_ready")
        o4_dve = sem("o4_dve")
        o4_act = sem("o4_act")
        scatter_filled = sem("scatter_filled")
        scatter_taken = sem("scatter_taken")
        last_tile_ready = sem("last_tile_ready")
        sigmoid_ready = sem("sigmoid_ready")
        loop_done = sem("loop_done")
        gain_loaded = sem("gain_loaded")
        out_ready = [sem(f"out_ready{t}") for t in range(TT)]
        out_stored = sem("out_stored")

        w_in = A["w_in"][0].rearrange("(t p) n -> p t n", p=P)
        w_out = A["w_out"][0].rearrange("(h p) n -> p h n", p=P)
        w1, w3 = (A[n][0].rearrange("e (p t) f -> e p (t f)", t=KT) for n in ("w1", "w3"))
        w2 = A["w2"][0].rearrange("e (j p) n -> e j p n", p=P)
        w_gate = A["w_ple_gate"][0].rearrange("(t p) n -> p t n", p=P)
        w_ple = A["w_ple_proj"][0].rearrange("(k p) n -> p k n", p=P)
        x_t = A["x"][0].rearrange("(t p) n -> t p n", p=P)
        out_t = out[0].rearrange("(t p) n -> t p n", p=P)

        def filled(eng, f):
            eng.wait_ge(dense_ready[f % 2], f // 2 + 1)

        def taken(eng, f):
            eng.wait_ge(dense_taken[f % 2], f // 2 + 1)

        def used(eng, n):
            if n < N_PROJ:
                filled(eng, D_PROJ + n)
                return
            tail = n >= N_HEAD
            c, half = HALVES[n - (N_HEAD if tail else N_PROJ)]
            if half == 0:
                eng.wait_ge(half_used, c + 1 + (N_OUT if tail else 0))
            else:
                filled(eng, (D_GATE if tail else D_OUT) + c)

        def dense_loaded(eng, n, turns):
            turn = n // HEAD_RING + 1
            eng.wait_ge(slot_loaded[n % HEAD_RING], 16 * turn if turns is None else turns + 16 * turn)

        def hi_of(n):
            return whi[n >= N_HEAD][n % HI_RING]

        def norm_bank(g):
            return bank[(2 if g < NORM_FILLS else 4) + g % 4]

        def norm_read(eng, g):
            eng.wait_ge(norm_taken[g % 2], g // 2 + 1)

        block = ctx.enter_context(nc.Block())

        @block.sync
        def _(sp):
            def fill_proj(n):
                if n >= HEAD_RING:
                    used(sp, n - HEAD_RING)
                col = PROJ[n][1]
                sp.dma_start(slots(n % HEAD_RING).rearrange("p (t c) -> p t c", t=KT),
                             w_in[:, :, col:col + HD]).then_inc(slot_loaded[n % HEAD_RING], 16)

            def fill_half(n, w, c, half):
                sp.dma_start(slots(n % HEAD_RING).rearrange("p (k c) -> p k c", k=KT // 2),
                             w[:, half * 8:half * 8 + 8, c * 256:c * 256 + 256])\
                  .then_inc(slot_loaded[n % HEAD_RING], 16)

            for t in range(TT):
                sp.dma_start(h[:, t, :], x_t[t]).then_inc(x_loaded[t], 16)
            sp.dma_start(cst[:, :], A["cst"]).then_inc(cst_loaded, 16)
            sp.dma_start(choice, A["choice"]).then_inc(table_loaded, 16)
            sp.wait_ge(table_masked, 1)
            sp.dma_start(table[0:BUCKETS, :], A["rel_bias"]).then_inc(table_loaded, 16)
            sp.dma_start(g_mixT[:, :], A["g_mix"]).then_inc(g_mix_loaded, 16)
            for n in range(2):
                fill_proj(n)
            loads = 0
            for dst, src in (
                (g_ffnT[:, :], A["g_ffn"][0].rearrange("(p t) -> p t", t=KT)),
                (sinks[:, :], A["swa_sinks"].partition_broadcast(P)),
                (subg[:, 1:2], A["diff_subln"][0].rearrange("(p a) -> p a", a=1)),
                (lam[:, 0, :], A["lam_q1"].partition_broadcast(P)),
                (lam[:, 1, :], A["lam_k1"].partition_broadcast(P)),
                (lam[:, 2, :], A["lam_q2"].partition_broadcast(P)),
                (lam[:, 3, :], A["lam_k2"].partition_broadcast(P)),
                (g_pleT[:, :], A["g_ple"]),
            ):
                sp.dma_start(dst, src).then_inc(small_loaded, 16)
                loads += 1
            assert loads == SMALL_LOADS
            for n in range(2, 4):
                fill_proj(n)
            def store_rows(i, h0, h1):
                sp.wait_ge(rows_copied, i + 1)
                row = rows_sb[0:h1 - h0, i * REL:(i + 1) * REL]
                sp.dma_start(bias_rows[h0:h1, :, :], row.unsqueeze(1).broadcast_to([h1 - h0, P, REL]))\
                    .then_inc(rows_stored[i], 16)

            store_rows(0, 0, SWA_HEADS)
            for n in range(4, 6):
                fill_proj(n)
            sp.wait_ge(bias_loaded[0], 16)
            store_rows(1, SWA_HEADS, HEADS)
            for n in range(6, N_PROJ):
                fill_proj(n)
            for i, (c, half) in enumerate(HALVES):
                if i == HEAD_RING:
                    used(sp, N_PROJ - 1)
                    for g in range(2):
                        sp.dma_start(ple_weights[:, g, :, :], w_ple[:, :, g * (D // 2):(g + 1) * (D // 2)])\
                            .then_inc(ple_loaded, 16)
                used(sp, N_PROJ + i - HEAD_RING)
                fill_half(N_PROJ + i, w_out, c, half)

            def fill_expert(e, k, turns=None):
                x, part = divmod(k, FILLS_X)
                if part < 8:
                    src = (w1, w3)[part % 2][e + x][:, (part // 2) * SLOT:(part // 2 + 1) * SLOT]
                else:
                    src = w2[e + x, part - 8]
                if turns is not None:
                    sp.wait_ge(ring_used, turns + (k + 1))
                elif k >= RING:
                    sp.wait_ge(ring_used, k + 1)
                sp.dma_start(slots(k), src).then_inc(slot_loaded[k % RING], 16)

            for k in range(HEAD_RING):
                used(sp, N_HEAD - HEAD_RING + k)
                fill_expert(0, k)
            for k in range(HEAD_RING + 2, RING):
                fill_expert(0, k)
            for g in range(2):
                filled(sp, D_PLE + (g + 1) * N_OUT // 2 - 1)
                fill_expert(0, HEAD_RING + g)
            for k in range(RING, FILLS_IT):
                fill_expert(0, k)
            with sp.Fori(1, BLOCKS) as b:
                for k in range(FILLS_IT):
                    fill_expert(b * QUAD, k, b * FILLS_IT)
            sp.wait_ge(rounds_known, 1)
            rounds = sp.value_load(rounds_i[0:1, 0:1], min_val=1, max_val=MAX_ROUNDS)
            with sp.If(rounds > 1):
                with sp.Fori(BLOCKS, rounds * BLOCKS, BLOCKS) as r:
                    with sp.Fori(0, BLOCKS) as b:
                        for k in range(FILLS_IT):
                            fill_expert(b * QUAD, k, (r + b) * FILLS_IT)
            for j, (c, half) in enumerate(HALVES):
                if j < HEAD_RING:
                    sp.wait_ge(ring_used, rounds * (BLOCKS * FILLS_IT) + (j + 1))
                else:
                    used(sp, N_HEAD + j - HEAD_RING)
                fill_half(N_HEAD + j, w_gate, c, half)
            for i in range(OUT_PIECES):
                for t in range(TT):
                    c0 = i * (D // OUT_PIECES)
                    sp.wait_ge(out_ready[t], i + 1)
                    sp.dma_start(out_t[t][:, c0:c0 + D // OUT_PIECES], h[:, t, c0:c0 + D // OUT_PIECES])\
                        .then_inc(out_stored, 16)
            sp.wait_ge(out_stored, 16 * OUT_PIECES * TT)

        @block.gpsimd
        def _(pool):
            def norm_power(n):
                nc.gpsimd.tensor_scalar(sumsq[:, n, :], sumsq[:, n, :], 1.0 / D, EPS,
                                        ALU.mult, ALU.add).then_inc(mean_done, 1)
                pool.wait_ge(mean_done, n + 1)
                nc.gpsimd.tensor_tensor(rstd[:, n, :], sumsq[:, n, :], cst[:, C_POW:C_POW + TT],
                                        ALU.pow).then_inc(rstd_done, 1)

            pool.wait_ge(cst_loaded, 16)
            pool.wait_ge(chunk_squares[0], TT)
            norm_power(0)

            def load_bias(a):
                if a >= 2:
                    pool.wait_ge(nmax_ready, NMAX[a - 1])
                src = bass.AP(tensor=bias_rows.tensor, offset=ORDER[a] * P * REL + P - 1, ap=[[REL - 1, P], [1, 2 * P]])
                pool.dma_start(bias[:, a % 2, :], src).then_inc(bias_loaded[a % 2], 16)

            assert ORDER[0] < SWA_HEADS
            pool.wait_ge(rows_stored[0], 16)
            load_bias(0)
            pool.wait_ge(rows_stored[1], 16)
            load_bias(1)
            pool.dma_start(wg_raw, A["w_group"][0].rearrange("(p t) g -> p (t g)", t=KT)).then_inc(router_loaded, 16)
            pool.dma_start(we_raw, A["w_expert"][0].rearrange("(p t) g -> p (t g)", t=KT)).then_inc(router_loaded, 16)
            pool.wait_ge(router_loaded, 32)
            nc.gpsimd.tensor_copy(router[:, :, 0:GROUPS], wg_raw.rearrange("p (t g) -> p t g", t=KT))
            nc.gpsimd.tensor_copy(router[:, :, GROUPS:], we_raw.rearrange("p (t g) -> p t g", t=KT))\
                .then_inc(router_ready, 1)
            n_diff = 0
            for a in range(HEADS):
                if a + 2 < HEADS:
                    load_bias(a + 2)
                if STEPS[a][0] == "diff":
                    n_diff += 1
                    pool.wait_ge(osq_ready, n_diff)
                    nc.gpsimd.tensor_scalar(osq, osq, 1.0 / HD, EPS, ALU.mult, ALU.add).then_inc(omean_ready, 1)
                    pool.wait_ge(omean_ready, n_diff)
                    nc.gpsimd.tensor_tensor(orstd, osq, cst[:, C_POW:C_POW + TT], ALU.pow)\
                        .then_inc(orstd_ready, 1)
            pool.wait_ge(y_ready, HEADS)
            pool.dma_start(p_tok, A["p"][0, 0].rearrange("(t p) c -> p t c", p=P)).then_inc(p_loaded, 16)
            pool.wait_ge(sumsq_ready[1], 1)
            norm_power(1)
            pool.wait_ge(whi_ready, N_HEAD + 1)
            nc.gpsimd.tensor_tensor(wlo[N_HEAD % HEAD_RING][:, :], slots(N_HEAD % HEAD_RING),
                                    hi_of(N_HEAD)[:, :].bitcast(F32), ALU.subtract).then_inc(wlo_ready, 1)
            pool.wait_ge(loop_done, 1)
            pool.dma_start(g_fin, A["g_final"].partition_broadcast(P)).then_inc(gain_loaded, 16)
            pool.wait_ge(chunk_squares[2], TT)
            norm_power(2)
            pool.wait_ge(sumsq_ready[3], 1)
            norm_power(3)

        @block.scalar
        def _(act):
            def squares(n, junk):
                for t in range(TT):
                    if n == 0:
                        act.wait_ge(x_loaded[t], 16)
                    nc.scalar.activation(junk[:, t, :], h[:, t, :], ACT.Square,
                                         accum_out=sumsq[:, n, t:t + 1]).then_inc(chunk_squares[n], 1)

            def squares_of(n, c, junk):
                if c > 0:
                    act.wait_ge(chunk_squares[n], TT * c)
                for t in range(TT):
                    nc.scalar.activation(junk[:, t, :], h[:, t, c * 256:c * 256 + 256], ACT.Square,
                                         accum_out=sq[:, n, t, c:c + 1]).then_inc(chunk_squares[n], 1)

            def split_hi(n, turns=None):
                dense_loaded(act, n, turns)
                if n >= HI_RING and not N_HEAD <= n < N_HEAD + HI_RING:
                    used(act, n - HI_RING)
                nc.scalar.copy(hi_of(n)[:, :], slots(n % HEAD_RING)).then_inc(whi_ready, 1)

            def take_hi(norm, gT, fills=range(NORM_FILLS)):
                for i in fills:
                    g = norm * NORM_FILLS + i
                    act.wait_ge(norm_ready, g + 1)
                    for k in range(2):
                        last = nc.scalar.activation(uhi[:, 2 * i + k, :], norm_bank(g)[:, k * S:(k + 1) * S],
                                                    ACT.Copy, scale=gT[:, 2 * i + k:2 * i + k + 1])
                    last.then_inc(uhi_ready, 1)

            squares(0, x_junk)
            act.wait_ge(g_mix_loaded, 16)
            split_hi(0)
            take_hi(0, g_mixT)
            split_hi(1)
            split_hi(2)
            act.wait_ge(small_loaded, 16 * SMALL_LOADS)
            act.wait_ge(lam_dots, 1)
            nc.scalar.activation(lamexp, lamdot, ACT.Exp).then_inc(lam_exps, 1)

            def take_block(n):
                f = D_PROJ + n
                b, _, buf = PROJ[n]
                filled(act, f)
                nc.scalar.copy(v_raw if b == "v" else qkv[b][buf], bank[f % 2][:, 0:S])\
                    .then_inc(dense_taken[f % 2], 1)

            def take_v(i):
                act.wait_ge(v_filled, i + 1)
                nc.scalar.copy(qkv["v"][PROJ[V_BLOCKS[i]][2]], bank[7][:, 0:S]).then_inc(v_ready, 1)

            def exps(a):
                kind = STEPS[a][0]
                for m in range(2 if kind == "diff" else 1):
                    act.wait_ge(nmax_ready, NMAX[a] + m + 1)
                    for t, (k0, k1) in enumerate(((0, P), (P, 3 * P))):
                        c = 2 * m + t
                        last = nc.scalar.activation(probs[:, m, k0:k1], probs[:, m, k0:k1], ACT.Exp,
                                                    bias=nmax[:, c:c + 1], accum_out=sums[:, c:c + 1])
                if kind == "swa":
                    last = nc.scalar.activation(esink, nmax[:, 0:TT], ACT.Exp, bias=sinks[:, ORDER[a]:ORDER[a] + 1])
                last.then_inc(exp_ready, 1)

            def take_probsT(a):
                act.wait_ge(probsT_filled, a + 1)
                nc.scalar.copy(probsT, bank[4][:, 0:3 * P]).then_inc(probsT_ready, 1)

            def take_yhi(a):
                act.wait_ge(outT_ready, a + 1)
                g = int(STEPS[a][0] == "diff")
                nc.scalar.activation(yhi[:, ORDER[a], :], bank[6][:, 0:S], ACT.Copy, scale=subg[:, g:g + 1])\
                    .then_inc(yhi_ready, 1)

            for j in range(N_HEAD + 1):
                if 0 < j <= N_PROJ:
                    take_block(j - 1)
                if j - 2 in V_BLOCKS:
                    take_v(V_BLOCKS.index(j - 2))
                for a in range(HEADS):
                    if START[a] + 1 == j:
                        take_probsT(a)
                    if OUT_AT[a] == j:
                        take_yhi(a)
                for a in range(HEADS):
                    if START[a] == j:
                        exps(a)
                if j + 3 < N_HEAD:
                    split_hi(j + 3)
                if j > N_PROJ and HALVES[j - 1 - N_PROJ][1] == 1:
                    c = HALVES[j - 1 - N_PROJ][0]
                    taken(act, D_OUT + c)
                    squares_of(1, c, work[:, 256:768].rearrange("p (t c) -> p t c", t=TT))

            def take_ple(c):
                f = D_PLE + c
                filled(act, f)
                for t in range(TT):
                    last = nc.scalar.copy(ple[t][:, c * 256:c * 256 + 256], bank[f % 2][:, t * 256:(t + 1) * 256])
                last.then_inc(dense_taken[f % 2], 1)

            take_ple(0)

            def take_hT(i):
                g = NORM_FILLS + i
                act.wait_ge(norm_ready, g + 1)
                if i >= 4:
                    act.wait_ge(hT_used, i - 3)
                for k in range(2):
                    last = nc.scalar.activation(hT[:, i % 4, k, :], norm_bank(g)[:, k * S:(k + 1) * S],
                                                ACT.Copy, scale=g_ffnT[:, 2 * i + k:2 * i + k + 1])
                last.then_inc(norm_taken[1], 1)

            for i in range(1, NORM_FILLS, 2):
                take_hT(i)
            for c in range(1, N_OUT):
                if c == 2:
                    act.wait_ge(chosen, 1)
                    nc.scalar.activation(gexp, gexp, ACT.Exp).then_inc(small_exps, 1)
                if c == 4:
                    act.wait_ge(chosen, 2)
                    nc.scalar.activation(ed, ed, ACT.Exp).then_inc(small_exps, 1)
                take_ple(c)

            act.wait_ge(rounds_known, 1)
            rounds = act.value_load(rounds_i[0:1, 0:1], min_val=1, max_val=MAX_ROUNDS)
            with act.Fori(0, rounds * BLOCKS) as it:
                for x in range(QUAD):
                    n = it * QUAD + (x + 1)
                    act.wait_ge(ring_used, it * FILLS_IT + (RING + x * FILLS_X + 8))
                    nc.scalar.activation(esig, bank[x % 2][:, 0:P], ACT.Exp, scale=-1.0).then_inc(esig_ready, 1)
                    act.wait_ge(hidT_filled, n)
                    nc.scalar.copy(hidT, bank[4][:, 0:P]).then_inc(hidT_ready, 1)
                    act.wait_ge(ring_used, it * FILLS_IT + (RING + (x + 1) * FILLS_X))
                    for q in (2, 3):
                        nc.scalar.copy(o4[SLOTS * x:SLOTS * (x + 1), q * 512:q * 512 + 512],
                                       bank[5 + x % 2][SLOTS * q:SLOTS * (q + 1), :]).then_inc(o4_act, 1)

            turns = rounds * (BLOCKS * FILLS_IT)
            for n in range(N_HEAD, N_HEAD + 3):
                split_hi(n, turns)
            act.wait_ge(loop_done, 1)
            take_hi(2, g_pleT)
            split_hi(N_HEAD + 3, turns)
            squares(2, gate_junk)
            act.wait_ge(rstd_done, 3)
            squares_junk = tokT[:, 0:4, :].rearrange("p (t a) c -> p t (a c)", t=TT)
            for j, (c, half) in enumerate(HALVES):
                if j + HI_RING < len(HALVES):
                    split_hi(N_HEAD + j + HI_RING, turns)
                if half == 0 or c == N_OUT - 1:
                    continue
                f = D_GATE + c
                filled(act, f)
                if c >= 2:
                    act.wait_ge(h_ready, c - 1)
                for t in range(TT):
                    last = nc.scalar.activation(gate_sig[:, c % 2, t, :], bank[f % 2][:, t * 256:(t + 1) * 256],
                                                ACT.Sigmoid, scale=rstd[:, 2, t:t + 1])
                last.then_inc(dense_taken[f % 2], 1)
                act.wait_ge(h_ready, c + 1)
                squares_of(3, c, squares_junk)
            c = N_OUT - 1
            act.wait_ge(h_ready, c - 1)
            for t in range(TT):
                if t == 0:
                    filled(act, D_GATE + c)
                    src = bank[(D_GATE + c) % 2][:, 0:256]
                else:
                    act.wait_ge(last_tile_ready, 1)
                    src = bank[2][:, 0:256]
                nc.scalar.activation(gate_sig[:, c % 2, t, :], src, ACT.Sigmoid, scale=rstd[:, 2, t:t + 1])\
                    .then_inc(sigmoid_ready, 1)
            act.wait_ge(chunk_squares[3], TT * c)
            for t in range(TT):
                act.wait_ge(h_ready, c + t + 1)
                nc.scalar.activation(squares_junk[:, t, :], h[:, t, c * 256:c * 256 + 256], ACT.Square,
                                     accum_out=sq[:, 3, t, c:c + 1]).then_inc(chunk_squares[3], 1)
            act.wait_ge(rstd_done, 4)
            act.wait_ge(scaled, N_OUT)
            for c0 in range(0, D, D // OUT_PIECES):
                nc.scalar.activation(h[:, 1, c0:c0 + D // OUT_PIECES], h[:, 1, c0:c0 + D // OUT_PIECES], ACT.Copy,
                                     scale=rstd[:, 3, 1:2]).then_inc(out_ready[1], 1)

        @block.vector
        def _(dve):
            V = nc.vector
            steps = [0]

            def link(ins):
                steps[0] += 1
                ins.then_inc(dve_step, 1)
                dve.wait_ge(dve_step, steps[0])

            V.memset(table, NEG).then_inc(table_masked, 1)
            V.memset(subg[:, 0:1], 1.0)

            def split_lo(n):
                dve.wait_ge(whi_ready, n + 1)
                V.tensor_tensor(wlo[n % HEAD_RING][:, :], slots(n % HEAD_RING), hi_of(n)[:, :].bitcast(F32),
                                ALU.subtract).then_inc(wlo_ready, 1)

            def take_lo(norm, gT, fills):
                for i in fills:
                    g = norm * NORM_FILLS + i
                    dve.wait_ge(uhi_ready, (norm > 0) * NORM_FILLS + i + 1)
                    for k in range(2):
                        kt = 2 * i + k
                        last = V.scalar_tensor_tensor(ulo[:, kt, :], norm_bank(g)[:, k * S:(k + 1) * S],
                                                      gT[:, kt:kt + 1], uhi[:, kt, :].bitcast(F32),
                                                      ALU.mult, ALU.subtract)
                    last.then_inc(norm_taken[g % 2], 1)

            dve.wait_ge(rstd_done, 1)
            for t in range(TT):
                V.tensor_scalar(diag[:, t, :], ident, rstd[:, 0, t:t + 1], None, ALU.mult).then_inc(diag_ready, 1)
            take_lo(0, g_mixT, range(NORM_FILLS // 2))
            for i, n in enumerate((SWA_HEADS, HEADS - SWA_HEADS)):
                dve.wait_ge(rows_filled, i + 1)
                V.tensor_copy(rows_sb[0:n, i * REL:(i + 1) * REL], bank[6 + i][0:n, 0:REL])\
                    .then_inc(rows_copied, 1)
            split_lo(0)
            take_lo(0, g_mixT, range(NORM_FILLS // 2, NORM_FILLS))
            split_lo(1)
            dve.wait_ge(small_loaded, 16 * SMALL_LOADS)
            for i in range(2):
                last = V.tensor_tensor_reduce(lam[:, 2 * i, :], lam[:, 2 * i, :], lam[:, 2 * i + 1, :], 1.0, 0.0,
                                              ALU.mult, ALU.add, lamdot[:, i:i + 1])
                if i == 0:
                    link(last)
            last.then_inc(lam_dots, 1)
            V.tensor_scalar(nsinks[:, :], sinks[:, :], -1.0, None, ALU.mult)
            link(V.tensor_scalar(subg[:, 1:2], subg[:, 1:2], 1.0 - LAMBDA_INIT, None, ALU.mult))
            dve.wait_ge(lam_exps, 1)
            link(V.tensor_tensor(neglam, lamexp[:, 1:2], lamexp[:, 0:1], ALU.subtract))
            link(V.tensor_scalar(neglam, neglam, -LAMBDA_INIT, None, ALU.add))

            def softmax_in(a):
                kind = STEPS[a][0]
                scale = (HD // 2 if kind == "diff" else HD) ** -0.5
                maps = 2 if kind == "diff" else 1
                dve.wait_ge(bias_loaded[a % 2], 16 * (a // 2 + 1))
                dve.wait_ge(logits_ready, a + 1)
                for m in range(maps):
                    nc.vector.scalar_tensor_tensor(probs[:, m, 0:P], bank[2 + m][:, 0:P], scale,
                                                   bias[:, a % 2, P:2 * P], ALU.mult, ALU.add)
                    link(nc.vector.scalar_tensor_tensor(probs[:, m, P:3 * P], bank[2 + m][:, P:3 * P], scale,
                                                        bias[:, a % 2, :], ALU.mult, ALU.add))
                    nc.vector.tensor_reduce(nmax[:, 2 * m:2 * m + 1], probs[:, m, 0:P], AX.X, ALU.max, negate=True)
                    last = nc.vector.tensor_reduce(nmax[:, 2 * m + 1:2 * m + 2], probs[:, m, P:3 * P], AX.X,
                                                   ALU.max, negate=True)
                    if kind == "swa":
                        link(last)
                        last = nc.vector.tensor_scalar(nmax[:, 0:TT], nmax[:, 0:TT],
                                                       nsinks[:, ORDER[a]:ORDER[a] + 1], None, ALU.min)
                    last.then_inc(nmax_ready, 1)

            def softmax_out(a):
                kind = STEPS[a][0]
                if a >= 1:
                    dve.wait_ge(head_out_ready, a)
                dve.wait_ge(exp_ready, a + 1)
                if kind == "swa":
                    link(nc.vector.tensor_tensor(den[:, 0:TT], sums[:, 0:TT], esink, ALU.add))
                    last = nc.vector.reciprocal(rden[:, 0:TT], den[:, 0:TT])
                elif kind == "moba":
                    last = nc.vector.reciprocal(rden[:, 0:TT], sums[:, 0:TT])
                else:
                    link(nc.vector.reciprocal(rden, sums))
                    link(nc.vector.tensor_scalar(rden[:, TT:2 * TT], rden[:, TT:2 * TT], neglam, None, ALU.mult))
                    for t, (k0, k1) in enumerate(((0, P), (P, 3 * P))):
                        last = nc.vector.tensor_scalar(probs[:, 0, k0:k1], probs[:, 0, k0:k1], rden[:, t:t + 1],
                                                       None, ALU.mult)
                    link(last)
                    for t, (k0, k1) in enumerate(((0, P), (P, 3 * P))):
                        last = nc.vector.scalar_tensor_tensor(
                            probs[:, 0, k0:k1], probs[:, 1, k0:k1], rden[:, TT + t:TT + t + 1],
                            probs[:, 0, k0:k1], ALU.mult, ALU.add)
                last.then_inc(probs_ready, 1)

            diffs = [0]

            def take_out(a):
                pv = bank[5][:, 0:S].rearrange("p (t d) -> p t d", t=TT)
                dve.wait_ge(pv_ready, a + 1)
                if a >= 1:
                    dve.wait_ge(outT_ready, a)
                if STEPS[a][0] == "diff":
                    diffs[0] += 1
                    link(nc.vector.tensor_copy(head_out, pv))
                    for t in range(TT):
                        last = nc.vector.tensor_tensor_reduce(junk[:, t * P:t * P + P], head_out[:, t, :],
                                                              head_out[:, t, :], 1.0, 0.0, ALU.mult, ALU.add,
                                                              osq[:, t:t + 1])
                    last.then_inc(osq_ready, 1)
                    dve.wait_ge(orstd_ready, diffs[0])
                    for t in range(TT):
                        last = nc.vector.tensor_scalar(head_out[:, t, :], head_out[:, t, :], orstd[:, t:t + 1],
                                                       None, ALU.mult)
                else:
                    for t in range(TT):
                        last = nc.vector.tensor_scalar(head_out[:, t, :], pv[:, t, :], rden[:, t:t + 1],
                                                       None, ALU.mult)
                last.then_inc(head_out_ready, 1)

            def take_ylo(a):
                g = int(STEPS[a][0] == "diff")
                dve.wait_ge(yhi_ready, a + 1)
                V.scalar_tensor_tensor(ylo[:, ORDER[a], :], bank[6][:, 0:S], subg[:, g:g + 1],
                                       yhi[:, ORDER[a], :].bitcast(F32), ALU.mult, ALU.subtract).then_inc(y_ready, 1)

            def add_chunk(c):
                f = D_OUT + c
                filled(dve, f)
                hc = h[:, :, c * 256:c * 256 + 256]
                V.tensor_tensor(hc, bank[f % 2][:, :].rearrange("p (t c) -> p t c", t=TT), hc, ALU.add)\
                    .then_inc(dense_taken[f % 2], 1)
                taken(dve, f)
                for t in range(TT):
                    last = V.tensor_copy(hp[:, t, :, 16 * c:16 * c + 16],
                                         h[:, t, c * 256:c * 256 + 256].rearrange("p (q k) -> p k q", k=KT))
                last.then_inc(hp_ready, 1)

            for j in range(N_HEAD + 1):
                for a in range(HEADS):
                    if START[a] == j:
                        softmax_in(a)
                for a in range(HEADS):
                    if START[a] + 2 == j:
                        take_out(a)
                    if OUT_AT[a] == j:
                        take_ylo(a)
                for a in range(HEADS):
                    if START[a] == j:
                        softmax_out(a)
                if j > N_PROJ and HALVES[j - 1 - N_PROJ][1] == 1:
                    add_chunk(HALVES[j - 1 - N_PROJ][0])
                if j == P_AT:
                    dve.wait_ge(pT_filled, 1)
                    V.tensor_copy(pT, bank[4][:, :].rearrange("p (k t) -> p k t", k=2)).then_inc(pT_ready, 1)
                if j + 2 < N_HEAD:
                    split_lo(j + 2)

            def take_hT(i):
                g = NORM_FILLS + i
                dve.wait_ge(norm_ready, g + 1)
                if i >= 4:
                    dve.wait_ge(hT_used, i - 3)
                V.tensor_tensor(hT[:, i % 4, :, :], norm_bank(g)[:, :].rearrange("p (k t) -> p k t", k=2),
                                g_ffnT[:, 2 * i:2 * i + 2].unsqueeze(2).broadcast_to([P, 2, S]),
                                ALU.mult).then_inc(norm_taken[0], 1)

            take_hT(0)
            take_hT(2)
            dve.wait_ge(chunk_squares[1], TT * N_OUT)
            V.tensor_reduce(sumsq[:, 1, :], sq[:, 1, :, :], AX.X, ALU.add).then_inc(sumsq_ready[1], 1)
            take_hT(4)
            take_hT(6)


            def over(ap, n):
                return ap.broadcast_to([P, TT, n])

            def first_max(onehot, values, top, scratch, low, iota, n):
                link(V.tensor_reduce(top, values, AX.X, ALU.max))
                link(V.tensor_tensor(onehot, values, over(top, n), ALU.is_ge))
                link(V.scalar_tensor_tensor(scratch, onehot, -64.0, iota, ALU.mult, ALU.add))
                link(V.tensor_reduce(low, scratch, AX.X, ALU.min))
                link(V.tensor_tensor(onehot, scratch, over(low, n), ALU.is_equal))

            dve.wait_ge(hT_used, NORM_FILLS)
            V.tensor_copy(rlT, bank[2][0:GROUPS + EXPERTS, 0:S]).then_inc(rlogits_copied, 1)
            dve.wait_ge(rlogits_ready, 1)
            dve.wait_ge(rstd_done, 2)
            rl = bank[3][:, 0:TT * (GROUPS + EXPERTS)].rearrange("p (t e) -> p t e", t=TT)
            for t in range(TT):
                V.tensor_scalar(gl[:, t, :], rl[:, t, 0:GROUPS], rstd[:, 1, t:t + 1], None, ALU.mult)
                last = V.tensor_scalar(el[:, t, :], rl[:, t, GROUPS:], rstd[:, 1, t:t + 1], None, ALU.mult)
            link(last)
            first_max(gone, gl, gmax, gcand, gmin, iota_g, GROUPS)
            V.tensor_tensor(gexp, gl, over(gmax, GROUPS), ALU.subtract).then_inc(chosen, 1)
            link(V.tensor_scalar(gcand, gone, 1.0, -NEG, ALU.subtract, ALU.mult))
            for t in range(TT):
                last = V.tensor_tensor(
                    masked[:, t, :].rearrange("p (g e) -> p g e", g=GROUPS),
                    el[:, t, :].rearrange("p (g e) -> p g e", g=GROUPS),
                    gcand[:, t, :].unsqueeze(2).broadcast_to([P, GROUPS, PER_GROUP]), ALU.add)
            link(last)
            first_max(one1, masked, m1, cand, cmin, iota_e, EXPERTS)
            link(V.scalar_tensor_tensor(masked, one1, 3 * NEG, masked, ALU.mult, ALU.add))
            first_max(one2, masked, m2, cand, cmin, iota_e, EXPERTS)
            V.tensor_tensor(ed, m2, m1, ALU.subtract).then_inc(chosen, 1)
            V.tensor_tensor(cand, one1, one2, ALU.add).then_inc(chosen, 1)
            dve.wait_ge(ranks_filled, 1)
            rank = bank[3][:, 0:TT * EXPERTS].rearrange("p (t e) -> p t e", t=TT)
            total = bank[3][:, TT * EXPERTS:(TT + 1) * EXPERTS]
            link(V.scalar_tensor_tensor(slot_of[:, :, :], rank, 1.0, cand, ALU.add, ALU.mult))
            link(V.tensor_scalar(slot_of[:, :, :], slot_of[:, :, :], -1.0, None, ALU.add))
            fullest = rt[:, 8, 0, 0:1]
            over_th = rt[:, 8, 1, 0:MAX_ROUNDS]
            nround = rt[:, 8, 0, 1:2]
            link(V.tensor_reduce(fullest, total, AX.X, ALU.max))
            link(V.tensor_tensor(over_th, fullest.broadcast_to([P, MAX_ROUNDS]), cst[:, C_TH:C_POW], ALU.is_gt))
            link(V.tensor_reduce(nround, over_th, AX.X, ALU.add))
            V.tensor_copy(rounds_i[:, :], nround).then_inc(rounds_known, 1)
            dve.wait_ge(small_exps, 2)
            link(V.tensor_reduce(gsum, gexp, AX.X, ALU.add))
            link(V.reciprocal(gw, gsum))
            link(V.tensor_scalar(den2, ed, 1.0, None, ALU.add))
            link(V.reciprocal(w_a, den2))
            link(V.tensor_tensor(w_a, w_a, gw, ALU.mult))
            link(V.tensor_tensor(w_b, w_a, ed, ALU.mult))
            V.tensor_tensor(one1, one1, over(w_a, EXPERTS), ALU.mult)
            link(V.tensor_tensor(one2, one2, over(w_b, EXPERTS), ALU.mult))
            link(V.tensor_tensor(gate_of[:, :, :], one1, one2, ALU.add))
            dve.wait_ge(rounds_known, 1)
            rounds = dve.value_load(rounds_i[0:1, 0:1], min_val=1, max_val=MAX_ROUNDS)
            LINKS = 1 + 3 * QUAD
            with dve.Fori(0, rounds * BLOCKS, BLOCKS) as r:
                with dve.Fori(0, BLOCKS) as b:
                    it = r + b
                    done = [0]

                    def link_in(ins):
                        done[0] += 1
                        ins.then_inc(dve_loop, 1)
                        dve.wait_ge(dve_loop, it * LINKS + done[0])

                    cols = bass.ds(b * QUAD, QUAD)
                    slot_no = cst[:, C_SLOT:C_SLOT + P].rearrange("p (e s) -> p e s", e=QUAD)
                    for t in range(TT):
                        last = nc.vector.tensor_tensor(
                            sel[:, t, :].rearrange("p (e s) -> p e s", e=QUAD),
                            slot_of[:, t, cols].unsqueeze(2).broadcast_to([P, QUAD, SLOTS]), slot_no, ALU.is_equal)
                    link_in(last)
                    for t in range(TT):
                        last = nc.vector.tensor_tensor(
                            selg[:, t, :].rearrange("p (e s) -> p e s", e=QUAD),
                            sel[:, t, :].rearrange("p (e s) -> p e s", e=QUAD),
                            gate_of[:, t, cols].unsqueeze(2).broadcast_to([P, QUAD, SLOTS]), ALU.mult)
                    for t in range(TT):
                        last = nc.vector.tensor_scalar(sel[:, t, :], sel[:, t, :], rstd[:, 1, t:t + 1], None, ALU.mult)
                    last.then_inc(sel_ready, 1)
                    nc.vector.tensor_scalar(slot_of[:, :, cols], slot_of[:, :, cols], -float(SLOTS), None, ALU.add)
                    for i in range(4):
                        dve.wait_ge(gather_filled, it * 4 + (i + 1))
                        nc.vector.tensor_tensor(
                            tokT[:, 4 * i:4 * i + 4, :], bank[2 + i % 2][:, :].rearrange("p (k c) -> p k c", k=4),
                            g_ffnT[:, 4 * i:4 * i + 4].unsqueeze(2).broadcast_to([P, 4, P]),
                            ALU.mult).then_inc(gather_taken, 1)
                    dve.wait_ge(selgT_filled, it + 1)
                    nc.vector.tensor_copy(selgT, bank[4][:, 0:S]).then_inc(selgT_ready, 1)
                    for x in range(QUAD):
                        n = it * QUAD + (x + 1)
                        dve.wait_ge(esig_ready, n)
                        link_in(nc.vector.tensor_scalar(sig1, esig, 1.0, None, ALU.add))
                        link_in(nc.vector.reciprocal(sig, sig1))
                        link_in(nc.vector.tensor_tensor(hmul, bank[x % 2][:, 0:P], sig, ALU.mult))
                        nc.vector.tensor_tensor(hid, bank[x % 2][:, P:2 * P], hmul, ALU.mult).then_inc(hid_ready, 1)
                        dve.wait_ge(ring_used, it * FILLS_IT + (RING + (x + 1) * FILLS_X))
                        for q in (0, 1):
                            nc.vector.tensor_copy(o4[SLOTS * x:SLOTS * (x + 1), q * 512:q * 512 + 512],
                                                  bank[5 + x % 2][SLOTS * q:SLOTS * (q + 1), :]).then_inc(o4_dve, 1)
                    for i in range(2 * TT * 2):
                        q, t = i // TT, i % TT
                        dve.wait_ge(scatter_filled, it * 8 + (i + 1))
                        hc = h[:, t, q * 512:q * 512 + 512]
                        nc.vector.tensor_tensor(hc, bank[2 + i % 2][:, :], hc, ALU.add).then_inc(scatter_taken, 1)
            V.memset(small[:, 60:61], 0.0).then_inc(loop_done, 1)

            take_lo(2, g_pleT, range(NORM_FILLS // 2))
            dve.wait_ge(wlo_ready, N_HEAD + 1)
            split_lo(N_HEAD + 1)
            take_lo(2, g_pleT, range(NORM_FILLS // 2, NORM_FILLS))
            split_lo(N_HEAD + 2)

            def scale_chunk(c):
                if c == 0:
                    dve.wait_ge(gain_loaded, 16)
                dve.wait_ge(chunk_squares[3], TT * (c + 1))
                for t in range(TT):
                    hc = h[:, t, c * 256:c * 256 + 256]
                    last = V.tensor_tensor(hc, hc, g_fin[:, c * 256:c * 256 + 256], ALU.mult)
                last.then_inc(scaled, 1)

            for j, (c, half) in enumerate(HALVES):
                if j + 3 < len(HALVES):
                    split_lo(N_HEAD + j + 3)
                if half == 0 or c == N_OUT - 1:
                    continue
                f = D_GATE + c
                sg = gate_sig[:, c % 2, :, :]
                taken(dve, f)
                for t in range(TT):
                    last = V.tensor_tensor(sg[:, t, :], sg[:, t, :], ple[t][:, c * 256:c * 256 + 256], ALU.mult)
                link(last)
                hc = h[:, :, c * 256:c * 256 + 256]
                V.tensor_tensor(hc, sg, hc, ALU.add).then_inc(h_ready, 1)
                if c >= 1:
                    scale_chunk(c - 1)
            scale_chunk(N_OUT - 2)
            c = N_OUT - 1
            for t in range(TT):
                dve.wait_ge(sigmoid_ready, t + 1)
                sg, hc = gate_sig[:, c % 2, t, :], h[:, t, c * 256:c * 256 + 256]
                link(V.tensor_tensor(sg, sg, ple[t][:, c * 256:c * 256 + 256], ALU.mult))
                V.tensor_tensor(hc, sg, hc, ALU.add).then_inc(h_ready, 1)
            dve.wait_ge(chunk_squares[3], TT * N_OUT)
            V.tensor_reduce(sumsq[:, 3, :], sq[:, 3, :, :], AX.X, ALU.add).then_inc(sumsq_ready[3], 1)
            scale_chunk(N_OUT - 1)
            dve.wait_ge(rstd_done, 4)
            dve.wait_ge(scaled, N_OUT)
            for c0 in range(0, D, D // OUT_PIECES):
                V.tensor_scalar(h[:, 0, c0:c0 + D // OUT_PIECES], h[:, 0, c0:c0 + D // OUT_PIECES], rstd[:, 3, 0:1], None,
                                ALU.mult).then_inc(out_ready[0], 1)

        @block.tensor
        def _(pe):
            mm = nc.tensor.matmul

            def bank_free(f):
                if f >= 2:
                    taken(pe, f - 2)

            def norm_free(norm, i):
                if i >= 4:
                    norm_read(pe, norm * NORM_FILLS + i - 4)

            pe.wait_ge(diag_ready, TT)
            for i in range(NORM_FILLS):
                if i == 4:
                    pe.wait_ge(table_loaded, 32)
                    mm(bank[6][0:SWA_HEADS, 0:REL], table[:, 0:SWA_HEADS], choice[:, REL:2 * REL],
                       start=True, stop=True).then_inc(rows_filled, 1)
                    mm(bank[7][0:HEADS - SWA_HEADS, 0:REL], table[:, SWA_HEADS:HEADS], choice[:, 0:REL],
                       start=True, stop=True).then_inc(rows_filled, 1)
                norm_free(0, i)
                for k in range(2):
                    for t in range(TT):
                        c0 = (2 * i + k) * P
                        last = mm(norm_bank(i)[:, (2 * k + t) * P:(2 * k + t + 1) * P], h[:, t, c0:c0 + P],
                                  diag[:, t, :], start=True, stop=True)
                last.then_inc(norm_ready, 1)

            def project(n):
                f = D_PROJ + n
                hi, lo = (w[:, :].rearrange("p (k c) -> p k c", k=KT) for w in (hi_of(n), wlo[n % HEAD_RING]))
                bank_free(f)
                pe.wait_ge(wlo_ready, n + 1)
                o = bank[f % 2][:, 0:S]
                for k in range(KT):
                    if n == 0 and k % 2 == 0:
                        norm_read(pe, k // 2)
                    mm(o, hi[:, k, :], uhi[:, k, :], start=k == 0, stop=False)
                    mm(o, hi[:, k, :], ulo[:, k, :], start=False, stop=False)
                    last = mm(o, lo[:, k, :], uhi[:, k, :], start=False, stop=k == KT - 1)
                last.then_inc(dense_ready[f % 2], 1)

            def transpose_v(n):
                i = V_BLOCKS.index(n)
                if i > 0:
                    pe.wait_ge(v_ready, i)
                taken(pe, D_PROJ + n)
                for t in range(TT):
                    last = nc.tensor.transpose(bank[7][:, t * P:(t + 1) * P], v_raw[:, t * P:(t + 1) * P], ident)
                last.then_inc(v_filled, 1)

            def logits(a):
                kind, kv, _ = STEPS[a]
                for b in range(2):
                    taken(pe, D_PROJ + NEED_K[a] - 1 - b)
                q, k = qkv["q"][a % 2], qkv["k"][kv]
                width = HD // 2 if kind == "diff" else HD
                for m in range(HD // width):
                    r0, r1 = m * width, (m + 1) * width
                    mm(bank[2 + m][:, 0:P], q[r0:r1, 0:P], k[r0:r1, 0:P], start=True, stop=True)
                    last = mm(bank[2 + m][:, P:3 * P], q[r0:r1, P:2 * P], k[r0:r1, :], start=True, stop=True)
                last.then_inc(logits_ready, 1)

            def transpose_probs(a):
                pe.wait_ge(probs_ready, a + 1)
                for i in range(3):
                    last = nc.tensor.transpose(bank[4][:, i * P:(i + 1) * P], probs[:, 0, i * P:(i + 1) * P], ident)
                last.then_inc(probsT_filled, 1)

            def times_v(a):
                kv = STEPS[a][1]
                v = qkv["v"][kv]
                pe.wait_ge(v_ready, sum(n < START[a] for n in V_BLOCKS))
                pe.wait_ge(probsT_ready, a + 1)
                mm(bank[5][:, 0:P], probsT[:, 0:P], v[:, 0:P], start=True, stop=True)
                mm(bank[5][:, P:2 * P], probsT[:, P:2 * P], v[:, 0:P], start=True, stop=False)
                mm(bank[5][:, P:2 * P], probsT[:, 2 * P:3 * P], v[:, P:2 * P], start=False, stop=True)\
                    .then_inc(pv_ready, 1)

            def transpose_out(a):
                pe.wait_ge(head_out_ready, a + 1)
                if a >= 1:
                    pe.wait_ge(y_ready, a)
                for t in range(TT):
                    last = nc.tensor.transpose(bank[6][:, t * P:(t + 1) * P], head_out[:, t, :], ident)
                last.then_inc(outT_ready, 1)

            def half_chunk(n, j, first_fill, xhi, xlo, norm=None, late=None):
                c, half = HALVES[j]
                f = first_fill + c
                hi, lo = (w[:, :].rearrange("p (k c) -> p k c", k=KT // 2) for w in (hi_of(n), wlo[n % HEAD_RING]))
                if half == 0:
                    bank_free(f)
                pe.wait_ge(wlo_ready, n + 1)
                order = [(t, k) for t in range(TT) for k in range(KT // 2) if k != late]
                if late is not None:
                    order += [(t, late) for t in range(TT)]
                for i, (t, k) in enumerate(order):
                    if late is not None and i == KT // 2 - 1:
                        transpose_out(HEADS - 1)
                    if k == late and t == 0:
                        pe.wait_ge(y_ready, HEADS)
                    o, ts = bank[f % 2][:, t * 256:(t + 1) * 256], slice(t * P, (t + 1) * P)
                    apart = norm is not None and c == N_OUT - 1 and t == 1
                    if apart:
                        o = bank[2][:, 0:256]
                    if norm is not None and j in (0, 2) and t == 0 and k % 2 == 0:
                        norm_read(pe, norm * NORM_FILLS + half * 4 + k // 2)
                    kk, first = half * 8 + k, half == 0 and (i == 0 or (apart and k == 0))
                    end = half == 1 and all(tt != t for tt, _ in order[i + 1:])
                    mm(o, xhi[:, kk, ts], hi[:, k, :], start=first, stop=False, skip_group_check=True)
                    mm(o, xhi[:, kk, ts], lo[:, k, :], start=False, stop=False, skip_group_check=True)
                    last = mm(o, xlo[:, kk, ts], hi[:, k, :], start=False, stop=end, skip_group_check=True)
                    if norm is not None and (c, half, t, k) == (N_OUT - 1, 1, 0, KT // 2 - 1):
                        last.then_inc(dense_ready[f % 2], 1)
                if half == 0:
                    last.then_inc(half_used, 1)
                elif apart:
                    last.then_inc(last_tile_ready, 1)
                else:
                    last.then_inc(dense_ready[f % 2], 1)

            for j in range(N_HEAD + 1):
                for a in range(HEADS):
                    if START[a] == j:
                        logits(a)
                for a in range(HEADS):
                    if START[a] + 2 == j:
                        times_v(a)
                if j - 2 in V_BLOCKS:
                    transpose_v(j - 2)
                for a in range(HEADS):
                    if START[a] + 1 == j:
                        transpose_probs(a)
                    if OUT_AT[a] == j and a < HEADS - 1:
                        transpose_out(a)
                if j == P_AT:
                    pe.wait_ge(p_loaded, 16)
                    for k in range(2):
                        for t in range(TT):
                            last = nc.tensor.transpose(bank[4][:, (2 * k + t) * P:(2 * k + t + 1) * P],
                                                       p_tok[:, t, k * P:(k + 1) * P], ident)
                    last.then_inc(pT_filled, 1)
                if j < N_PROJ:
                    project(j)
                elif j < N_HEAD:
                    last_heads = j == N_PROJ + 2
                    if j == N_PROJ or last_heads:
                        pe.wait_ge(y_ready, HEADS - 1 if last_heads else HALF_READY)
                    half_chunk(j, j - N_PROJ, D_OUT, yhi, ylo, late=ORDER[-1] - 8 if last_heads else None)

            def ple_chunk(c):
                f = D_PLE + c
                bank_free(f)
                g, c0 = divmod(c * 256, D // 2)
                for t in range(TT):
                    for k in range(2):
                        last = mm(bank[f % 2][:, t * 256:(t + 1) * 256], pT[:, k, t * P:(t + 1) * P],
                                  ple_weights[:, g, k, c0:c0 + 256], start=k == 0, stop=k == 1)
                last.then_inc(dense_ready[f % 2], 1)

            pe.wait_ge(pT_ready, 1)
            pe.wait_ge(ple_loaded, 32)
            ple_chunk(0)
            pe.wait_ge(hp_ready, N_OUT)
            pe.wait_ge(router_ready, 1)

            def transpose_h(i):
                norm_free(1, i)
                for k in range(2):
                    for t in range(TT):
                        last = nc.tensor.transpose(norm_bank(NORM_FILLS + i)[:, (2 * k + t) * P:(2 * k + t + 1) * P],
                                                   hp[:, t, 2 * i + k, :], ident)
                last.then_inc(norm_ready, 1)

            n_r = GROUPS + EXPERTS

            def route(i):
                norm_read(pe, NORM_FILLS + i)
                for k in range(2):
                    last = mm(bank[2][0:n_r, 0:S], router[:, 2 * i + k, :], hT[:, i % 4, k, :],
                              start=i == k == 0, stop=i == NORM_FILLS - 1 and k == 1)
                last.then_inc(hT_used, 1)

            for i in range(NORM_FILLS):
                transpose_h(i)
                if i >= 1:
                    route(i - 1)
            route(NORM_FILLS - 1)
            pe.wait_ge(rlogits_copied, 1)
            for t in range(TT):
                last = nc.tensor.transpose(bank[3][:, t * n_r:(t + 1) * n_r], rlT[:, t * P:(t + 1) * P],
                                           ident[0:n_r, 0:n_r])
            last.then_inc(rlogits_ready, 1)

            for c in range(1, 4):
                ple_chunk(c)
            pe.wait_ge(chosen, 3)
            picked = rt[:, 2, :, :]
            rank = bank[3]
            mm(rank[:, 0:EXPERTS], before, picked[:, 0, :], start=True, stop=True).then_inc(ring_used, RING)
            mm(rank[:, EXPERTS:2 * EXPERTS], ones, picked[:, 0, :], start=True, stop=False)
            mm(rank[:, EXPERTS:2 * EXPERTS], before, picked[:, 1, :], start=False, stop=True)
            mm(rank[:, 2 * EXPERTS:3 * EXPERTS], ones, picked[:, 0, :], start=True, stop=False)
            mm(rank[:, 2 * EXPERTS:3 * EXPERTS], ones, picked[:, 1, :], start=False, stop=True)\
                .then_inc(ranks_filled, 1)
            for c in range(4, 6):
                ple_chunk(c)
            pe.wait_ge(rounds_known, 1)
            rounds = pe.value_load(rounds_i[0:1, 0:1], min_val=1, max_val=MAX_ROUNDS)
            for c in range(6, N_OUT):
                ple_chunk(c)

            def slot_here(fill, turns):
                pos = fill % RING
                landed = 16 * (fill // RING + 1) + (16 * HEAD_TURNS if pos < HEAD_RING else 0)
                pe.wait_ge(slot_loaded[pos], turns + landed)

            with pe.Fori(0, rounds * BLOCKS) as it:
                pe.wait_ge(sel_ready, it + 1)

                def gather(i):
                    if i >= 2:
                        pe.wait_ge(gather_taken, it * 4 + (i - 1))
                    for k in range(4):
                        for t in range(TT):
                            last = mm(bank[2 + i % 2][:, k * P:(k + 1) * P], hp[:, t, 4 * i + k, :], sel[:, t, :],
                                      start=t == 0, stop=t == TT - 1)
                    last.then_inc(gather_filled, 1)

                turns = it * FILLS_IT

                def w13_quarter(x, quarter):
                    fill = x * FILLS_X + 2 * quarter
                    slot_here(fill, turns)
                    slot_here(fill + 1, turns)
                    w = slots(fill, 2).rearrange("p (m k f) -> p k m f", m=2, k=4)
                    for k in range(4):
                        for j in range(QUAD):
                            last = mm(bank[x % 2][SLOTS * j:SLOTS * (j + 1), 0:2 * P]
                                      .rearrange("p (m f) -> p m f", m=2),
                                      tokT[:, 4 * quarter + k, SLOTS * x:SLOTS * (x + 1)],
                                      w[:, k, :, j * P:(j + 1) * P],
                                      start=quarter == 0 and k == 0, stop=quarter == 3 and k == 3)
                    last.then_inc(ring_used, 2)

                gather(0)
                for b in range(2):
                    taken(pe, D_GATE - 1 - b)
                for x in range(QUAD):
                    n = it * QUAD + (x + 1)
                    for quarter in range(4):
                        if x == 0:
                            if 1 <= quarter < 3:
                                gather(quarter + 1)
                            pe.wait_ge(gather_taken, it * 4 + (quarter + 1))
                        w13_quarter(x, quarter)
                        if x == quarter == 0:
                            gather(1)
                    if x == 0:
                        for t in range(TT):
                            last = nc.tensor.transpose(bank[4][:, t * P:(t + 1) * P], selg[:, t, :], ident)
                        last.then_inc(selgT_filled, 1)
                        pe.wait_ge(selgT_ready, it + 1)
                    pe.wait_ge(hid_ready, n)
                    nc.tensor.transpose(bank[4][:, 0:P], hid, ident).then_inc(hidT_filled, 1)
                    pe.wait_ge(hidT_ready, n)
                    for j in range(JT):
                        fill = x * FILLS_X + 8 + j
                        slot_here(fill, turns)
                        w = slots(fill)
                        for q in range(QUAD):
                            last = mm(bank[5 + x % 2][SLOTS * q:SLOTS * (q + 1), :], hidT[:, SLOTS * j:SLOTS * (j + 1)],
                                      w[:, q * 512:(q + 1) * 512], start=j == 0, stop=j == JT - 1)
                        last.then_inc(ring_used, 1)
                for i in range(8):
                    q, t = i // TT, i % TT
                    if t == 0:
                        pe.wait_ge((o4_dve, o4_act)[q // 2], it * (2 * QUAD) + (2 * QUAD - 1 + q % 2))
                    if i >= 2:
                        pe.wait_ge(scatter_taken, it * 8 + (i - 1))
                    mm(bank[2 + i % 2][:, :], selgT[:, t * P:(t + 1) * P], o4[:, q * 512:(q + 1) * 512],
                       start=True, stop=True).then_inc(scatter_filled, 1)
            pe.wait_ge(loop_done, 1)

            def transpose_sum(i):
                norm_free(2, i)
                g = 2 * NORM_FILLS + i
                for k in range(2):
                    for t in range(TT):
                        c0 = (2 * i + k) * P
                        last = nc.tensor.transpose(norm_bank(g)[:, (2 * k + t) * P:(2 * k + t + 1) * P],
                                                   h[:, t, c0:c0 + P], ident)
                last.then_inc(norm_ready, 1)
            for i in range(NORM_FILLS // 2):
                transpose_sum(i)
            for j, (c, half) in enumerate(HALVES):
                if j == 1:
                    for i in range(NORM_FILLS // 2, NORM_FILLS):
                        transpose_sum(i)
                half_chunk(N_HEAD + j, j, D_GATE, uhi, ulo, norm=2)


_INPUTS = ["x", "p", "rel_bias", "g_final", "g_mix", "w_in", "swa_sinks", "lam_q1", "lam_k1", "lam_q2", "lam_k2",
           "diff_subln", "w_out", "g_ffn", "w_group", "w_expert", "w1", "w3", "w2", "g_ple", "w_ple_gate",
           "w_ple_proj"]


def kernel(**inputs):
    import concourse.bacc as bacc
    from concourse.bass_utils import run_bass_kernel_spmd

    nc = bacc.Bacc("TRN2", target_bir_lowering=False, num_devices=1)
    arrays = {f"in_{n}": np.ascontiguousarray(inputs[n]) for n in _INPUTS}
    for g in ("in_g_mix", "in_g_ple"):
        arrays[g] = np.ascontiguousarray(arrays[g].reshape(KT, P).T)
    arrays["in_cst"] = constants()
    arrays["in_choice"] = bucket_choice()
    A = {n[3:]: nc.dram_tensor(n, a.shape, mybir.dt.from_np(a.dtype), kind="ExternalInput").ap()
         for n, a in arrays.items()}
    out = nc.dram_tensor("out_h", (1, S, D), F32, kind="ExternalOutput").ap()
    layer(nc, A, out)
    r = run_bass_kernel_spmd(nc, [arrays], core_ids=[0])
    return r.results[0]["out_h"]
```
